# Optimizing a Trainium2 kernel written in Bass

```python
import jax
import jax.numpy as jnp
from jax import lax
import numpy as np

D_MODEL = 1024
BATCH = 1
SEQ = 512
DEPTH = 2
DEC_BATCH = 1
DEC_SEQ = 64
PAST_LEN = 256

CHUNK = 64
Q_BLOCK = 128
ROPE_THETA = 10000.0
NORM_EPS = 1e-6
NEG_INF = -1e30

A_HEADS = 8
A_D_NOPE = 64
A_D_ROPE = 32
A_D_QK = A_D_NOPE + A_D_ROPE
A_D_V = 64
A_D_CQ = 256
A_D_C = 128
A_COLS = A_D_CQ + A_D_C + A_D_ROPE
B_HEADS = 8
B_HD = 64
B_WIDTH = B_HEADS * B_HD
B_W_LORA = 64
B_A_LORA = 64
B_G_LORA = 128
B_PROJ = 3 * B_WIDTH + B_W_LORA + B_A_LORA + B_G_LORA
B_LN_EPS = 64e-5
C_HEADS = 8
C_KV_HEADS = 2
C_HD = 64
C_IDX_HEADS = 8
C_IDX_D = 64
C_TOPK = 256
C_COLS = C_HEADS * C_HD + 2 * C_KV_HEADS * C_HD + C_IDX_HEADS * C_IDX_D + C_IDX_D + C_IDX_HEADS
D_GROUPS = 4
D_WIDTH = 512
D_SPAN = 128
D_COLS = 2 * D_WIDTH
PEER_HEADS = 8
PEER_N_KEYS = 128
PEER_N_EXPERTS = PEER_N_KEYS * PEER_N_KEYS
PEER_DK = 128
PEER_TOPK = 16
PEER_BLOCK = 128

L0_IN = A_COLS + B_PROJ
L1_IN = C_COLS + D_COLS
L0_OUT_IN = A_HEADS * A_D_V + B_WIDTH
L1_OUT_IN = C_HEADS * C_HD + D_WIDTH

kernel_name = 'hybrid_mla_rwkv7_dsa_gmlp_peer_stream_step'

def rmsnorm(x, g, eps=NORM_EPS):
    xf = x.astype(jnp.float32)
    y = xf * lax.rsqrt(jnp.mean(xf * xf, axis=-1, keepdims=True) + eps)
    return (y * g.astype(jnp.float32)).astype(x.dtype)

def layernorm(x, g, b, eps):
    xf = x.astype(jnp.float32)
    mu = jnp.mean(xf, axis=-1, keepdims=True)
    var = jnp.mean(jnp.square(xf - mu), axis=-1, keepdims=True)
    y = (xf - mu) * lax.rsqrt(var + eps) * g.astype(jnp.float32) + b.astype(jnp.float32)
    return y.astype(x.dtype)

def split_cols(p, sizes):
    return jnp.split(p, [int(i) for i in np.cumsum(sizes)[:-1]], axis=-1)

def rope(x, pos):
    half = x.shape[-1] // 2
    inv_freq = ROPE_THETA ** (-jnp.arange(half, dtype=jnp.float32) / half)
    ang = pos.astype(jnp.float32)[:, None] * inv_freq[None, :]
    cos = jnp.cos(ang)[:, None, :]
    sin = jnp.sin(ang)[:, None, :]
    xf = x.astype(jnp.float32)
    x1, x2 = xf[..., :half], xf[..., half:]
    return jnp.concatenate([x1 * cos - x2 * sin, x1 * sin + x2 * cos], axis=-1).astype(x.dtype)

def chunk_mask(qpos, kpos):
    return (kpos[None, :] // CHUNK) <= (qpos[:, None] // CHUNK)

def query_blocks(s):
    qb = Q_BLOCK if s % Q_BLOCK == 0 else s
    return qb, s // qb

def to_blocks(a, qb):
    b, s = a.shape[:2]
    return jnp.swapaxes(a.reshape((b, s // qb, qb) + a.shape[2:]), 0, 1)

def from_blocks(o):
    nb, b, qb = o.shape[:3]
    return jnp.swapaxes(o, 0, 1).reshape((b, nb * qb) + o.shape[3:])

def chunk_causal_attention(q, k, v, qpos, kpos):
    s_len, dq = q.shape[1], q.shape[-1]
    qb, nb = query_blocks(s_len)
    scale = dq ** -0.5

    def block(args):
        qblk, qp = args
        s = jnp.einsum('bqhd,bkhd->bhqk', qblk, k).astype(jnp.float32) * scale
        s = jnp.where(chunk_mask(qp, kpos)[None, None], s, NEG_INF)
        p = jax.nn.softmax(s, axis=-1).astype(v.dtype)
        return jnp.einsum('bhqk,bkhd->bqhd', p, v)

    return from_blocks(lax.map(block, (to_blocks(q, qb), qpos.reshape(nb, qb))))

def mla_mixer(p_a, qpos, kpos, cache_ckv, cache_krope, a_q_norm, a_w_uq, a_kv_norm, a_w_ukv, a_q_gain, a_k_gain):
    b, s, _ = p_a.shape
    cq, ckv, krope = split_cols(p_a, [A_D_CQ, A_D_C, A_D_ROPE])
    q = (rmsnorm(cq, a_q_norm) @ a_w_uq).reshape(b, s, A_HEADS, A_D_QK)
    ckv = rmsnorm(ckv, a_kv_norm)
    ckv_all = jnp.concatenate([cache_ckv, ckv], axis=1)
    kr_all = jnp.concatenate([cache_krope, krope], axis=1)
    l = ckv_all.shape[1]
    kv = (ckv_all @ a_w_ukv).reshape(b, l, A_HEADS, A_D_NOPE + A_D_V)
    k_nope, v = kv[..., :A_D_NOPE], kv[..., A_D_NOPE:]
    k = jnp.concatenate([k_nope, jnp.broadcast_to(kr_all[:, :, None, :], (b, l, A_HEADS, A_D_ROPE))], axis=-1)
    q = rmsnorm(q, a_q_gain)
    k = rmsnorm(k, a_k_gain)
    q = jnp.concatenate([q[..., :A_D_NOPE], rope(q[..., A_D_NOPE:], qpos)], axis=-1)
    k = jnp.concatenate([k[..., :A_D_NOPE], rope(k[..., A_D_NOPE:], kpos)], axis=-1)
    out = chunk_causal_attention(q, k, v, qpos, kpos)
    return out.reshape(b, s, A_HEADS * A_D_V), ckv, krope

def rwkv7_mixer(p_b, shift_state, wkv_state, b_mu, b_w0, b_w2, b_a0, b_a2, b_g2, b_kk, b_ka, b_rk, b_ln_g, b_ln_b):
    b, s, _ = p_b.shape
    f32 = jnp.float32
    prev = jnp.concatenate([shift_state[:, None, :], p_b[:, :-1]], axis=1)
    xs = p_b + (prev - p_b) * b_mu
    r, k, v, wl, al, gl = split_cols(xs, [B_WIDTH, B_WIDTH, B_WIDTH, B_W_LORA, B_A_LORA, B_G_LORA])
    w_log = -jax.nn.softplus(-(b_w0 + jnp.tanh(wl) @ b_w2)) - 0.5
    decay = jnp.exp(-jnp.exp(w_log.astype(f32)))
    a = jax.nn.sigmoid(b_a0 + al @ b_a2)
    g = jax.nn.sigmoid(gl) @ b_g2

    def heads(t):
        return t.reshape(b, s, B_HEADS, B_HD).astype(f32)

    kk = heads(k * b_kk)
    kk = kk * lax.rsqrt(jnp.sum(kk * kk, axis=-1, keepdims=True) + 1e-12)
    k = k * (1.0 + (a - 1.0) * b_ka)
    rh, kh, vh, ah, wh = heads(r), heads(k), heads(v), heads(a), heads(decay)

    def step(state, inp):
        r_t, w_t, k_t, v_t, a_t, bb_t = inp
        sa = jnp.einsum('bhij,bhj->bhi', state, a_t)
        state = state * w_t[:, :, None, :] + sa[..., None] * bb_t[:, :, None, :] + v_t[..., None] * k_t[:, :, None, :]
        return state, jnp.einsum('bhij,bhj->bhi', state, r_t)

    seq = tuple(jnp.swapaxes(t, 0, 1) for t in (rh, wh, kh, vh, -kk, kk * ah))
    state, y = lax.scan(step, wkv_state.astype(f32), seq)
    y = jnp.swapaxes(y, 0, 1)
    y = layernorm(y, b_ln_g.reshape(B_HEADS, B_HD), b_ln_b.reshape(B_HEADS, B_HD), B_LN_EPS)
    bonus = jnp.sum(rh * kh * b_rk, axis=-1, keepdims=True) * vh
    out = ((y + bonus).reshape(b, s, B_WIDTH) * g).astype(p_b.dtype)
    return out, p_b[:, -1], state.astype(wkv_state.dtype)

def dsa_mixer(p_c, qpos, kpos, cache_k, cache_v, cache_kidx, c_q_gain, c_k_gain, c_kidx_gain):
    b, s, _ = p_c.shape
    f32 = jnp.float32
    q, k, v, iq, ik, iw = split_cols(p_c, [C_HEADS * C_HD, C_KV_HEADS * C_HD, C_KV_HEADS * C_HD,
                                           C_IDX_HEADS * C_IDX_D, C_IDX_D, C_IDX_HEADS])
    q = rope(rmsnorm(q.reshape(b, s, C_HEADS, C_HD), c_q_gain), qpos)
    k = rope(rmsnorm(k.reshape(b, s, C_KV_HEADS, C_HD), c_k_gain), qpos)
    v = v.reshape(b, s, C_KV_HEADS, C_HD)
    iq = rope(iq.reshape(b, s, C_IDX_HEADS, C_IDX_D), qpos)
    ik = rope(rmsnorm(ik, c_kidx_gain)[:, :, None, :], qpos)[:, :, 0]
    iw = iw * (C_IDX_HEADS ** -0.5)
    k_all = jnp.concatenate([cache_k, k], axis=1)
    v_all = jnp.concatenate([cache_v, v], axis=1)
    ik_all = jnp.concatenate([cache_kidx, ik], axis=1)
    l = k_all.shape[1]
    n_sel = min(C_TOPK, l // 4)
    rep = C_HEADS // C_KV_HEADS
    qb, nb = query_blocks(s)
    gather_rows = jax.vmap(lambda rows, idx: rows[idx])

    def block(args):
        qblk, iqblk, iwblk, qp = args
        logits = jnp.einsum('bqhd,bkd->bqhk', iqblk, ik_all).astype(f32) * (C_IDX_D ** -0.5)
        score = jnp.einsum('bqh,bqhk->bqk', iwblk.astype(f32), jax.nn.relu(logits))
        score = jnp.where(chunk_mask(qp, kpos)[None], score, NEG_INF)
        top_val, top_idx = lax.top_k(score, n_sel)
        valid = top_val > 0.5 * NEG_INF
        ksel = gather_rows(k_all, top_idx)
        vsel = gather_rows(v_all, top_idx)
        qg = qblk.reshape(b, qb, C_KV_HEADS, rep, C_HD)
        sc = jnp.einsum('bqcrd,bqkcd->bqcrk', qg, ksel).astype(f32) * (C_HD ** -0.5)
        sc = jnp.where(valid[:, :, None, None, :], sc, NEG_INF)
        p = jax.nn.softmax(sc, axis=-1).astype(vsel.dtype)
        o = jnp.einsum('bqcrk,bqkcd->bqcrd', p, vsel)
        return o.reshape(b, qb, C_HEADS * C_HD)

    out = from_blocks(lax.map(block, (to_blocks(q, qb), to_blocks(iq, qb), to_blocks(iw, qb), qpos.reshape(nb, qb))))
    return out, k, v, ik

def gmlp_mixer(p_d, d_ln_g, d_ln_b, d_ws, d_bs):
    b, s, _ = p_d.shape
    u, v = split_cols(jax.nn.gelu(p_d, approximate=False), [D_WIDTH, D_WIDTH])
    v = layernorm(v, d_ln_g, d_ln_b, NORM_EPS)
    span = D_SPAN if s % D_SPAN == 0 else s
    nc = s // span
    w = jnp.tril(d_ws[:, :span, :span])
    vg = v.reshape(b, nc, span, D_GROUPS, D_WIDTH // D_GROUPS)
    mixed = jnp.einsum('gts,bnsgc->bntgc', w, vg) + jnp.swapaxes(d_bs[:, :span], 0, 1)[:, :, None]
    return u * mixed.reshape(b, s, D_WIDTH), v

def peer_ffn(x, w_q, keys, u_tab, v_tab):
    b, s, d = x.shape
    t = b * s
    nb = -(-t // PEER_BLOCK)
    xt = jnp.pad(x.reshape(t, d), ((0, nb * PEER_BLOCK - t), (0, 0))).reshape(nb, PEER_BLOCK, d)
    half = PEER_DK // 2

    def block(xb):
        q = (xb @ w_q).reshape(PEER_BLOCK, PEER_HEADS, 2, half)
        sc = jnp.einsum('thpd,hpnd->thpn', q, keys).astype(jnp.float32)
        s1, i1 = lax.top_k(sc[:, :, 0], PEER_TOPK)
        s2, i2 = lax.top_k(sc[:, :, 1], PEER_TOPK)
        cand = (s1[..., :, None] + s2[..., None, :]).reshape(PEER_BLOCK, PEER_HEADS, PEER_TOPK * PEER_TOPK)
        cidx = (i1[..., :, None] * PEER_N_KEYS + i2[..., None, :]).reshape(PEER_BLOCK, PEER_HEADS, PEER_TOPK * PEER_TOPK)
        top_s, top_pos = lax.top_k(cand, PEER_TOPK)
        eidx = jnp.take_along_axis(cidx, top_pos, axis=-1)
        gate = jax.nn.softmax(top_s, axis=-1)
        ue = u_tab[eidx]
        ve = v_tab[eidx]
        h = jax.nn.gelu(jnp.einsum('td,thkd->thk', xb, ue), approximate=False)
        return jnp.einsum('thk,thkd->td', (gate * h).astype(ve.dtype), ve)

    out = lax.map(block, xt).reshape(nb * PEER_BLOCK, d)[:t]
    return out.reshape(b, s, d)

def even_layer(x, qpos, kpos, cache_ckv, cache_krope, state_wkv, state_shift, w):
    (norm_mix, w_in, a_q_norm, a_w_uq, a_kv_norm, a_w_ukv, a_q_gain, a_k_gain,
     b_mu, b_w0, b_w2, b_a0, b_a2, b_g2, b_kk, b_ka, b_rk, b_ln_g, b_ln_b, w_out) = w
    proj = rmsnorm(x, norm_mix) @ w_in
    p_a, p_b = proj[..., :A_COLS], proj[..., A_COLS:]
    o_a, ckv, krope = mla_mixer(p_a, qpos, kpos, cache_ckv, cache_krope,
                                a_q_norm, a_w_uq, a_kv_norm, a_w_ukv, a_q_gain, a_k_gain)
    o_b, shift, wkv = rwkv7_mixer(p_b, state_shift, state_wkv, b_mu, b_w0, b_w2, b_a0, b_a2,
                                  b_g2, b_kk, b_ka, b_rk, b_ln_g, b_ln_b)
    x = x + jnp.concatenate([o_a, o_b], axis=-1) @ w_out
    return x, [ckv, krope, wkv, shift]

def odd_layer(x, qpos, kpos, cache_k, cache_v, cache_kidx, w):
    (norm_mix, w_in, c_q_gain, c_k_gain, c_kidx_gain, d_ln_g, d_ln_b, d_ws, d_bs, w_out) = w
    proj = rmsnorm(x, norm_mix) @ w_in
    p_c, p_d = proj[..., :C_COLS], proj[..., C_COLS:]
    o_c, k, v, kidx = dsa_mixer(p_c, qpos, kpos, cache_k, cache_v, cache_kidx, c_q_gain, c_k_gain, c_kidx_gain)
    o_d, d_v = gmlp_mixer(p_d, d_ln_g, d_ln_b, d_ws, d_bs)
    x = x + jnp.concatenate([o_c, o_d], axis=-1) @ w_out
    return x, [k, v, kidx, d_v]

def run_trunk(x, states, mix_w, ffn_w):
    s = x.shape[1]
    past = states[0][0].shape[1]
    qpos = past + jnp.arange(s, dtype=jnp.int32)
    kpos = jnp.arange(past + s, dtype=jnp.int32)
    new_state = []
    for layer in range(DEPTH):
        if layer % 2 == 0:
            x, st = even_layer(x, qpos, kpos, *states[layer], mix_w[layer])
        else:
            x, st = odd_layer(x, qpos, kpos, *states[layer], mix_w[layer])
        new_state.extend(st)
        norm_ffn, p_wq, p_keys, p_u, p_v = ffn_w[layer]
        x = x + peer_ffn(rmsnorm(x, norm_ffn), p_wq, p_keys, p_u, p_v)
    return x, new_state

def setup_inputs(seed: int = 0) -> dict:
    key = jax.random.key(seed)
    ks = jax.random.split(key, 64)
    f32 = jnp.float32
    d = D_MODEL

    def nrm(i, shape, scale):
        return jax.random.normal(ks[i], shape, f32) * scale

    def gain(i, n):
        return 1.0 + nrm(i, (n,), 0.02)

    return {
        'x_prompt': nrm(0, (BATCH, SEQ, d), 1.0),
        'x_sample': nrm(1, (DEC_BATCH, DEC_SEQ, d), 1.0),
        'cache_a_ckv': nrm(2, (DEC_BATCH, PAST_LEN, A_D_C), 1.0),
        'cache_a_krope': nrm(3, (DEC_BATCH, PAST_LEN, A_D_ROPE), 1.0),
        'state_b_wkv': nrm(4, (DEC_BATCH, B_HEADS, B_HD, B_HD), 0.5),
        'state_b_shift': nrm(5, (DEC_BATCH, B_PROJ), 1.0),
        'cache_c_k': nrm(6, (DEC_BATCH, PAST_LEN, C_KV_HEADS, C_HD), 1.0),
        'cache_c_v': nrm(7, (DEC_BATCH, PAST_LEN, C_KV_HEADS, C_HD), 1.0),
        'cache_c_kidx': nrm(8, (DEC_BATCH, PAST_LEN, C_IDX_D), 1.0),
        'l0_norm_mix': gain(9, d),
        'l0_w_in': nrm(10, (d, L0_IN), d ** -0.5),
        'a_q_norm': gain(11, A_D_CQ),
        'a_w_uq': nrm(12, (A_D_CQ, A_HEADS * A_D_QK), A_D_CQ ** -0.5),
        'a_kv_norm': gain(13, A_D_C),
        'a_w_ukv': nrm(14, (A_D_C, A_HEADS * (A_D_NOPE + A_D_V)), A_D_C ** -0.5),
        'a_q_gain': gain(15, A_D_QK),
        'a_k_gain': gain(16, A_D_QK),
        'b_mu': jax.random.uniform(ks[17], (B_PROJ,), f32),
        'b_w0': -2.0 + nrm(18, (B_WIDTH,), 1.0),
        'b_w2': nrm(19, (B_W_LORA, B_WIDTH), 0.1),
        'b_a0': nrm(20, (B_WIDTH,), 0.1),
        'b_a2': nrm(21, (B_A_LORA, B_WIDTH), 0.1),
        'b_g2': nrm(22, (B_G_LORA, B_WIDTH), B_G_LORA ** -0.5),
        'b_kk': 0.85 + nrm(23, (B_WIDTH,), 0.02),
        'b_ka': gain(24, B_WIDTH),
        'b_rk': nrm(25, (B_HEADS, B_HD), 0.1),
        'b_ln_g': gain(26, B_WIDTH),
        'b_ln_b': nrm(27, (B_WIDTH,), 0.02),
        'l0_w_out': nrm(28, (L0_OUT_IN, d), L0_OUT_IN ** -0.5),
        'l0_norm_ffn': gain(29, d),
        'l0_peer_wq': nrm(30, (d, PEER_HEADS * PEER_DK), d ** -0.5),
        'l0_peer_keys': nrm(31, (PEER_HEADS, 2, PEER_N_KEYS, PEER_DK // 2), (PEER_DK // 2) ** -0.5),
        'l0_peer_u': nrm(32, (PEER_N_EXPERTS, d), d ** -0.5),
        'l0_peer_v': nrm(33, (PEER_N_EXPERTS, d), PEER_HEADS ** -0.5),
        'l1_norm_mix': gain(34, d),
        'l1_w_in': nrm(35, (d, L1_IN), d ** -0.5),
        'c_q_gain': gain(36, C_HD),
        'c_k_gain': gain(37, C_HD),
        'c_kidx_gain': gain(38, C_IDX_D),
        'd_ln_g': gain(39, D_WIDTH),
        'd_ln_b': nrm(40, (D_WIDTH,), 0.02),
        'd_ws': nrm(41, (D_GROUPS, D_SPAN, D_SPAN), D_SPAN ** -0.5),
        'd_bs': 1.0 + nrm(42, (D_GROUPS, D_SPAN), 0.02),
        'l1_w_out': nrm(43, (L1_OUT_IN, d), L1_OUT_IN ** -0.5),
        'l1_norm_ffn': gain(44, d),
        'l1_peer_wq': nrm(45, (d, PEER_HEADS * PEER_DK), d ** -0.5),
        'l1_peer_keys': nrm(46, (PEER_HEADS, 2, PEER_N_KEYS, PEER_DK // 2), (PEER_DK // 2) ** -0.5),
        'l1_peer_u': nrm(47, (PEER_N_EXPERTS, d), d ** -0.5),
        'l1_peer_v': nrm(48, (PEER_N_EXPERTS, d), PEER_HEADS ** -0.5),
    }

def reference(x_prompt, x_sample, cache_a_ckv, cache_a_krope, state_b_wkv, state_b_shift,
              cache_c_k, cache_c_v, cache_c_kidx,
              l0_norm_mix, l0_w_in, a_q_norm, a_w_uq, a_kv_norm, a_w_ukv, a_q_gain, a_k_gain,
              b_mu, b_w0, b_w2, b_a0, b_a2, b_g2, b_kk, b_ka, b_rk, b_ln_g, b_ln_b,
              l0_w_out, l0_norm_ffn, l0_peer_wq, l0_peer_keys, l0_peer_u, l0_peer_v,
              l1_norm_mix, l1_w_in, c_q_gain, c_k_gain, c_kidx_gain, d_ln_g, d_ln_b, d_ws, d_bs,
              l1_w_out, l1_norm_ffn, l1_peer_wq, l1_peer_keys, l1_peer_u, l1_peer_v):
    mix_w = (
        (l0_norm_mix, l0_w_in, a_q_norm, a_w_uq, a_kv_norm, a_w_ukv, a_q_gain, a_k_gain,
         b_mu, b_w0, b_w2, b_a0, b_a2, b_g2, b_kk, b_ka, b_rk, b_ln_g, b_ln_b, l0_w_out),
        (l1_norm_mix, l1_w_in, c_q_gain, c_k_gain, c_kidx_gain, d_ln_g, d_ln_b, d_ws, d_bs, l1_w_out),
    )
    ffn_w = (
        (l0_norm_ffn, l0_peer_wq, l0_peer_keys, l0_peer_u, l0_peer_v),
        (l1_norm_ffn, l1_peer_wq, l1_peer_keys, l1_peer_u, l1_peer_v),
    )
    bp = x_prompt.shape[0]
    dt = x_prompt.dtype
    prompt_states = (
        (jnp.zeros((bp, 0, A_D_C), dt), jnp.zeros((bp, 0, A_D_ROPE), dt),
         jnp.zeros((bp, B_HEADS, B_HD, B_HD), dt), jnp.zeros((bp, B_PROJ), dt)),
        (jnp.zeros((bp, 0, C_KV_HEADS, C_HD), dt), jnp.zeros((bp, 0, C_KV_HEADS, C_HD), dt),
         jnp.zeros((bp, 0, C_IDX_D), dt)),
    )
    sample_states = (
        (cache_a_ckv, cache_a_krope, state_b_wkv, state_b_shift),
        (cache_c_k, cache_c_v, cache_c_kidx),
    )
    y_prompt, new_p = run_trunk(x_prompt, prompt_states, mix_w, ffn_w)
    y_sample, new_s = run_trunk(x_sample, sample_states, mix_w, ffn_w)
    a_ckv_p, a_krope_p, b_wkv_p, b_shift_p, c_k_p, c_v_p, c_kidx_p, _d_v_p = new_p
    a_ckv_s, a_krope_s, b_wkv_s, b_shift_s, c_k_s, c_v_s, c_kidx_s, d_v_s = new_s
    return (y_prompt, y_sample,
            a_ckv_p, a_krope_p, b_wkv_p, b_shift_p, c_k_p, c_v_p, c_kidx_p,
            a_ckv_s, a_krope_s, b_wkv_s, b_shift_s, c_k_s, c_v_s, c_kidx_s, d_v_s)


_drawn_inputs = setup_inputs


def setup_inputs(seed=0):
    import zlib

    import numpy as np

    out = dict(_drawn_inputs(seed))
    spreads = {}
    factors = {'a_q_norm': 3.475,
     'a_kv_norm': 2.777,
     'a_q_gain': 3.018,
     'a_k_gain': 2.926,
     'b_kk': 2.684,
     'c_q_gain': 5.932,
     'c_k_gain': 2.716,
     'c_kidx_gain': 3.053,
     'd_ln_g': 2.875,
     'd_bs': 3.537,
     'l1_norm_ffn': 2.668}
    for name, (base, spread) in spreads.items():
        noise = np.random.default_rng([zlib.crc32(name.encode()), seed]).standard_normal(out[name].shape)
        drawn = base * np.exp(spread * noise) if base else spread * noise
        out[name] = jnp.asarray(drawn.astype(out[name].dtype))
    for name, factor in factors.items():
        out[name] = (out[name] * factor).astype(out[name].dtype)
    return out
```

```python
from contextlib import ExitStack

import numpy as np

import concourse.bass as bass
from concourse import mybir

P = 128
F32 = mybir.dt.float32
U32 = mybir.dt.uint32
ALU = mybir.AluOpType
ACT = mybir.ActivationFunctionType
AX = mybir.AxisListType

D = 1024
KD = D // P
SEQ, DEC, PAST = 512, 64, 256
NT = 5
TOK = SEQ + DEC
PADT = NT * P
KT7 = 7
EPS = 1e-6
NEG = -1e30

AH, ANOPE, AROPE, AQK, AV = 8, 64, 32, 96, 64
ACQ, AC = 256, 128
ACOLS = ACQ + AC + AROPE
BH, BHD, BW = 8, 64, 512
BT = 14
BPROJ = BT * P
BLN_EPS = 64e-5
DECAY = float(np.exp(-0.5))
CHK = 64
NCH = TOK // CHK
CH_, CKV, CHD = 8, 2, 64
CCOLS = 1352
DW = 512
NK = 128
PH, PK = 8, 16
NEXP = NK * NK
QT_KEYS = [1, 2, 3, 4, 3]
QT_FIRST = [0, 0, 0, 0, 4]
SEL_KEYS = [0, 128, 128, 128, 80]
RING = 8
SLOTS = 16


class Signal:

    def __init__(self, handle):
        self.h, self.base = handle, 0

    def at(self, n):
        return self.base + n

    def end(self, n):
        self.base += n


class Chain:

    def __init__(self, eng, signal, base=0):
        self.eng, self.s, self.base, self.n = eng, signal, base, 0

    def __call__(self, ins):
        ins.then_inc(self.s.h, 1)
        self.n += 1
        self.eng.wait_ge(self.s.h, self.s.at(self.base + self.n))


class Roots:

    half = None

    def __init__(self, sig):
        self.asked, self.done, self.n = sig("roots_asked"), sig("roots_done"), 0

    def ask(self, dve, ins):
        ins.then_inc(self.asked.h, 1)
        self.n += 1
        dve.wait_ge(self.done.h, self.done.at(self.n))

    def give(self, pool, i, ap):
        pool.wait_ge(self.asked.h, self.asked.at(i + 1))
        half = self.half[:, 0:1]
        half = half.broadcast_to(list(ap.shape)) if len(ap.shape) == 2 else half
        pool.tensor_tensor(ap, ap, half, ALU.pow).then_inc(self.done.h, 1)

    def end(self):
        self.asked.end(self.n), self.done.end(self.n)


def encoder(nc, io):
    ctx = ExitStack()
    with ctx:
        def sb(stack, name, shape, dt=F32):
            return stack.enter_context(nc.sbuf_tensor(name, shape, dt))

        names = {}

        def sig(name):
            if name not in names:
                names[name] = Signal(ctx.enter_context(nc.semaphore(name)))
            return names[name]

        bank = [ctx.enter_context(nc.psum_tensor(f"bank{i}", [P, 512], F32)) for i in range(8)]

        X = sb(ctx, "X", [P, NT, D])
        CST = sb(ctx, "CST", [P, 1537])
        Roots.half = CST[:, 1536:1537]
        ident = CST[:, 0:128]
        onesbd = CST[:, 128:256]
        maskSI = CST[:, 256:512]
        mask16 = CST[:, 512:640]
        maskO = CST[:, 640:768]
        stackI = CST[:, 768:832]
        scanm = CST[:, 832:1408]

        dve_chain = sig("dve_chain")
        act_chain = sig("act_chain")
        loaded = sig("loaded")
        stored = sig("stored")

        def load_x(eng):
            for t in range(4):
                eng.dma_start(X[:, t, :], io["x_prompt"][0, t * P:(t + 1) * P, :]).then_inc(loaded.h, 16)
            eng.dma_start(X[0:DEC, 4, :], io["x_sample"][0]).then_inc(loaded.h, 16)

        def norm(stack, tag, gain, src_load, XN, XT, more_loads=None, XL=None):
            with ExitStack() as st:
                gB = sb(st, f"gB{tag}", [P, D])
                junk = sb(st, f"junk{tag}", [P, D])
                ss = sb(st, f"ss{tag}", [P, 8])
                xz, sq, xn, tr, ev = (sig(n) for n in ("x_zeroed", "squares", "normed", "transposed", "evacuated"))
                nload = [0]
                roots = Roots(sig)
                with nc.Block() as block:
                    @block.sync
                    def _(sp):
                        sp.dma_start(gB[:, :], gain.partition_broadcast(P)).then_inc(loaded.h, 16)
                        nload[0] += 1
                        if src_load:
                            load_x(sp)
                            nload[0] += 5
                            sp.dma_start(CST[:, :], io["cst"]).then_inc(loaded.h, 16)
                            nload[0] += 1
                        if more_loads:
                            more_loads(sp)

                    @block.scalar
                    def _(act):
                        act.wait_ge(loaded.h, loaded.at(16 * nload[0]))
                        if src_load:
                            act.wait_ge(xz.h, xz.at(1))
                        for t in range(NT):
                            act.activation(junk[:, :], X[:, t, :], ACT.Square,
                                           accum_out=ss[:, t:t + 1]).then_inc(sq.h, 1)
                            act.wait_ge(sq.h, sq.base + t + 1)
                        for t in range(NT):
                            for b in range(2):
                                act.wait_ge(tr.h, tr.at(2 * t + b + 1))
                                act.activation(XT[:, 4 * b:4 * b + 4, t * P:(t + 1) * P],
                                               bank[(2 * t + b) % 4][:, :].rearrange("p (k n) -> p k n", k=4),
                                               ACT.Copy).then_inc(ev.h, 1)

                    @block.vector
                    def _(dve):
                        if src_load:
                            dve.memset(X[DEC:P, 4, :], 0.0).then_inc(xz.h, 1)
                        dve.wait_ge(loaded.h, loaded.at(16 * nload[0]))
                        dve.wait_ge(sq.h, sq.at(NT))
                        roots.ask(dve, dve.tensor_scalar(ss[:, 0:NT], ss[:, 0:NT], 1.0 / D, EPS, ALU.mult, ALU.add))
                        for t in range(NT):
                            dve.scalar_tensor_tensor(XN[:, t, :], X[:, t, :], ss[:, t:t + 1], gB[:, :],
                                                     ALU.mult, ALU.mult).then_inc(xn.h, 1)

                    @block.gpsimd
                    def _(pool):
                        roots.give(pool, 0, ss[:, 0:NT])

                    @block.tensor
                    def _(pe):
                        for t in range(NT):
                            pe.wait_ge(xn.h, xn.at(t + 1))
                            for b in range(2):
                                if t >= 2:
                                    pe.wait_ge(ev.h, ev.at(2 * (t - 2) + b + 1))
                                for k in range(4):
                                    mm = pe.transpose(bank[(2 * t + b) % 4][:, k * P:(k + 1) * P],
                                                      XN[:, t, (4 * b + k) * P:(4 * b + k + 1) * P], ident)
                                mm.then_inc(tr.h, 1)
                loaded.end(16 * nload[0])
                if src_load:
                    xz.end(1)
                roots.end()
                sq.end(NT), xn.end(NT), tr.end(2 * NT), ev.end(2 * NT)

        def attention(tag, rows, QT, key_of, V_of, SEL, scale, OUT):
            with ExitStack() as st:
                S = sb(st, f"S{tag}", [P, 2, 512])
                E = sb(st, f"E{tag}", [P, 2, 512])
                ET = sb(st, f"ET{tag}", [P, 2, 512])
                mx = sb(st, f"mx{tag}", [P, 2, 1])
                nmx = sb(st, f"nmx{tag}", [P, 2, 1])
                den = sb(st, f"den{tag}", [P, 2, 1])
                rden = sb(st, f"rden{tag}", [P, 2, 1])
                sc, so, ex, tr, pt, pv, fi = (sig(n) for n in (
                    "scores", "masked", "exped", "probs_turned", "probs_copied", "weighted", "heads_out"))
                every = (sc, so, ex, tr, pt, pv, fi)
                N = NT
                with nc.Block() as block:
                    @block.sync
                    def _(sp):
                        for s in every:
                            sp.sem_inc(s.h, 2)
                            s.base += 2

                    @block.tensor
                    def _(pe):
                        for h in range(AH):
                            a = h // 4
                            it = h * N

                            def scores(j):
                                pe.wait_ge(so.h, so.at(it + max(j - 1, 0)))
                                n = QT_KEYS[j] * P
                                pe.matmul(sbank(j)[:, 0:n], QT[0:rows, h, j * P:(j + 1) * P],
                                          key_of(a, h, QT_FIRST[j] * P, n),
                                          start=True, stop=True).then_inc(sc.h, 1)

                            def turn(j):
                                pe.wait_ge(ex.h, ex.at(it + j + 1))
                                pe.wait_ge(pt.h, pt.at(it + j))
                                for k in range(QT_KEYS[j]):
                                    mm = pe.transpose(bank[2][:, k * P:(k + 1) * P],
                                                      E[:, eslot(j), k * P:(k + 1) * P], ident)
                                mm.then_inc(tr.h, 1)

                            def weigh(j):
                                pe.wait_ge(pt.h, pt.at(it + j + 1))
                                pe.wait_ge(fi.h, fi.at(it + j))
                                for k in range(QT_KEYS[j]):
                                    mm = pe.matmul(bank[3][:, 0:64], ET[:, 0, k * P:(k + 1) * P],
                                                   V_of(a, h, QT_FIRST[j] + k),
                                                   start=(k == 0), stop=(k == QT_KEYS[j] - 1))
                                mm.then_inc(pv.h, 1)

                            scores(0)
                            for j in range(N):
                                if j + 1 < N:
                                    scores(j + 1)
                                turn(j)
                                weigh(j)

                    @block.vector
                    def _(dve):
                        for h in range(AH):
                            a = h // 4
                            it = h * N
                            ch = Chain(dve, dve_chain, h * (2 * N + N))

                            def soft(j):
                                n, s = QT_KEYS[j] * P, eslot(j)
                                dve.wait_ge(sc.h, sc.at(it + j + 1))
                                dve.wait_ge(ex.h, ex.at(it + max(j - 1, 0)))
                                dve.scalar_tensor_tensor(S[:, s, 0:n], sbank(j)[:, 0:n], scale, SEL[:, j, 0:n],
                                                         ALU.mult, ALU.add).then_inc(so.h, 1)
                                dve.wait_ge(so.h, so.at(it + j + 1))
                                ch(dve.tensor_reduce(mx[:, s, :], S[:, s, 0:n], AX.X, ALU.max))
                                ch(dve.tensor_scalar(nmx[:, s, :], mx[:, s, :], -1.0, None, ALU.mult))

                            def finish(j):
                                s = eslot(j)
                                dve.wait_ge(ex.h, ex.at(it + j + 1))
                                ch(dve.reciprocal(rden[:, s, :], den[:, s, :]))
                                dve.wait_ge(pv.h, pv.at(it + j + 1))
                                dve.tensor_scalar(OUT[:, j, h * 64:h * 64 + 64], bank[3][:, 0:64],
                                                  rden[:, s, :], None, ALU.mult).then_inc(fi.h, 1)

                            soft(0)
                            for j in range(N):
                                if j + 1 < N:
                                    soft(j + 1)
                                finish(j)
                            assert ch.n == 3 * N

                    @block.scalar
                    def _(act):
                        for h in range(AH):
                            a = h // 4
                            it = h * N

                            def expo(j):
                                n, s = QT_KEYS[j] * P, eslot(j)
                                at = {0: 2}.get(j, 2 + 3 * (j - 1) + 2)
                                act.wait_ge(dve_chain.h, dve_chain.at(h * 3 * N + at))
                                act.wait_ge(tr.h, tr.at(it + max(j - 1, 0)))
                                act.wait_ge(fi.h, fi.at(it + max(j - 1, 0)))
                                act.activation(E[:, s, 0:n], S[:, s, 0:n], ACT.Exp, bias=nmx[:, s, :],
                                               accum_out=den[:, s, :]).then_inc(ex.h, 1)

                            def copy(j):
                                n = QT_KEYS[j] * P
                                act.wait_ge(tr.h, tr.at(it + j + 1))
                                act.wait_ge(pv.h, pv.at(it + j))
                                act.activation(ET[:, 0, 0:n], bank[2][:, 0:n], ACT.Copy).then_inc(pt.h, 1)

                            expo(0)
                            for j in range(N):
                                copy(j)
                                if j + 1 < N:
                                    expo(j + 1)
                for s in every:
                    s.end(8 * N)
                dve_chain.end(8 * 3 * N)

        def eslot(j):
            return j % 2

        def sbank(j):
            return bank[4 + j % 2]

        OC = sb(ctx, "OC", [P, NT, 512])
        OBT = sb(ctx, "OBT", [P, 4, PADT])

        l0 = ExitStack()
        PA = sb(l0, "PA", [P, NT, ACOLS])
        PB = sb(l0, "PB", [P, BT, 2 + TOK])
        SH = sb(l0, "SH", [P, 3, BT])
        w_loaded = [sig(f"weights_loaded{i}") for i in range(4)]

        with ExitStack() as st:
            XT = sb(st, "XT", [P, KD, PADT])
            W = sb(st, "W0", [P, KD, ACOLS + BPROJ])
            wv = io["l0_w_in"].rearrange("(k p) n -> p k n", p=P)
            CW = [(0, ACOLS), (ACOLS, ACOLS + 640), (ACOLS + 640, ACOLS + 1280), (ACOLS + 1280, ACOLS + BPROJ)]

            def load_w(sp):
                for i, (a, b) in enumerate(CW):
                    sp.dma_start(W[:, :, a:b], wv[:, :, a:b]).then_inc(w_loaded[i].h, 16)

            norm(st, "a", io["l0_norm_mix"], True, X, XT, load_w)
            mm_, ev = sig("products"), sig("evacuated")
            border = sig("borders")
            with nc.Block() as block:
                @block.sync
                def _(sp):
                    sp.dma_start(SH[:, 0, :], io["shift_t"]).then_inc(border.h, 16)

                @block.tensor
                def _(pe):
                    n = 0
                    pe.wait_ge(w_loaded[0].h, w_loaded[0].at(16))
                    for t in range(NT):
                        if n >= 4:
                            pe.wait_ge(ev.h, ev.at(n - 3))
                        for k in range(KD):
                            m = pe.matmul(bank[n % 4][:, 0:ACOLS], XT[:, k, t * P:(t + 1) * P], W[:, k, 0:ACOLS],
                                          start=(k == 0), stop=(k == KD - 1))
                        m.then_inc(mm_.h, 1)
                        n += 1
                    for f in range(BT):
                        if f % 5 == 0:
                            pe.wait_ge(w_loaded[1 + f // 5].h, w_loaded[1 + f // 5].at(16))
                        for a, b in ((0, SEQ), (SEQ, TOK)):
                            if n >= 4:
                                pe.wait_ge(ev.h, ev.at(n - 3))
                            for k in range(KD):
                                m = pe.matmul(bank[n % 4][:, 0:b - a],
                                              W[:, k, ACOLS + f * P:ACOLS + (f + 1) * P], XT[:, k, a:b],
                                              start=(k == 0), stop=(k == KD - 1))
                            m.then_inc(mm_.h, 1)
                            n += 1

                @block.scalar
                def _(act):
                    n = 0
                    for t in range(NT):
                        act.wait_ge(mm_.h, mm_.at(n + 1))
                        act.activation(PA[:, t, :], bank[n % 4][:, 0:ACOLS], ACT.Copy).then_inc(ev.h, 1)
                        n += 1
                    for f in range(BT):
                        for a, b, o in ((0, SEQ, 1), (SEQ, TOK, 2)):
                            act.wait_ge(mm_.h, mm_.at(n + 1))
                            act.activation(PB[:, f, a + o:b + o], bank[n % 4][:, 0:b - a], ACT.Copy).then_inc(ev.h, 1)
                            n += 1

                @block.vector
                def _(dve):
                    dve.memset(PB[:, :, 0:1], 0.0)
                    dve.wait_ge(border.h, border.at(16))
                    dve.tensor_copy(PB[:, :, 1 + SEQ], SH[:, 0, :])
                    dve.wait_ge(ev.h, ev.at(NT + 2 * BT))
                    dve.tensor_copy(SH[:, 1, :], PB[:, :, SEQ])
                    dve.tensor_copy(SH[:, 2, :], PB[:, :, TOK + 1])
            for s in w_loaded:
                s.end(16)
            mm_.end(NT + 2 * BT), ev.end(NT + 2 * BT), border.end(16)

        mla(nc, io, sb, sig, bank, ident, PA, OC, attention)
        rwkv(nc, io, sb, sig, bank, CST, PB, OBT, X)
        with nc.Block() as block:
            @block.sync
            def _(sp):
                load_x(sp)
                sp.wait_ge(loaded.h, loaded.at(80))
                sp.dma_start(io["out_b_shift_p"], SH[:, 1, :]).then_inc(stored.h, 16)
                sp.dma_start(io["out_b_shift_s"], SH[:, 2, :]).then_inc(stored.h, 16)
                sp.wait_ge(stored.h, stored.at(32))

            @block.vector
            def _(dve):
                dve.memset(X[DEC:P, 4, :], 0.0)
                dve.memset(OBT[:, :, TOK:PADT], 0.0)
        loaded.end(80), stored.end(32)
        l0.close()
        project_out(nc, io["l0_w_out"], sb, sig, bank, ident, OC, OBT, None, X, "0")
        peer(nc, io, 0, sb, sig, bank, ident, X, norm)
        layer1(nc, io, sb, sig, bank, CST, X, OC, norm, attention)
        peer(nc, io, 1, sb, sig, bank, ident, X, norm)
        with nc.Block() as block:
            @block.sync
            def _(sp):
                for t in range(4):
                    sp.dma_start(io["out_y_p"][0, t * P:(t + 1) * P, :], X[:, t, :]).then_inc(stored.h, 16)
                sp.dma_start(io["out_y_s"][0], X[0:DEC, 4, :]).then_inc(stored.h, 16)
                sp.wait_ge(stored.h, stored.at(80))
        stored.end(80)


def mla(nc, io, sb, sig, bank, ident, PA, OC, attention):
    st = ExitStack()
    QT = sb(st, "QT", [P, AH, PADT])
    KT = sb(st, "KT", [P, AH, KT7 * P])
    V = sb(st, "V", [P, KT7, AH, AV])
    MSK = sb(st, "MSK", [P, NT, 512])
    loaded, stored, dve_chain = sig("loaded"), sig("stored"), sig("dve_chain")
    with ExitStack() as s2:
        gq = sb(s2, "gq", [P, ACQ])
        gc = sb(s2, "gc", [P, AC])
        gains = sb(s2, "gains", [P, 2, AQK])
        wuq = sb(s2, "wuq", [P, 2, AH * AQK])
        wukv = sb(s2, "wukv", [P, AH * (ANOPE + AV)])
        CQT = sb(s2, "CQT", [P, 2, PADT])
        LT = sb(s2, "LT", [P, KT7 * P])
        KRC = sb(s2, "KRC", [P, 2, AROPE])
        RT = sb(s2, "RT", [P, KT7, 32])
        CN = sb(s2, "CN", [P, NT, ACQ + AC])
        ss = sb(s2, "ssA", [P, 2, NT])
        junk = sb(s2, "junkA", [P, ACQ])
        Y = sb(s2, "Y", [P, 2, AH, AQK])
        SQ = sb(s2, "SQ", [P, AH, AQK])
        hs = sb(s2, "hs", [P, AH])
        RC = sb(s2, "RC", [P, AH, 2, 16])
        RS = sb(s2, "RS", [P, AH, 2, 16])
        sq, cn, tr, ev = sig("squares"), sig("normed"), sig("transposed"), sig("evacuated")
        up, cp, kr, ro, t2, e2 = (sig(n) for n in (
            "lifted", "lifted_copied", "krope_copied", "rotated", "heads_turned", "heads_copied"))
        NL = 10
        units = [("q", t, [0, 1, 2, 3, 6][t]) for t in range(NT)] + [("k", k, k) for k in range(KT7)]
        NU = len(units)
        roots = Roots(sig)
        with nc.Block() as block:
            @block.sync
            def _(sp):
                for dst, src in (
                    (gq[:, :], io["a_q_norm"].partition_broadcast(P)),
                    (gc[:, :], io["a_kv_norm"].partition_broadcast(P)),
                    (gains[:, 0, :], io["a_q_gain"].partition_broadcast(P)),
                    (gains[:, 1, :], io["a_k_gain"].partition_broadcast(P)),
                    (wuq[:, :, :], io["a_w_uq"].rearrange("(k p) n -> p k n", p=P)),
                    (wukv[:, :], io["a_w_ukv"]),
                    (LT[:, 4 * P:6 * P], io["ckv_t"]),
                    (KRC[:, :, :], io["cache_a_krope"][0].rearrange("(k p) n -> p k n", p=P)),
                    (RT[:, :, :], io["rope_a"]),
                    (MSK[:, :, :], io["mask"]),
                ):
                    sp.dma_start(dst, src).then_inc(loaded.h, 16)
                sp.wait_ge(cn.h, cn.at(2 * NT))
                for t in range(4):
                    sp.dma_start(io["out_a_ckv_p"][0, t * P:(t + 1) * P, :], CN[:, t, ACQ:]).then_inc(stored.h, 16)
                    sp.dma_start(io["out_a_krope_p"][0, t * P:(t + 1) * P, :], PA[:, t, ACQ + AC:]).then_inc(stored.h, 16)
                sp.dma_start(io["out_a_ckv_s"][0], CN[0:DEC, 4, ACQ:]).then_inc(stored.h, 16)
                sp.dma_start(io["out_a_krope_s"][0], PA[0:DEC, 4, ACQ + AC:]).then_inc(stored.h, 16)
                sp.wait_ge(stored.h, stored.at(160))

            @block.scalar
            def _(act):
                for t in range(NT):
                    act.activation(junk[:, :], PA[:, t, 0:ACQ], ACT.Square, accum_out=ss[:, 0, t:t + 1]).then_inc(sq.h, 1)
                    act.wait_ge(sq.h, sq.base + 2 * t + 1)
                    act.activation(junk[:, 0:AC], PA[:, t, ACQ:ACQ + AC], ACT.Square,
                                   accum_out=ss[:, 1, t:t + 1]).then_inc(sq.h, 1)
                    act.wait_ge(sq.h, sq.base + 2 * t + 2)
                for t in range(NT):
                    act.wait_ge(tr.h, tr.at(t + 1))
                    b = bank[t % 2]
                    act.activation(CQT[:, :, t * P:(t + 1) * P], b[:, 0:256].rearrange("p (k n) -> p k n", k=2),
                                   ACT.Copy).then_inc(ev.h, 1)
                    kt = t if t < 4 else 6
                    act.activation(LT[:, kt * P:(kt + 1) * P], b[:, 256:384], ACT.Copy).then_inc(ev.h, 1)

                def take(u):
                    kind, t, kt = units[u]
                    act.wait_ge(up.h, up.at(u + 1))
                    if u >= 2:
                        act.wait_ge(t2.h, t2.at(u - 1))
                    for b in range(2):
                        src = bank[2 * (u % 2) + b]
                        y = Y[:, u % 2, 4 * b:4 * b + 4, :]
                        if kind == "q":
                            ins = act.activation(y, src[:, 0:384].rearrange("p (h n) -> p h n", h=4), ACT.Copy)
                        else:
                            s4 = src[:, :].rearrange("p (h n) -> p h n", h=4)
                            act.activation(y[:, :, 0:ANOPE], s4[:, :, 0:ANOPE], ACT.Copy)
                            ins = act.activation(V[:, t, 4 * b:4 * b + 4, :], s4[:, :, ANOPE:], ACT.Copy)
                    ins.then_inc(cp.h, 1)

                def give(u):
                    kind, t, kt = units[u]
                    act.wait_ge(t2.h, t2.at(u + 1))
                    dst = QT if kind == "q" else KT
                    for b in range(2):
                        act.activation(dst[0:AQK, 4 * b:4 * b + 4, t * P:(t + 1) * P],
                                       bank[4 + 2 * (u % 2) + b][0:AQK, :].rearrange("p (h n) -> p h n", h=4),
                                       ACT.Copy).then_inc(e2.h, 1)

                act.wait_ge(loaded.h, loaded.at(16 * NL))
                take(0)
                for u in range(NU):
                    if u + 1 < NU:
                        take(u + 1)
                    give(u)

            @block.vector
            def _(dve):
                ch = Chain(dve, dve_chain)
                dve.wait_ge(loaded.h, loaded.at(16 * NL))
                dve.wait_ge(sq.h, sq.at(2 * NT))
                for i, w in ((0, ACQ), (1, AC)):
                    roots.ask(dve, dve.tensor_scalar(ss[:, i, :], ss[:, i, :], 1.0 / w, EPS, ALU.mult, ALU.add))
                for t in range(NT):
                    dve.scalar_tensor_tensor(CN[:, t, 0:ACQ], PA[:, t, 0:ACQ], ss[:, 0, t:t + 1], gq[:, :],
                                             ALU.mult, ALU.mult).then_inc(cn.h, 1)
                    dve.scalar_tensor_tensor(CN[:, t, ACQ:], PA[:, t, ACQ:ACQ + AC], ss[:, 1, t:t + 1], gc[:, :],
                                             ALU.mult, ALU.mult).then_inc(cn.h, 1)
                for u, (kind, t, kt) in enumerate(units):
                    y = Y[:, u % 2, :, :]
                    if kind == "k":
                        if u >= 2:
                            dve.wait_ge(t2.h, t2.at(u - 1))
                        src = PA[:, t, ACQ + AC:] if t < 4 else PA[:, 4, ACQ + AC:] if t == 6 else KRC[:, t - 4, :]
                        ch(dve.tensor_copy(y[:, :, ANOPE:], src.unsqueeze(1).broadcast_to([P, AH, AROPE])))
                    dve.wait_ge(cp.h, cp.at(u + 1))
                    rms_heads(dve, ch, roots, y, SQ[:, :, :], hs[:, :], AH, AQK)
                    ch(dve.tensor_tensor(y, y, gains[:, int(kind == "k"), :].unsqueeze(1).broadcast_to([P, AH, AQK]), ALU.mult))
                    rotate(dve, ch, y[:, :, ANOPE:], RT[:, kt, :], RC[:, :, :, :], RS[:, :, :, :], AH, 16, ro)
                dve_chain.end(ch.n)

            @block.gpsimd
            def _(pool):
                for i in range(2):
                    roots.give(pool, i, ss[:, i, :])
                for u in range(NU):
                    roots.give(pool, 2 + u, hs[:, :])

            @block.tensor
            def _(pe):
                for t in range(NT):
                    pe.wait_ge(cn.h, cn.at(2 * t + 2))
                    if t >= 2:
                        pe.wait_ge(ev.h, ev.at(2 * t - 2))
                    for k in range(3):
                        m = pe.transpose(bank[t % 2][:, k * P:(k + 1) * P], CN[:, t, k * P:(k + 1) * P], ident)
                    m.then_inc(tr.h, 1)

                def lift(u):
                    kind, t, kt = units[u]
                    if u >= 2:
                        pe.wait_ge(cp.h, cp.at(u - 1))
                    for b in range(2):
                        dst = bank[2 * (u % 2) + b]
                        if kind == "q":
                            for k in range(2):
                                m = pe.matmul(dst[:, 0:384], CQT[:, k, t * P:(t + 1) * P],
                                              wuq[:, k, b * 384:(b + 1) * 384], start=(k == 0), stop=(k == 1))
                        else:
                            m = pe.matmul(dst[:, :], LT[:, t * P:(t + 1) * P], wukv[:, b * 512:(b + 1) * 512],
                                          start=True, stop=True)
                    m.then_inc(up.h, 1)

                pe.wait_ge(ev.h, ev.at(2 * NT))
                pe.wait_ge(loaded.h, loaded.at(16 * NL))
                lift(0)
                for u in range(NU):
                    if u + 1 < NU:
                        lift(u + 1)
                    pe.wait_ge(ro.h, ro.at(u + 1))
                    if u >= 2:
                        pe.wait_ge(e2.h, e2.at(2 * (u - 1)))
                    for h in range(AH):
                        m = pe.transpose(bank[4 + 2 * (u % 2) + h // 4][0:AQK, (h % 4) * P:(h % 4 + 1) * P],
                                         Y[:, u % 2, h, :], ident)
                    m.then_inc(t2.h, 1)
        loaded.end(16 * NL), stored.end(160), sq.end(2 * NT), cn.end(2 * NT), tr.end(NT), ev.end(2 * NT)
        roots.end()
        up.end(NU), cp.end(NU), ro.end(NU), t2.end(NU), e2.end(2 * NU)
    attention("A", AQK, QT, lambda a, h, c, n: KT[0:AQK, h, c:c + n], lambda a, h, k: V[:, k, h, :],
              MSK, float(AQK) ** -0.5, OC)
    st.close()


def rms_heads(dve, ch, roots, y, sq, hs, heads, width):
    ch(dve.tensor_tensor(sq, y, y, ALU.mult))
    ch(dve.tensor_reduce(hs, sq, AX.X, ALU.add))
    roots.ask(dve, dve.tensor_scalar(hs, hs, 1.0 / width, EPS, ALU.mult, ALU.add))
    ch(dve.tensor_tensor(y, y, hs.unsqueeze(2).broadcast_to([P, heads, width]), ALU.mult))


def rotate(dve, ch, y, cs, rc, rs, heads, half, done):
    y4 = y.rearrange("p h (a n) -> p h a n", a=2)
    cos = cs[:, 0:half].unsqueeze(1)
    sin = cs[:, half:2 * half].unsqueeze(1)
    for a in range(2):
        ch(dve.tensor_tensor(rc[:, :, a, :], y4[:, :, a, :], cos.broadcast_to([P, heads, half]), ALU.mult))
        ch(dve.tensor_tensor(rs[:, :, a, :], y4[:, :, 1 - a, :], sin.broadcast_to([P, heads, half]), ALU.mult))
    ch(dve.tensor_tensor(y4[:, :, 0, :], rc[:, :, 0, :], rs[:, :, 0, :], ALU.subtract))
    ins = dve.tensor_tensor(y4[:, :, 1, :], rc[:, :, 1, :], rs[:, :, 1, :], ALU.add)
    if done is None:
        ch(ins)
    else:
        ins.then_inc(done.h, 1)


def project_out(nc, w_dram, sb, sig, bank, ident, OC, OBT, OD, X, tag):
    loaded, tr, ev, mm_, ad = (sig(n) for n in ("loaded", "transposed", "evacuated", "products", "added"))
    with ExitStack() as st:
        W = sb(st, f"WO{tag}", [P, KD, D])
        OT = sb(st, f"OT{tag}", [P, 2, KD, P])
        nb = 1 if OD is None else 2
        with nc.Block() as block:
            @block.sync
            def _(sp):
                wv = w_dram.rearrange("(k p) n -> p k n", p=P)
                for i in range(2):
                    sp.dma_start(W[:, 4 * i:4 * i + 4, :], wv[:, 4 * i:4 * i + 4, :]).then_inc(loaded.h, 16)

            @block.tensor
            def _(pe):
                def turn(t):
                    if t >= 1:
                        pe.wait_ge(ev.h, ev.at(nb * t))
                    for b in range(nb):
                        src = (OC, OD)[b]
                        for k in range(4):
                            m = pe.transpose(bank[b][:, k * P:(k + 1) * P], src[:, t, k * P:(k + 1) * P], ident)
                        m.then_inc(tr.h, 1)

                def product(t):
                    pe.wait_ge(ev.h, ev.at(nb * (t + 1)))
                    if t >= 2:
                        pe.wait_ge(ad.h, ad.at(2 * (t - 1)))
                    for b in range(2):
                        for k in range(KD):
                            lhs = OT[:, t % 2, k, :] if k < 4 or OBT is None else OBT[:, k - 4, t * P:(t + 1) * P]
                            m = pe.matmul(bank[2 + 2 * (t % 2) + b][:, :], lhs, W[:, k, b * 512:(b + 1) * 512],
                                          start=(k == 0), stop=(k == KD - 1))
                        m.then_inc(mm_.h, 1)

                turn(0)
                pe.wait_ge(loaded.h, loaded.at(32))
                for t in range(NT):
                    if t + 1 < NT:
                        turn(t + 1)
                    product(t)

            @block.scalar
            def _(act):
                for t in range(NT):
                    for b in range(nb):
                        act.wait_ge(tr.h, tr.at(nb * t + b + 1))
                        if t >= 2:
                            act.wait_ge(mm_.h, mm_.at(2 * (t - 1)))
                        act.activation(OT[:, t % 2, 4 * b:4 * b + 4, :],
                                       bank[b][:, :].rearrange("p (k n) -> p k n", k=4), ACT.Copy).then_inc(ev.h, 1)

            @block.vector
            def _(dve):
                for t in range(NT):
                    for b in range(2):
                        dve.wait_ge(mm_.h, mm_.at(2 * t + b + 1))
                        x = X[:, t, b * 512:(b + 1) * 512]
                        dve.tensor_tensor(x, bank[2 + 2 * (t % 2) + b][:, :], x, ALU.add).then_inc(ad.h, 1)
        loaded.end(32), tr.end(nb * NT), ev.end(nb * NT), mm_.end(2 * NT), ad.end(2 * NT)


V_W0, V_A0, V_KK, V_KA, V_RK, V_LG, V_LB, V_MU = 0, 4, 8, 12, 16, 20, 24, 28


def rwkv(nc, io, sb, sig, bank, CST, PB, OBT, X):
    ident, onesbd = CST[:, 0:128], CST[:, 128:256]
    maskSI, mask16, maskO = CST[:, 256:512], CST[:, 512:640], CST[:, 640:768]
    stackI, scanm = CST[:, 768:832], CST[:, 832:1408]
    loaded, stored, dve_chain, act_chain = sig("loaded"), sig("stored"), sig("dve_chain"), sig("act_chain")
    st = ExitStack()
    AR = sb(st, "AR", [P, NCH, 4, 2, P])
    BB = sb(st, "BB", [P, NCH, 4, P])
    KB = sb(st, "KB", [P, NCH, 4, P])
    VC = sb(st, "VC", [P, NCH, 4, 64])
    PC = sb(st, "PCe", [P, NCH, 4])
    XV = X[:, :, :].rearrange("p t d -> p (t d)").rearrange("p (s n) -> p s n", s=8)
    G = XV[:, 0:4, :]
    with ExitStack() as s2:
        XS = sb(s2, "XS", [P, 5, TOK])
        W2A = sb(s2, "W2A", [P, 2, BW])
        G2 = sb(s2, "G2", [P, BW])
        BV = sb(s2, "BV", [P, V_MU + BT])
        oka = sb(s2, "oka", [P, 4])
        T4 = sb(s2, "T4", [P, TOK])
        T5 = sb(s2, "T5", [P, TOK])
        VB = sb(s2, "VB", [P, NCH, P])
        T0, T1, T2, T3 = (XV[:, 4 + i, 0:TOK] for i in range(4))
        R, K, V, LW, LG = (XS[:, i, :] for i in range(5))
        sh, tn, za, zg, zc, d1, e1, d2, sp1, d3, d4, sp2, d5, vb, vm, vcp = (sig(n) for n in (
            "shifted", "lora_in", "lora_out", "gates_taken", "zeroed", "summed", "exps", "kk_squared", "kk_sums",
            "kk_done", "bonus_in", "bonus_sums", "bonus_done", "v_blocks", "v_turned", "v_copied"))
        roots = Roots(sig)
        with nc.Block() as block:
            @block.sync
            def _(sp):
                sp.wait_ge(zc.h, zc.at(1))
                for dst, src in ((W2A[0:64, 0, :], io["b_w2"]), (W2A[64:P, 1, :], io["b_a2"]), (G2[:, :], io["b_g2"]),
                                 (BV[:, :], io["bvec"])):
                    sp.dma_start(dst, src).then_inc(loaded.h, 16)
                sp.wait_ge(loaded.h, loaded.at(64))

            @block.gpsimd
            def _(pool):
                pool.memset(W2A[:, :, :], 0.0).then_inc(zc.h, 1)
                pool.memset(AR[:, :, :, :, :], 0.0).then_inc(zc.h, 1)
                pool.memset(BB[:, :, :, :], 0.0).then_inc(zc.h, 1)
                pool.memset(KB[:, :, :, :], 0.0).then_inc(zc.h, 1)
                pool.memset(VB[:, :, :], 0.0).then_inc(zc.h, 1)
                for p in range(4):
                    roots.give(pool, p, T2)

            @block.vector
            def _(dve):
                ch = Chain(dve, dve_chain)

                def shift(slot, ft):
                    x = XS[:, slot, :]
                    ch(dve.tensor_tensor(x[:, 0:SEQ], PB[:, ft, 0:SEQ], PB[:, ft, 1:SEQ + 1], ALU.subtract))
                    ch(dve.tensor_tensor(x[:, SEQ:], PB[:, ft, SEQ + 1:TOK + 1], PB[:, ft, SEQ + 2:], ALU.subtract))
                    mu = BV[:, V_MU + ft:V_MU + ft + 1]
                    ch(dve.scalar_tensor_tensor(x[:, 0:SEQ], x[:, 0:SEQ], mu, PB[:, ft, 1:SEQ + 1], ALU.mult, ALU.add))
                    ch(dve.scalar_tensor_tensor(x[:, SEQ:], x[:, SEQ:], mu, PB[:, ft, SEQ + 2:], ALU.mult, ALU.add))

                def blocks(dst, in0, in1, scalar=None):
                    for h in range(2):
                        q = slice(64 * h, 64 * h + 64)
                        o = dst[q, :, 64 * h:64 * h + 64]
                        a = in0[q, :].rearrange("p (c n) -> p c n", c=NCH)
                        b = in1[q, :].rearrange("p (c n) -> p c n", c=NCH)
                        if scalar is None:
                            ch(dve.tensor_tensor(o, a, b, ALU.mult))
                        else:
                            ch(dve.scalar_tensor_tensor(o, a, scalar, b, ALU.mult, ALU.mult))

                dve.wait_ge(loaded.h, loaded.at(64))
                dve.wait_ge(zc.h, zc.at(5))
                shift(3, 12)
                shift(4, 13)
                ch(dve.tensor_scalar(oka[:, :], BV[:, V_KA:V_KA + 4], -1.0, 1.0, ALU.mult, ALU.add))
                dve.engine_nop().then_inc(sh.h, 1)
                for p in range(4):
                    shift(0, p)
                    shift(1, 4 + p)
                    shift(2, 8 + p)
                    dve.wait_ge(zg.h, zg.at(3 * p + 2))
                    ch(dve.tensor_tensor_scan(T1, scanm, T0, 0.0, ALU.mult, ALU.add))
                    dve.tensor_tensor(T2, T1, T0, ALU.subtract).then_inc(d1.h, 1)
                    dve.wait_ge(e1.h, e1.at(3 * p + 3))
                    ch(dve.tensor_scalar(T1, K, BV[:, V_KK + p:V_KK + p + 1], None, ALU.mult))
                    dve.tensor_tensor(T2, T1, T1, ALU.mult).then_inc(d2.h, 1)
                    dve.wait_ge(sp1.h, sp1.at(p + 1))
                    ch(dve.tensor_scalar(T2[:, 0:512], bank[6][:, :], 1e-12, None, ALU.add))
                    roots.ask(dve, dve.tensor_scalar(T2[:, 512:], bank[7][:, 0:64], 1e-12, None, ALU.add))
                    ch(dve.tensor_tensor(T1, T1, T2, ALU.mult))
                    blocks(AR[:, :, p, 0, :], T1, T0, -1.0)
                    ch(dve.tensor_scalar(T2, T3, BV[:, V_KA + p:V_KA + p + 1], oka[:, p:p + 1], ALU.mult, ALU.add))
                    ch(dve.tensor_tensor(K, K, T2, ALU.mult))
                    ch(dve.tensor_tensor(T3, T1, T3, ALU.mult))
                    blocks(BB[:, :, p, :], T3, T5)
                    blocks(KB[:, :, p, :], K, T5)
                    blocks(AR[:, :, p, 1, :], R, T4)
                    ch(dve.tensor_copy(PC[:, :, p], T4[:, 63:TOK:64]))
                    dve.scalar_tensor_tensor(T1, R, BV[:, V_RK + p:V_RK + p + 1], K, ALU.mult, ALU.mult).then_inc(d4.h, 1)
                    if p >= 1:
                        dve.wait_ge(vm.h, vm.at(p))
                    for h in range(2):
                        q = slice(64 * h, 64 * h + 64)
                        ins = dve.tensor_copy(VB[q, :, 64 * h:64 * h + 64], V[q, :].rearrange("p (c n) -> p c n", c=NCH))
                        ins.then_inc(vb.h, 1)
                    dve.wait_ge(sp2.h, sp2.at(p + 1))
                    dve.tensor_tensor(OBT[:, p, 0:512], bank[6][:, :], V[:, 0:512], ALU.mult).then_inc(d5.h, 1)
                    dve.tensor_tensor(OBT[:, p, 512:TOK], bank[7][:, 0:64], V[:, 512:], ALU.mult).then_inc(d5.h, 1)
                    dve.wait_ge(d5.h, d5.at(2 * p + 2))
                    dve.wait_ge(vb.h, vb.at(2 * p + 2))
                dve_chain.end(ch.n)

            @block.scalar
            def _(act):
                act.wait_ge(sh.h, sh.at(1))
                act.activation(LW[0:64, :], LW[0:64, :], ACT.Tanh).then_inc(tn.h, 1)
                act.activation(LG, LG, ACT.Sigmoid).then_inc(tn.h, 1)
                for p in range(4):
                    act.wait_ge(za.h, za.at(p + 1))
                    if p >= 1:
                        act.wait_ge(d5.h, d5.at(2 * p))
                    for i, (dst, col) in enumerate(((T0, V_W0), (T3, V_A0))):
                        act.activation(dst[:, 0:512], bank[2 * i][:, :], ACT.Sigmoid, bias=BV[:, col + p:col + p + 1])
                        act.activation(dst[:, 512:], bank[2 * i + 1][:, 0:64], ACT.Sigmoid,
                                       bias=BV[:, col + p:col + p + 1]).then_inc(zg.h, 1)
                    act.activation(G[:, p, 0:512], bank[4][:, :], ACT.Copy)
                    act.activation(G[:, p, 512:TOK], bank[5][:, 0:64], ACT.Copy).then_inc(zg.h, 1)
                    act.wait_ge(d1.h, d1.at(p + 1))
                    act.activation(T0, T2, ACT.Exp, scale=-DECAY).then_inc(e1.h, 1)
                    act.activation(T4[:, :], T1, ACT.Exp, scale=-DECAY).then_inc(e1.h, 1)
                    act.activation(T5[:, :], T1, ACT.Exp, scale=DECAY).then_inc(e1.h, 1)
                    act.wait_ge(vm.h, vm.at(p + 1))
                    act.activation(VC[:, 0:8, p, :], bank[0][:, :].rearrange("p (c n) -> p c n", c=8), ACT.Copy)
                    act.activation(VC[:, 8, p, :], bank[1][:, 0:64], ACT.Copy).then_inc(vcp.h, 1)

            @block.tensor
            def _(pe):
                pe.wait_ge(tn.h, tn.at(2))
                for p in range(4):
                    if p >= 1:
                        pe.wait_ge(vcp.h, vcp.at(p))
                    w = slice(p * P, (p + 1) * P)
                    for i, (lhs, rhs) in enumerate(((W2A[:, 0, w], LW), (W2A[:, 1, w], LW), (G2[:, w], LG))):
                        pe.matmul(bank[2 * i][:, :], lhs, rhs[:, 0:512], start=True, stop=True)
                        m = pe.matmul(bank[2 * i + 1][:, 0:64], lhs, rhs[:, 512:], start=True, stop=True)
                    m.then_inc(za.h, 1)
                    pe.wait_ge(d2.h, d2.at(p + 1))
                    pe.matmul(bank[6][:, :], onesbd, T2[:, 0:512], start=True, stop=True)
                    pe.matmul(bank[7][:, 0:64], onesbd, T2[:, 512:], start=True, stop=True).then_inc(sp1.h, 1)
                    pe.wait_ge(d4.h, d4.at(p + 1))
                    pe.matmul(bank[6][:, :], onesbd, T1[:, 0:512], start=True, stop=True)
                    pe.matmul(bank[7][:, 0:64], onesbd, T1[:, 512:], start=True, stop=True).then_inc(sp2.h, 1)
                    pe.wait_ge(vb.h, vb.at(2 * p + 2))
                    pe.wait_ge(zg.h, zg.at(3 * p + 3))
                    for c in range(NCH):
                        m = pe.matmul(bank[c // 8][:, (c % 8) * 64:(c % 8) * 64 + 64], VB[:, c, :], stackI,
                                      start=True, stop=True)
                    m.then_inc(vm.h, 1)
        roots.end()
        loaded.end(64), zc.end(5), sh.end(1), tn.end(2), za.end(4), zg.end(12), d1.end(4), e1.end(12), d2.end(4)
        sp1.end(4), d4.end(4), sp2.end(4), d5.end(8), vb.end(8), vm.end(4), vcp.end(4)

    with ExitStack() as s2:
        BV = sb(s2, "BV2", [P, V_MU + BT])
        XF = X[:, :, :].rearrange("p t d -> p (t d)")
        M1 = XF[:, 2560:3584].rearrange("p (q a n) -> p q a n", q=4, a=2)
        M2 = XF[:, 3584:4608].rearrange("p (q a n) -> p q a n", q=4, a=2)
        Bt = sb(s2, "Bt", [P, 4, P])
        Kt = sb(s2, "Kt", [P, 4, P])
        (Dt, Dg, O_, ID, D2, D2T, D4, D4T, D8T, W1, W2, WT, NTm) = (
            sb(s2, f"c{i}", [P, 4, P]) for i in range(13))
        ST = sb(s2, "STr", [P, 4, 64])
        TMP = sb(s2, "TMP", [P, 4, 64])
        SA = sb(s2, "SAr", [P, 4, 64])
        YC = sb(s2, "YC", [P, 4, 64])
        YQ = sb(s2, "YQ", [P, 4, 64])
        YB = sb(s2, "YB", [P, 4, P])
        ys = sb(s2, "ys", [P, 2, 4])
        stage, taken, bt = sig("stage_products"), sig("stage_taken"), sig("b_turned")
        NS, NC_ = 14, 40
        roots = Roots(sig)

        def v4(b):
            return b[:, :].rearrange("p (q n) -> p q n", q=4)

        def v64(b):
            return b[:, 0:256].rearrange("p (q n) -> p q n", q=4)

        def pe_chunk(pe, c, it):
            def go(k):
                pe.wait_ge(taken.h, taken.at(it * NS + k))

            def four(b, lhs, rhs, n=P):
                for p in range(4):
                    m = pe.matmul(b[:, p * n:(p + 1) * n], lhs(p), rhs(p), start=True, stop=True)
                return m

            if not (isinstance(it, int) and it == 0):
                go(0)
            for p in range(4):
                pe.matmul(bank[p // 2][:, (p % 2) * 256:(p % 2) * 256 + 256], BB[:, c, p, :],
                          AR[:, c, p, :, :].rearrange("p a n -> p (a n)"), start=True, stop=True)
                pe.matmul(bank[2 + p // 2][:, (p % 2) * 256:(p % 2) * 256 + 256], KB[:, c, p, :],
                          AR[:, c, p, :, :].rearrange("p a n -> p (a n)"), start=True, stop=True)
            four(bank[4], lambda p: AR[:, c, p, 0, :], lambda p: BB[:, c, p, :])
            for p in range(4):
                pe.transpose(bank[5][:, p * P:(p + 1) * P], BB[:, c, p, :], ident)
                m = pe.transpose(bank[6][:, p * P:(p + 1) * P], KB[:, c, p, :], ident)
            m.then_inc(stage.h, 1)
            go(1)
            four(bank[0], lambda p: Dt[:, p, :], lambda p: Dg[:, p, :])
            four(bank[1], lambda p: Dg[:, p, :], lambda p: Dt[:, p, :]).then_inc(stage.h, 1)
            go(2)
            four(bank[2], lambda p: D2T[:, p, :], lambda p: D2[:, p, :])
            four(bank[3], lambda p: D2[:, p, :], lambda p: D2T[:, p, :])
            four(bank[4], lambda p: D2T[:, p, :], lambda p: ID[:, p, :]).then_inc(stage.h, 1)
            go(3)
            four(bank[0], lambda p: D4[:, p, :], lambda p: D4T[:, p, :])
            four(bank[1], lambda p: D4T[:, p, :], lambda p: W1[:, p, :]).then_inc(stage.h, 1)
            go(4)
            four(bank[2], lambda p: D8T[:, p, :], lambda p: W2[:, p, :]).then_inc(stage.h, 1)
            go(5)
            for p in range(4):
                m = pe.transpose(bank[3][:, p * P:(p + 1) * P], W1[:, p, :], ident)
            m.then_inc(stage.h, 1)
            go(6)
            four(bank[4], lambda p: O_[:, p, :], lambda p: WT[:, p, :]).then_inc(stage.h, 1)
            go(7)
            four(bank[0], lambda p: NTm[:, p, :], lambda p: W1[:, p, :]).then_inc(stage.h, 1)
            go(8)
            four(bank[1], lambda p: NTm[:, p, :], lambda p: W2[:, p, :]).then_inc(stage.h, 1)
            go(9)
            four(bank[2], lambda p: NTm[:, p, :], lambda p: W2[:, p, :]).then_inc(stage.h, 1)
            go(10)
            for p in range(4):
                o = bank[3][:, p * 64:(p + 1) * 64]
                pe.matmul(o, AR[:, c, p, 0, :], ST[:, p, :], start=True, stop=False)
                m = pe.matmul(o, M2[:, p, 0, :], VC[:, c, p, :], start=False, stop=True)
            m.then_inc(stage.h, 1)
            go(11)
            four(bank[4], lambda p: W2[:, p, :], lambda p: TMP[:, p, :], 64).then_inc(stage.h, 1)
            go(12)
            for p in range(4):
                o = bank[5][:, p * 64:(p + 1) * 64]
                pe.matmul(o, AR[:, c, p, 1, :], ST[:, p, :], start=True, stop=False)
                pe.matmul(o, M1[:, p, 1, :], SA[:, p, :], start=False, stop=False)
                pe.matmul(o, M2[:, p, 1, :], VC[:, c, p, :], start=False, stop=True)
                o = bank[6][:, p * 64:(p + 1) * 64]
                pe.matmul(o, Bt[:, p, :], SA[:, p, :], start=True, stop=False)
                m = pe.matmul(o, Kt[:, p, :], VC[:, c, p, :], start=False, stop=True)
            m.then_inc(stage.h, 1)
            go(13)
            four(bank[7], lambda p: YB[:, p, :], lambda p: stackI, 64).then_inc(stage.h, 1)

        def dve_chunk(dve, c, it):
            ch = Chain(dve, dve_chain, it * NC_)

            def ready(k):
                dve.wait_ge(stage.h, stage.at(it * NS + k))

            bc4 = lambda m: m.unsqueeze(1).broadcast_to([P, 4, P])
            tt = dve.tensor_tensor
            ready(1)
            for g, M in ((0, M1), (2, M2)):
                for q in range(2):
                    ch(tt(M[:, 2 * q:2 * q + 2, :, :].rearrange("p q a n -> p q (a n)"),
                          bank[g + q][:, :].rearrange("p (q n) -> p q n", q=2),
                          maskSI.unsqueeze(1).broadcast_to([P, 2, 256]), ALU.mult))
            ch(tt(Dt[:, :, :], v4(bank[4]), bc4(CST[:, 1408:1536]), ALU.mult))
            ch(tt(Dg[:, :, :], M1[:, :, 0, :], bc4(mask16), ALU.mult))
            ch(tt(O_[:, :, :], M1[:, :, 0, :], bc4(maskO), ALU.mult))
            ch(tt(ID[:, :, :], Dg[:, :, :], bc4(ident), ALU.add))
            ch(dve.tensor_copy(Bt[:, :, :], v4(bank[5])))
            ch(dve.tensor_copy(Kt[:, :, :], v4(bank[6])))
            dve.engine_nop().then_inc(taken.h, 1)
            steps = [
                (2, [(D2, 0, None), (D2T, 1, None)]),
                (3, [(D4, 2, None), (D4T, 3, None), (W1, 4, ID)]),
                (4, [(D8T, 0, None), (W2, 1, W1)]),
                (5, [(W1, 2, W2)]),
                (6, [(WT, 3, None)]),
                (7, [(NTm, 4, None)]),
                (8, [(W2, 0, W1)]),
                (9, [(W2, 1, W1)]),
                (10, [(W2, 2, W1)]),
            ]
            for k, takes in steps:
                ready(k)
                for dst, b, plus in takes:
                    if plus is None:
                        ch(dve.tensor_copy(dst[:, :, :], v4(bank[b])))
                    else:
                        ch(tt(dst[:, :, :], v4(bank[b]), plus[:, :, :], ALU.add))
                dve.engine_nop().then_inc(taken.h, 1)
            ready(11)
            ch(dve.tensor_copy(TMP[:, :, :], v64(bank[3])))
            dve.engine_nop().then_inc(taken.h, 1)
            ready(12)
            ch(dve.tensor_copy(SA[:, :, :], v64(bank[4])))
            dve.engine_nop().then_inc(taken.h, 1)
            ready(13)
            ch(tt(ST[:, :, :], v64(bank[6]), ST[:, :, :], ALU.add))
            ch(tt(ST[:, :, :], ST[:, :, :], PC[:, c, :].unsqueeze(2).broadcast_to([P, 4, 64]), ALU.mult))
            y4 = YC[:, :, :]
            ch(dve.tensor_reduce(ys[:, 0, :], v64(bank[5]), AX.X, ALU.add))
            ch(dve.tensor_scalar(ys[:, 0, :], ys[:, 0, :], 1.0 / BHD, None, ALU.mult))
            ch(tt(y4, v64(bank[5]), ys[:, 0, :].unsqueeze(2).broadcast_to([P, 4, 64]), ALU.subtract))
            ch(tt(YQ[:, :, :], y4, y4, ALU.mult))
            ch(dve.tensor_reduce(ys[:, 1, :], YQ[:, :, :], AX.X, ALU.add))
            roots.ask(dve, dve.tensor_scalar(ys[:, 1, :], ys[:, 1, :], 1.0 / BHD, BLN_EPS, ALU.mult, ALU.add))
            for h in range(2):
                q = slice(64 * h, 64 * h + 64)
                ch(tt(YB[q, :, 64 * h:64 * h + 64], YC[q, :, :],
                      ys[q, 1, :].unsqueeze(2).broadcast_to([64, 4, 64]), ALU.mult))
            dve.engine_nop().then_inc(taken.h, 1)
            ready(14)
            for p in range(4):
                ch(dve.tensor_scalar(YQ[:, p, :], bank[7][:, p * 64:(p + 1) * 64], BV[:, V_LG + p:V_LG + p + 1],
                                     BV[:, V_LB + p:V_LB + p + 1], ALU.mult, ALU.add))
            o = OBT[:, :, c * 64:c * 64 + 64]
            ch(tt(o, o, YQ[:, :, :], ALU.add))
            ch(tt(o, o, G[:, :, c * 64:c * 64 + 64], ALU.mult))
            dve.engine_nop().then_inc(taken.h, 1)
            assert ch.n == NC_, ch.n

        last = NCH - 1
        zs, pd = sig("state_zeroed"), sig("prompt_state_done")
        with nc.Block() as block:
            @block.sync
            def _(sp):
                sp.dma_start(BV[:, :], io["bvec"]).then_inc(loaded.h, 16)
                sp.wait_ge(taken.h, taken.at(last * NS))
                sp.dma_start(io["out_b_wkv_p"], ST[:, :, :]).then_inc(stored.h, 16)
                sp.wait_ge(stored.h, stored.at(16))
                sp.dma_start(ST[:, :, :], io["wkv_t"]).then_inc(loaded.h, 16)
                sp.wait_ge(taken.h, taken.at(NCH * NS))
                sp.dma_start(io["out_b_wkv_s"], ST[:, :, :]).then_inc(stored.h, 16)
                sp.wait_ge(stored.h, stored.at(32))

            @block.tensor
            def _(pe):
                pe.wait_ge(zs.h, zs.at(1))
                pe_chunk(pe, 0, 0)
                for c in range(1, last):
                    pe_chunk(pe, c, c)
                pe.wait_ge(loaded.h, loaded.at(32))
                pe_chunk(pe, last, last)

            @block.gpsimd
            def _(pool):
                for c in range(NCH):
                    roots.give(pool, c, ys[:, 1, :])

            @block.vector
            def _(dve):
                dve.memset(ST[:, :, :], 0.0).then_inc(zs.h, 1)
                dve.wait_ge(zs.h, zs.at(1))
                dve.memset(YB[:, :, :], 0.0).then_inc(zs.h, 1)
                dve.wait_ge(zs.h, zs.at(2))
                dve.wait_ge(loaded.h, loaded.at(16))
                for c in range(last):
                    dve_chunk(dve, c, c)
                dve.wait_ge(loaded.h, loaded.at(32))
                dve_chunk(dve, last, last)
        roots.end()
        loaded.end(32), stored.end(32), zs.end(2), stage.end(NCH * NS), taken.end(NCH * NS), dve_chain.end(NCH * NC_)
    st.close()


def peer(nc, io, layer, sb, sig, bank, ident, X, norm):
    loaded, dve_chain = sig("loaded"), sig("dve_chain")
    st = ExitStack()
    L = f"l{layer}"
    XN = sb(st, f"XN{L}", [P, NT, D])
    QP = sb(st, f"QP{L}", [P, NT, PH, P])
    KB = sb(st, f"KY{L}", [P, PH + 1, 2 * NK])
    IOT = sb(st, f"IOT{L}", [P, PK])
    with ExitStack() as s2:
        XT = sb(s2, f"XT{L}", [P, KD, PADT])
        WQ = sb(s2, f"WQ{L}", [P, KD, D])
        wl, kz, kl = sig("weights_loaded0"), sig("keys_zeroed"), sig("keys_loaded")
        mm_, ev = sig("products"), sig("evacuated")

        def load_w(sp):
            sp.dma_start(WQ[:, :, :], io[f"l{layer}_peer_wq"].rearrange("(k p) n -> p k n", p=P)).then_inc(wl.h, 16)

        norm(s2, L, io[f"l{layer}_norm_ffn"], False, XN, XT, load_w)
        with nc.Block() as block:
            @block.sync
            def _(sp):
                sp.wait_ge(kz.h, kz.at(1))
                kv = io[f"keys_t{layer}"]
                for half in range(2):
                    q, n = slice(64 * half, 64 * half + 64), slice(NK * half, NK * half + NK)
                    sp.dma_start(KB[q, 0:PH, n], kv[:, half].rearrange("h d n -> d h n")).then_inc(kl.h, 16)
                    sp.dma_start(KB[q, PH, n], kv[0, half]).then_inc(kl.h, 16)
                sp.wait_ge(kl.h, kl.at(64))

            @block.gpsimd
            def _(pool):
                pool.memset(KB[:, :, :], 0.0).then_inc(kz.h, 1)
                pool.iota(IOT[:, :], [[1, PK]], base=0, channel_multiplier=0, allow_small_or_imprecise_dtypes=True)

            @block.tensor
            def _(pe):
                pe.wait_ge(wl.h, wl.at(16))
                n = 0
                for h in range(PH):
                    for a, b in ((0, 512), (512, PADT)):
                        if n >= 4:
                            pe.wait_ge(ev.h, ev.at(n - 3))
                        for k in range(KD):
                            m = pe.matmul(bank[n % 4][:, 0:b - a], WQ[:, k, h * P:(h + 1) * P], XT[:, k, a:b],
                                          start=(k == 0), stop=(k == KD - 1))
                        m.then_inc(mm_.h, 1)
                        n += 1

            @block.scalar
            def _(act):
                n = 0
                for h in range(PH):
                    for t0, t1 in ((0, 4), (4, 5)):
                        act.wait_ge(mm_.h, mm_.at(n + 1))
                        act.activation(QP[:, t0:t1, h, :],
                                       bank[n % 4][:, 0:(t1 - t0) * P].rearrange("p (t n) -> p t n", n=P),
                                       ACT.Copy).then_inc(ev.h, 1)
                        n += 1
        wl.end(16), kz.end(1), kl.end(64), mm_.end(16), ev.end(16)

    QS = sb(st, f"QS{L}", [P, P])
    QPF = QP[:, :, :, :].rearrange("p t h n -> p (t h n)")
    ring = sb(st, f"ring{L}", [P, RING, 2 * D])
    J = sb(st, f"J{L}", [P, 2, D])
    SC = sb(st, f"SC{L}", [P, 2, NK])
    SW = sb(st, f"SW{L}", [P, 2, NK])
    TS_ = sb(st, f"TS{L}", [P, 2, PK])
    TI = sb(st, f"TI{L}", [P, 2, PK], U32)
    TF = sb(st, f"TF{L}", [P, 2, PK])
    CA = sb(st, f"CA{L}", [P, PK, PK])
    CW = sb(st, f"CW{L}", [P, PK * PK])
    BS = sb(st, f"BS{L}", [P, PK])
    BP = sb(st, f"BP{L}", [P, PK], U32)
    BQ = sb(st, f"BQ{L}", [P, 2, PK], U32)
    BF = sb(st, f"BF{L}", [P, 2, PK])
    OH = sb(st, f"OH{L}", [P, PK, PK])
    SEL = sb(st, f"SEL{L}", [P, 2, PK])
    EF = sb(st, f"EF{L}", [P, PK])
    EI = sb(st, f"EI{L}", [P, 2, PK], U32)
    NM = sb(st, f"NM{L}", [P, 1])
    GX = sb(st, f"GX{L}", [P, PK])
    GS = sb(st, f"GS{L}", [P, 2])
    GT = sb(st, f"GT{L}", [P, 2, PK])
    HD = sb(st, f"HD{L}", [P, 2, PK])
    HG = sb(st, f"HG{L}", [P, 2, PK])
    HW = sb(st, f"HW{L}", [P, 2, PK])
    rp, rc, rm, rx, ri, ud, ge, vd = (sig(n) for n in (
        "key_scores", "key_scores_copied", "best_known", "gate_exps", "experts_known", "u_dots", "gelus", "v_added"))
    passed, passed_v = sig("slot_waits_passed"), sig("score_waits_passed")
    qs, steps = sig("queries_placed"), sig("route_steps")
    gd = [sig(f"gathered{i}") for i in range(RING)]
    rows = io[f"uv{layer}"]

    def pe_route(pe, g, qoff, kh):
        pe.wait_ge(qs.h, qs.at(g))
        pe.wait_ge(rc.h, rc.at(g))
        pe.matmul(bank[0][:, 0:2 * NK], QS[:, :],
                  KB[:, kh, :], start=True, stop=True).then_inc(rp.h, 1)

    def act_route_in(act, g, qoff):
        act.wait_ge(rp.h, rp.at(g))
        act.activation(QS[:, :], QPF[:, bass.ds(qoff, P)], ACT.Copy).then_inc(qs.h, 1)
        act.wait_ge(rp.h, rp.at(g + 1))
        act.wait_ge(ri.h, ri.at(g))
        act.activation(SC[:, :, :].rearrange("p a n -> p (a n)"), bank[0][:, 0:2 * NK], ACT.Copy).then_inc(rc.h, 1)

    def act_route_exp(act, g):
        act.wait_ge(rm.h, rm.at(g + 1))
        act.activation(GX[:, :], BS[:, :], ACT.Exp, bias=NM[:, :], accum_out=GS[:, 0:1]).then_inc(rx.h, 1)

    def dve_route(dve, g, par):
        dve.sem_clear(steps.h)
        ch = Chain(dve, steps)
        dve.wait_ge(rc.h, rc.at(g + 1))
        dve.sem_inc(passed_v.h, 1)
        for a in range(2):
            ch(dve.max(TS_[:, a, 0:8], SC[:, a, :]))
            ch(dve.match_replace(SW[:, a, :], TS_[:, a, 0:8], SC[:, a, :], -3e38))
            ch(dve.max(TS_[:, a, 8:16], SW[:, a, :]))
            ch(dve.max_index(TI[:, a, 0:8], TS_[:, a, 0:8], SC[:, a, :]))
            ch(dve.max_index(TI[:, a, 8:16], TS_[:, a, 8:16], SW[:, a, :]))
        ch(dve.tensor_copy(TF[:, :, :], TI[:, :, :]))
        ch(dve.tensor_tensor(CA[:, :, :], TS_[:, 0, :].unsqueeze(2).broadcast_to([P, PK, PK]),
                             TS_[:, 1, :].unsqueeze(1).broadcast_to([P, PK, PK]), ALU.add))
        cf = CA[:, :, :].rearrange("p a b -> p (a b)")
        ch(dve.max(BS[:, 0:8], cf))
        ch(dve.match_replace(CW[:, :], BS[:, 0:8], cf, -3e38))
        ch(dve.max(BS[:, 8:16], CW[:, :]))
        dve.tensor_scalar(NM[:, :], BS[:, 0:1], -1.0, None, ALU.mult).then_inc(rm.h, 1)
        ch(dve.max_index(BP[:, 0:8], BS[:, 0:8], cf))
        ch(dve.max_index(BP[:, 8:16], BS[:, 8:16], CW[:, :]))
        ch(dve.tensor_single_scalar(BQ[:, 0, :], BP[:, :], 4, op=ALU.logical_shift_right))
        ch(dve.tensor_single_scalar(BQ[:, 1, :], BP[:, :], 15, op=ALU.bitwise_and))
        ch(dve.tensor_copy(BF[:, :, :], BQ[:, :, :]))
        for a in range(2):
            ch(dve.tensor_tensor(OH[:, :, :], BF[:, a, :].unsqueeze(2).broadcast_to([P, PK, PK]),
                                 IOT[:, :].unsqueeze(1).broadcast_to([P, PK, PK]), ALU.is_equal))
            ch(dve.tensor_tensor(OH[:, :, :], OH[:, :, :], TF[:, a, :].unsqueeze(1).broadcast_to([P, PK, PK]),
                                 ALU.mult))
            ch(dve.tensor_reduce(SEL[:, a, :], OH[:, :, :], AX.X, ALU.add))
        ch(dve.scalar_tensor_tensor(EF[:, :], SEL[:, 0, :], float(NK), SEL[:, 1, :], ALU.mult, ALU.add))
        ch(dve.tensor_copy(EI[:, par, :], EF[:, :]))
        dve.wait_ge(rx.h, rx.at(g + 1))
        ch(dve.reciprocal(GS[:, 1:2], GS[:, 0:1]))
        dve.tensor_scalar(GT[:, par, :], GX[:, :], GS[:, 1:2], None, ALU.mult).then_inc(ri.h, 1)

    def use(g, k):
        return g * (SLOTS // RING) + k // RING + 1

    def pool_group(pool, g, par, n):
        pool.wait_ge(ri.h, ri.at(g + 1))
        for k in range(SLOTS):
            pool.wait_ge(vd.h, vd.at(g * SLOTS + k + 1))
            pool.sem_inc(passed.h, 1)
            pool.indirect_dma_start(ring[0:n, k % RING, :], None, rows,
                                    bass.IndirectOffsetOnAxis(ap=EI[0:n, par, k:k + 1], axis=0)
                                    ).then_inc(gd[k % RING].h, 16)

    def act_group(act, g, par, n):
        for b in range(SLOTS // 2):
            act.wait_ge(ud.h, ud.at(g * SLOTS + 2 * b + 2 + 2))
            act.activation(HG[0:n, par, 2 * b:2 * b + 2], HD[0:n, par, 2 * b:2 * b + 2], ACT.Gelu).then_inc(ge.h, 1)

    def dve_group(dve, ch, g, t, par, n, route=None):
        vd_base = g * SLOTS

        def dot(k):
            dve.wait_ge(gd[k % RING].h, gd[k % RING].at(16 * use(g, k)))
            dve.wait_ge(ud.h, ud.at(g * SLOTS + k + 1))
            dve.scalar_tensor_tensor(J[0:n, k % 2, :], ring[0:n, k % RING, 0:D], 1.0, XN[0:n, t, :], ALU.mult, ALU.mult,
                                     accum_out=HD[0:n, par, k:k + 1]).then_inc(ud.h, 1)

        def add(k):
            dve.wait_ge(vd.h, vd.at(vd_base + k + RING))
            dve.scalar_tensor_tensor(X[0:n, t, :], ring[0:n, k % RING, D:2 * D], HW[0:n, par, k:k + 1],
                                     X[0:n, t, :], ALU.mult, ALU.add).then_inc(vd.h, 1)

        def weigh(b):
            dve.wait_ge(ge.h, ge.at(g * (SLOTS // 2) + b + 1))
            q = slice(2 * b, 2 * b + 2)
            ch(dve.tensor_tensor(HW[0:n, par, q], HG[0:n, par, q], GT[0:n, par, q], ALU.mult))

        for b in range(SLOTS // 2):
            dot(2 * b)
            if b:
                weigh(b - 1)
                add(2 * b - 2)
            dot(2 * b + 1)
            if b:
                add(2 * b - 1)
            if b == 1 and route is not None:
                route()
        weigh(SLOTS // 2 - 1)
        add(SLOTS - 2)
        add(SLOTS - 1)

    NG = SLOTS // 2
    TILES = NT - 1

    def groups(eng, body):
        with eng.Fori(0, TILES) as t, eng.Fori(0, PH // 2) as j:
            for par in range(2):
                body(t * PH + j * 2 + par, t, par, j * 2 + par + 1, P, False)
        with eng.Fori(0, PH // 2 - 1) as j:
            for par in range(2):
                body(TILES * PH + j * 2 + par, TILES, par, j * 2 + par + 1, DEC, False)
        for par in range(2):
            body(NT * PH - 2 + par, TILES, par, PH - 1 + par, DEC, par == 1)

    with nc.Block() as block:
        @block.gpsimd
        def _(pool):
            groups(pool, lambda g, t, par, hn, n, last: pool_group(pool, g, par, n))

        @block.tensor
        def _(pe):
            pe.matmul(bank[0][:, 0:2 * NK], QP[:, 0, 0, :], KB[:, 0, :], start=True, stop=True).then_inc(rp.h, 1)

            def body(g, t, par, hn, n, last):
                if not last:
                    pe_route(pe, g + 1, (g + 1) * P, hn)
            groups(pe, body)

        @block.scalar
        def _(act):
            act.wait_ge(rp.h, rp.at(1))
            act.activation(SC[:, :, :].rearrange("p a n -> p (a n)"), bank[0][:, 0:2 * NK], ACT.Copy).then_inc(rc.h, 1)
            act_route_exp(act, 0)

            def body(g, t, par, hn, n, last):
                if last:
                    act_group(act, g, par, n)
                    return
                act_route_in(act, g + 1, (g + 1) * P)
                for b in range(SLOTS // 2):
                    act.wait_ge(ud.h, ud.at(g * SLOTS + 2 * b + 2 + 2))
                    act.activation(HG[0:n, par, 2 * b:2 * b + 2], HD[0:n, par, 2 * b:2 * b + 2],
                                   ACT.Gelu).then_inc(ge.h, 1)
                    if b == 1:
                        act_route_exp(act, g + 1)
            groups(act, body)

        @block.vector
        def _(dve):
            dve.engine_nop().then_inc(vd.h, RING)
            dve.engine_nop().then_inc(ud.h, 2)
            dve_route(dve, 0, 0)

            def body(g, t, par, hn, n, last):
                ch = Chain(dve, dve_chain, g * NG)
                dve_group(dve, ch, g, t, par, n, None if last else lambda: dve_route(dve, g + 1, 1 - par))
            groups(dve, body)
    G = NT * PH
    dve_chain.end(G * NG)
    passed.end(G * SLOTS), passed_v.end(G)
    qs.end(G - 1), rp.end(G), rc.end(G), rm.end(G), rx.end(G), ri.end(G), ud.end(2 + G * SLOTS), ge.end(G * SLOTS // 2)
    vd.end(RING + G * SLOTS)
    for s in gd:
        s.end(16 * G * SLOTS // RING)
    st.close()


def layer1(nc, io, sb, sig, bank, CST, X, OC, norm, attention):
    ident = CST[:, 0:128]
    loaded, stored, dve_chain = sig("loaded"), sig("stored"), sig("dve_chain")
    st = ExitStack()
    PCm = sb(st, "PCm", [P, NT, CCOLS])
    OD = sb(st, "OD", [P, NT, 2 * DW])
    with ExitStack() as s2:
        XT = sb(s2, "XT1", [P, KD, PADT])
        XN = sb(s2, "XN1", [P, NT, D])
        W = sb(s2, "W1", [P, KD, 1024 + 512])
        CW = [(0, 512, 0), (512, 1024, 512), (1024, CCOLS, 1024), (CCOLS, CCOLS + 512, 0), (CCOLS + 512, CCOLS + 1024, 512)]
        wv = io["l1_w_in"].rearrange("(k p) n -> p k n", p=P)
        wl = [sig(f"weights_loaded{i}") for i in range(5)]
        mm_, ev = sig("products"), sig("evacuated")

        def load_w(sp):
            for i in range(3):
                a, b, o = CW[i]
                sp.dma_start(W[:, :, o:o + b - a], wv[:, :, a:b]).then_inc(wl[i].h, 16)

        norm(s2, "c", io["l1_norm_mix"], False, XN, XT, load_w)
        with nc.Block() as block:
            @block.sync
            def _(sp):
                for i in (3, 4):
                    a, b, o = CW[i]
                    sp.wait_ge(mm_.h, mm_.at(NT * (i - 2)))
                    sp.dma_start(W[:, :, o:o + b - a], wv[:, :, a:b]).then_inc(wl[i].h, 16)

            @block.tensor
            def _(pe):
                n = 0
                for i, (a, b, o) in enumerate(CW):
                    pe.wait_ge(wl[i].h, wl[i].at(16))
                    for t in range(NT):
                        if n >= 4:
                            pe.wait_ge(ev.h, ev.at(n - 3))
                        for k in range(KD):
                            m = pe.matmul(bank[n % 4][:, 0:b - a], XT[:, k, t * P:(t + 1) * P], W[:, k, o:o + b - a],
                                          start=(k == 0), stop=(k == KD - 1))
                        m.then_inc(mm_.h, 1)
                        n += 1

            @block.scalar
            def _(act):
                n = 0
                for i, (a, b, o) in enumerate(CW):
                    for t in range(NT):
                        act.wait_ge(mm_.h, mm_.at(n + 1))
                        src = bank[n % 4][:, 0:b - a]
                        if i < 3:
                            ins = act.activation(PCm[:, t, a:b], src, ACT.Copy)
                        else:
                            ins = act.activation(OD[:, t, a - CCOLS:b - CCOLS], src, ACT.Gelu)
                        ins.then_inc(ev.h, 1)
                        n += 1
        for s in wl:
            s.end(16)
        mm_.end(5 * NT), ev.end(5 * NT)

    with ExitStack() as s2:
        lg = sb(s2, "dlg", [P, DW])
        lb = sb(s2, "dlb", [P, DW])
        WT = sb(s2, "dwt", [P, 4, P])
        DB = sb(s2, "dbs", [P, 4])
        VN = sb(s2, "VN", [P, NT, DW])
        JQ = sb(s2, "JQ", [P, DW])
        ms = sb(s2, "ms", [P, NT, 2])
        roots = Roots(sig)
        wm, vn, mm_, dd = sig("mix_masked"), sig("normed"), sig("products"), sig("added")
        with nc.Block() as block:
            @block.sync
            def _(sp):
                for dst, src in ((lg[:, :], io["d_ln_g"].partition_broadcast(P)),
                                 (lb[:, :], io["d_ln_b"].partition_broadcast(P)),
                                 (WT[:, :, :], io["dws_t"]), (DB[:, :], io["dbs_t"])):
                    sp.dma_start(dst, src).then_inc(loaded.h, 16)
                sp.wait_ge(vn.h, vn.at(NT))
                sp.dma_start(io["out_d_v_s"][0], VN[0:DEC, 4, :]).then_inc(stored.h, 16)
                sp.wait_ge(stored.h, stored.at(16))

            @block.gpsimd
            def _(pool):
                pool.wait_ge(loaded.h, loaded.at(64))
                pool.affine_select(out=WT[:, :, :], in_=WT[:, :, :], compare_op=ALU.is_ge, fill=0.0, base=0,
                                   pattern=[[0, 4], [1, P]], channel_multiplier=-1).then_inc(wm.h, 1)
                for t in range(NT):
                    roots.give(pool, t, ms[:, t, 1:2])

            @block.vector
            def _(dve):
                ch = Chain(dve, dve_chain)
                dve.wait_ge(loaded.h, loaded.at(64))
                for t in range(NT):
                    v = OD[:, t, DW:]
                    mean, var = ms[:, t, 0:1], ms[:, t, 1:2]
                    ch(dve.tensor_reduce(mean, v, AX.X, ALU.add))
                    ch(dve.tensor_scalar(mean, mean, 1.0 / DW, None, ALU.mult))
                    ch(dve.tensor_scalar(VN[:, t, :], v, mean, None, ALU.subtract))
                    ch(dve.tensor_tensor(JQ[:, :], VN[:, t, :], VN[:, t, :], ALU.mult))
                    ch(dve.tensor_reduce(var, JQ[:, :], AX.X, ALU.add))
                    roots.ask(dve, dve.tensor_scalar(var, var, 1.0 / DW, EPS, ALU.mult, ALU.add))
                    ch(dve.scalar_tensor_tensor(VN[:, t, :], VN[:, t, :], var, lg[:, :], ALU.mult, ALU.mult))
                    dve.tensor_tensor(VN[:, t, :], VN[:, t, :], lb[:, :], ALU.add).then_inc(vn.h, 1)
                for t in range(NT):
                    dve.wait_ge(mm_.h, mm_.at(t + 1))
                    for g in range(4):
                        q = slice(g * P, (g + 1) * P)
                        ins = dve.scalar_tensor_tensor(OD[:, t, q], bank[t % 2][:, q], DB[:, g:g + 1], OD[:, t, q],
                                                       ALU.add, ALU.mult)
                    ins.then_inc(dd.h, 1)
                dve_chain.end(ch.n)

            @block.tensor
            def _(pe):
                pe.wait_ge(wm.h, wm.at(1))
                for t in range(NT):
                    pe.wait_ge(vn.h, vn.at(t + 1))
                    if t >= 2:
                        pe.wait_ge(dd.h, dd.at(t - 1))
                    for g in range(4):
                        q = slice(g * P, (g + 1) * P)
                        m = pe.matmul(bank[t % 2][:, q], WT[:, g, :], VN[:, t, q], start=True, stop=True)
                    m.then_inc(mm_.h, 1)
        roots.end()
        loaded.end(64), stored.end(16), wm.end(1), vn.end(NT), mm_.end(NT), dd.end(NT)

    s3 = ExitStack()
    QT = sb(s3, "QTc", [P, CH_, PADT])
    KT = sb(s3, "KTc", [P, CKV, KT7 * P])
    VV = sb(s3, "VVc", [P, KT7, CKV, CHD])
    MSK = sb(s3, "MSKc", [P, NT, 512])
    with ExitStack() as s2:
        IQT = sb(s2, "IQT", [P, 8, PADT])
        IKT = sb(s2, "IKT", [P, KT7 * P])
        gn = sb(s2, "gnc", [P, 3, CHD])
        RT = sb(s2, "RTc", [P, NT, 64])
        SQ = sb(s2, "SQc", [P, 10, CHD])
        hs = sb(s2, "hsc", [P, 11])
        RC = sb(s2, "RCc", [P, 10, 2, 32])
        RS = sb(s2, "RSc", [P, 10, 2, 32])
        IW = sb(s2, "IWc", [P, NT, 8])
        LG = sb(s2, "LGc", [P, 2, 512])
        SCO = sb(s2, "SCO", [P, 512])
        WK = sb(s2, "WKc", [P, 512])
        M8 = sb(s2, "M8c", [P, 8])
        roots = Roots(sig)
        kz, ro, tr, ev = sig("keys_zeroed"), sig("rotated"), sig("heads_turned"), sig("heads_copied")
        ix, rl, ac = sig("index_scores"), sig("index_relu"), sig("index_added")
        cols = [h * 64 for h in range(8)] + [768 + h * 64 for h in range(8)] + [512, 576, 1280]
        with nc.Block() as block:
            @block.gpsimd
            def _(pool):
                for buf in (QT, IQT, KT):
                    pool.memset(buf[64:P, :, :], 0.0).then_inc(kz.h, 1)
                pool.memset(IKT[64:P, :], 0.0).then_inc(kz.h, 1)
                pool.wait_ge(kz.h, kz.at(4))
                for t in range(NT):
                    roots.give(pool, 2 * t, hs[:, 0:10])
                    roots.give(pool, 2 * t + 1, hs[:, 10:11])

            @block.sync
            def _(sp):
                kvw = io["cache_c_v"][0].rearrange("(k p) h n -> p k h n", p=P)
                for dst, src in (
                    (gn[:, 0, :], io["c_q_gain"].partition_broadcast(P)),
                    (gn[:, 1, :], io["c_k_gain"].partition_broadcast(P)),
                    (gn[:, 2, :], io["c_kidx_gain"].partition_broadcast(P)),
                    (RT[:, :, :], io["rope_c"]), (MSK[:, :, :], io["mask"]),
                    (KT[0:64, :, 4 * P:6 * P], io["ck_t"]), (IKT[0:64, 4 * P:6 * P], io["kidx_t"]),
                    (VV[:, 4:6, :, :].rearrange("p k h n -> p k (h n)"), kvw.rearrange("p k h n -> p k (h n)")),
                ):
                    sp.dma_start(dst, src).then_inc(loaded.h, 16)
                ns = 0
                for t in range(NT):
                    sp.wait_ge(ro.h, ro.at(t + 1))
                    n = P if t < 4 else DEC
                    for name, a, b in (("c_k", 512, 640), ("c_v", 640, 768), ("c_kidx", 1280, 1344)):
                        o = io[f"out_{name}_{'p' if t < 4 else 's'}"][0]
                        if name != "c_kidx":
                            o = o.rearrange("s h n -> s (h n)")
                        sp.dma_start(o[t % 4 * P:t % 4 * P + n, :], PCm[0:n, t, a:b]).then_inc(stored.h, 16)
                        ns += 1
                sp.wait_ge(stored.h, stored.at(16 * ns))

            @block.vector
            def _(dve):
                ch = Chain(dve, dve_chain)
                dve.wait_ge(loaded.h, loaded.at(128))
                for t in range(NT):
                    qk = PCm[:, t, 0:640].rearrange("p (h n) -> p h n", h=10)
                    ik = PCm[:, t, 1280:1344].unsqueeze(1)
                    rms_heads(dve, ch, roots, qk, SQ[:, :, :], hs[:, 0:10], 10, CHD)
                    rms_heads(dve, ch, roots, ik, SQ[:, 0:1, :], hs[:, 10:11], 1, CHD)
                    for a, n, g in ((0, 8, 0), (8, 2, 1)):
                        y = qk[:, a:a + n, :]
                        ch(dve.tensor_tensor(y, y, gn[:, g, :].unsqueeze(1).broadcast_to([P, n, CHD]), ALU.mult))
                    ch(dve.tensor_tensor(ik[:, 0, :], ik[:, 0, :], gn[:, 2, :], ALU.mult))
                    rotate(dve, ch, qk, RT[:, t, :], RC[:, :, :, :], RS[:, :, :, :], 10, 32, None)
                    ch(dve.tensor_copy(VV[:, t if t < 4 else 6, :, :].rearrange("p h n -> p (h n)"), PCm[:, t, 640:768]))
                    ch(dve.tensor_scalar(IW[:, t, :], PCm[:, t, 1344:1352], float(8 ** -0.5) * 0.125, None, ALU.mult))
                    iqk = PCm[:, t, 768:1344].rearrange("p (h n) -> p h n", h=9)
                    rotate(dve, ch, iqk, RT[:, t, :], RC[:, 0:9, :, :], RS[:, 0:9, :, :], 9, 32, ro)
                for t in range(NT):
                    n = QT_KEYS[t] * P
                    for h in range(8):
                        i = t * 8 + h
                        dve.wait_ge(rl.h, rl.at(i + 1))
                        w = IW[:, t, h:h + 1]
                        prev = MSK[:, t, 0:n] if h == 0 else SCO[:, 0:n]
                        ch(dve.scalar_tensor_tensor(SCO[:, 0:n], LG[:, i % 2, 0:n], w, prev, ALU.mult, ALU.add))
                        dve.engine_nop().then_inc(ac.h, 1)
                    if SEL_KEYS[t]:
                        for r in range(SEL_KEYS[t] // 8):
                            src = SCO if r == 0 else WK
                            ch(dve.max(M8[:, :], src[:, 0:n]))
                            ch(dve.match_replace(WK[:, 0:n], M8[:, :], src[:, 0:n], -3e38))
                        ch(dve.tensor_scalar(WK[:, 0:n], WK[:, 0:n], -1e38, NEG, ALU.is_ge, ALU.mult))
                        ch(dve.tensor_tensor(MSK[:, t, 0:n], MSK[:, t, 0:n], WK[:, 0:n], ALU.min))
                dve_chain.end(ch.n)

            @block.tensor
            def _(pe):
                for t in range(NT):
                    pe.wait_ge(ro.h, ro.at(t + 1))
                    for i, c in enumerate(cols):
                        b, o = i // 4, (i % 4) * P
                        if i % 4 == 0 and t >= 1:
                            pe.wait_ge(ev.h, ev.at(5 * (t - 1) + b + 1))
                        m = pe.transpose(bank[b][0:64, o:o + P], PCm[:, t, c:c + 64], ident)
                        if i % 4 == 3 or i == len(cols) - 1:
                            m.then_inc(tr.h, 1)
                pe.wait_ge(kz.h, kz.at(4))
                pe.wait_ge(loaded.h, loaded.at(128))
                pe.wait_ge(ev.h, ev.at(5 * NT))
                for t in range(NT):
                    n, f = QT_KEYS[t] * P, QT_FIRST[t] * P
                    for h in range(8):
                        i = t * 8 + h
                        if i >= 2:
                            pe.wait_ge(rl.h, rl.at(i - 1))
                        pe.matmul(bank[6 + i % 2][:, 0:n], IQT[:, h, t * P:(t + 1) * P], IKT[:, f:f + n],
                                  start=True, stop=True).then_inc(ix.h, 1)

            @block.scalar
            def _(act):
                for t in range(NT):
                    kt = t if t < 4 else 6
                    s = slice(t * P, (t + 1) * P)
                    kk = slice(kt * P, (kt + 1) * P)
                    v = lambda b, n: bank[b][0:64, 0:n * P].rearrange("p (h n) -> p h n", h=n)
                    for b, dst in enumerate((QT[0:64, 0:4, s], QT[0:64, 4:8, s], IQT[0:64, 0:4, s], IQT[0:64, 4:8, s])):
                        act.wait_ge(tr.h, tr.at(5 * t + b + 1))
                        act.activation(dst, v(b, 4), ACT.Copy).then_inc(ev.h, 1)
                    act.wait_ge(tr.h, tr.at(5 * t + 5))
                    act.activation(KT[0:64, :, kk], v(4, 2), ACT.Copy)
                    act.activation(IKT[0:64, kk], bank[4][0:64, 256:384], ACT.Copy).then_inc(ev.h, 1)
                for t in range(NT):
                    n = QT_KEYS[t] * P
                    for h in range(8):
                        i = t * 8 + h
                        act.wait_ge(ix.h, ix.at(i + 1))
                        if i >= 2:
                            act.wait_ge(ac.h, ac.at(i - 1))
                        act.activation(LG[:, i % 2, 0:n], bank[6 + i % 2][:, 0:n], ACT.Relu).then_inc(rl.h, 1)
        roots.end()
        loaded.end(128), stored.end(16 * 15), kz.end(4), ro.end(NT), tr.end(5 * NT), ev.end(5 * NT)
        ix.end(40), rl.end(40), ac.end(40)
    attention("C", P, QT, lambda a, h, c, n: KT[:, a, c:c + n], lambda a, h, k: VV[:, k, a, :],
              MSK, 0.125, OC)
    s3.close()
    project_out(nc, io["l1_w_out"], sb, sig, bank, ident, OC, None, OD, X, "1")
    st.close()


_OUTS = [
    ("y_p", (1, SEQ, D)), ("y_s", (1, DEC, D)),
    ("a_ckv_p", (1, SEQ, AC)), ("a_krope_p", (1, SEQ, AROPE)), ("b_wkv_p", (P, 4, 64)), ("b_shift_p", (P, BT)),
    ("c_k_p", (1, SEQ, CKV, CHD)), ("c_v_p", (1, SEQ, CKV, CHD)), ("c_kidx_p", (1, SEQ, 64)),
    ("a_ckv_s", (1, DEC, AC)), ("a_krope_s", (1, DEC, AROPE)), ("b_wkv_s", (P, 4, 64)), ("b_shift_s", (P, BT)),
    ("c_k_s", (1, DEC, CKV, CHD)), ("c_v_s", (1, DEC, CKV, CHD)), ("c_kidx_s", (1, DEC, 64)),
    ("d_v_s", (1, DEC, DW)),
]
_AS_THEY_ARE = [
    "x_prompt", "x_sample", "cache_a_krope", "cache_c_v", "l0_norm_mix", "l0_w_in", "a_q_norm", "a_w_uq",
    "a_kv_norm", "a_w_ukv", "a_q_gain", "a_k_gain", "b_w2", "b_a2", "b_g2", "l0_w_out", "l0_norm_ffn",
    "l0_peer_wq", "l1_norm_mix", "l1_w_in", "c_q_gain", "c_k_gain", "c_kidx_gain", "d_ln_g", "d_ln_b",
    "l1_w_out", "l1_norm_ffn", "l1_peer_wq",
]


def _constants():
    i = np.arange(P)
    blk = (i[:, None] // 64) == (i[None, :] // 64)
    b16 = (i[:, None] // 16) == (i[None, :] // 16)
    lt, le = i[:, None] < i[None, :], i[:, None] <= i[None, :]
    scan = np.ones(TOK)
    scan[::CHK] = 0
    cst = np.concatenate([
        np.eye(P), blk, blk & lt, blk & le, b16, ~b16, (i[:, None] % 64) == np.arange(64)[None, :],
        np.broadcast_to(scan, (P, TOK)), b16 & (i[:, None] > i[None, :]), np.full((P, 1), -0.5)], axis=1).astype(np.float32)
    mask = np.zeros((P, NT, 512), np.float32)
    for t in range(4):
        mask[0:64, t, t * P + 64:] = NEG
        mask[:, t, (t + 1) * P:] = NEG
    mask[:, 4, PAST + DEC:] = NEG

    def rope(pos, half):
        f = (np.float32(10000.0) ** (-np.arange(half, dtype=np.float32) / np.float32(half))).astype(np.float32)
        ang = (pos.astype(np.float32)[:, None] * f[None, :]).astype(np.float32)
        t = np.concatenate([np.cos(ang), np.sin(ang)], axis=1).astype(np.float32)
        return np.ascontiguousarray(t.reshape(-1, P, 2 * half).transpose(1, 0, 2))

    own = np.concatenate([np.arange(SEQ), PAST + np.arange(P)])
    keys = np.concatenate([np.arange(SEQ), np.arange(PAST + P)])
    return {"cst": cst, "mask": mask, "rope_a": rope(keys, 16), "rope_c": rope(own, 32)}


def kernel(**inputs):
    import concourse.bacc as _bacc
    from concourse.bass_utils import run_bass_kernel_spmd as _run

    a = {k: np.asarray(v) for k, v in inputs.items()}
    col = lambda v: v.reshape(-1, P).T
    ins = {k: a[k] for k in _AS_THEY_ARE}
    ins |= _constants()
    ins["bvec"] = np.concatenate([col(a[k]) for k in ("b_w0", "b_a0", "b_kk", "b_ka")] + [col(a["b_rk"].reshape(-1))]
                                 + [col(a[k]) for k in ("b_ln_g", "b_ln_b", "b_mu")], axis=1)
    ins["shift_t"] = col(a["state_b_shift"][0])
    ins["wkv_t"] = a["state_b_wkv"][0].transpose(0, 2, 1).reshape(4, P, 64).transpose(1, 0, 2)
    ins["ckv_t"] = a["cache_a_ckv"][0].T
    ins["ck_t"] = a["cache_c_k"][0].transpose(2, 1, 0)
    ins["kidx_t"] = a["cache_c_kidx"][0].T
    ins["dws_t"] = a["d_ws"].transpose(2, 0, 1)
    ins["dbs_t"] = a["d_bs"].T
    for i in range(2):
        ins[f"keys_t{i}"] = a[f"l{i}_peer_keys"].transpose(0, 1, 3, 2)
        ins[f"uv{i}"] = np.concatenate([a[f"l{i}_peer_u"], a[f"l{i}_peer_v"]], axis=1)

    nc = _bacc.Bacc("TRN2", target_bir_lowering=False, num_devices=1)
    arrays, io = {}, {}
    for name, v in ins.items():
        v = np.ascontiguousarray(v)
        arrays[f"in_{name}"] = v
        io[name] = nc.dram_tensor(f"in_{name}", v.shape, mybir.dt.from_np(v.dtype), kind="ExternalInput").ap()
    for name, shape in _OUTS:
        io[f"out_{name}"] = nc.dram_tensor(f"out_{name}", shape, F32, kind="ExternalOutput").ap()
    encoder(nc, io)
    got = _run(nc, [arrays], core_ids=[0]).results[0]
    res = []
    for name, _ in _OUTS:
        v = got[f"out_{name}"]
        if "wkv" in name:
            v = v.reshape(2, 64, 4, 64).transpose(2, 0, 3, 1).reshape(1, BH, BHD, BHD)
        elif "shift" in name:
            v = v.T.reshape(1, BPROJ)
        res.append(np.ascontiguousarray(v))
    return tuple(res)
```

```python
from contextlib import ExitStack

import numpy as np

import concourse.bass as bass
from concourse import mybir

P = 128
F32 = mybir.dt.float32
U32 = mybir.dt.uint32
ALU = mybir.AluOpType
ACT = mybir.ActivationFunctionType
AX = mybir.AxisListType

D = 1024
KD = D // P
SEQ, DEC, PAST = 512, 64, 256
NT = 5
TOK = SEQ + DEC
PADT = NT * P
KT7 = 7
EPS = 1e-6
NEG = -1e30

AH, ANOPE, AROPE, AQK, AV = 8, 64, 32, 96, 64
ACQ, AC = 256, 128
ACOLS = ACQ + AC + AROPE
BH, BHD, BW = 8, 64, 512
BT = 14
BPROJ = BT * P
BLN_EPS = 64e-5
DECAY = float(np.exp(-0.5))
CHK = 64
NCH = TOK // CHK
CH_, CKV, CHD = 8, 2, 64
CCOLS = 1352
DW = 512
NK = 128
PH, PK = 8, 16
NEXP = NK * NK
QT_KEYS = [1, 2, 3, 4, 3]
QT_FIRST = [0, 0, 0, 0, 4]
SEL_KEYS = [0, 128, 128, 128, 80]
RING = 16
SLOTS = 16


class Signal:

    def __init__(self, handle):
        self.h, self.base = handle, 0

    def at(self, n):
        return self.base + n

    def end(self, n):
        self.base += n


class Chain:

    def __init__(self, eng, signal, base=0):
        self.eng, self.s, self.base, self.n = eng, signal, base, 0

    def __call__(self, ins):
        ins.then_inc(self.s.h, 1)
        self.n += 1
        self.eng.wait_ge(self.s.h, self.s.at(self.base + self.n))


class Roots:

    half = None

    def __init__(self, sig):
        self.asked, self.done, self.n = sig("roots_asked"), sig("roots_done"), 0

    def send(self, ins):
        ins.then_inc(self.asked.h, 1)
        self.n += 1

    def get(self, dve):
        dve.wait_ge(self.done.h, self.done.at(self.n))

    def ask(self, dve, ins):
        self.send(ins)
        self.get(dve)

    def give(self, pool, i, ap):
        pool.wait_ge(self.asked.h, self.asked.at(i + 1))
        half = self.half[:, 0:1]
        half = half.broadcast_to(list(ap.shape)) if len(ap.shape) == 2 else half
        pool.tensor_tensor(ap, ap, half, ALU.pow).then_inc(self.done.h, 1)

    def end(self):
        self.asked.end(self.n), self.done.end(self.n)


def encoder(nc, io):
    ctx = ExitStack()
    with ctx:
        def sb(stack, name, shape, dt=F32):
            return stack.enter_context(nc.sbuf_tensor(name, shape, dt))

        names = {}

        def sig(name):
            if name not in names:
                names[name] = Signal(ctx.enter_context(nc.semaphore(name)))
            return names[name]

        pairs = [ctx.enter_context(nc.psum_tensor(f"banks{i}", [P, 1024], F32)) for i in range(4)]
        bank = [pairs[i // 2][:, 512 * (i % 2):512 * (i % 2) + 512] for i in range(8)]

        X = sb(ctx, "X", [P, NT, D])
        IDN = sb(ctx, "IDN", [P, 130])
        ident = IDN[:, 0:128]
        Roots.half = IDN[:, 128:129]
        lo = ExitStack()
        CST = sb(lo, "CST", [P, 1408])

        dve_chain = sig("dve_chain")
        act_chain = sig("act_chain")
        loaded = sig("loaded")
        stored = sig("stored")

        def load_x(eng):
            for t in range(4):
                eng.dma_start(X[:, t, :], io["x_prompt"][0, t * P:(t + 1) * P, :]).then_inc(loaded.h, 16)
            eng.dma_start(X[0:DEC, 4, :], io["x_sample"][0]).then_inc(loaded.h, 16)

        def norm(stack, tag, gain, src_load, XN, XT, more_loads=None, zero_rows=False, place=None):
            with ExitStack() as st:
                gB = place(D) if place else sb(st, f"gB{tag}", [P, D])
                junk = place(D) if place else sb(st, f"junk{tag}", [P, D])
                ss = sb(st, f"ss{tag}", [P, 8])
                xz, sq, xn, tr, ev = (sig(n) for n in ("x_zeroed", "squares", "normed", "transposed", "evacuated"))
                nload = [0]
                roots = Roots(sig)
                with nc.Block() as block:
                    @block.sync
                    def _(sp):
                        sp.dma_start(gB[:, 0:D], gain.partition_broadcast(P)).then_inc(loaded.h, 16)
                        nload[0] += 1
                        if src_load:
                            load_x(sp)
                            nload[0] += 5
                            sp.dma_start(CST[:, :], io["cst"]).then_inc(loaded.h, 16)
                            sp.dma_start(IDN[:, :], io["idn"]).then_inc(loaded.h, 16)
                            nload[0] += 2
                        if more_loads:
                            more_loads(sp)

                    @block.scalar
                    def _(act):
                        act.wait_ge(loaded.h, loaded.at(16 * nload[0]))
                        if src_load or zero_rows:
                            act.wait_ge(xz.h, xz.at(1))
                        for t in range(NT):
                            act.activation(junk[:, :], X[:, t, :], ACT.Square,
                                           accum_out=ss[:, t:t + 1]).then_inc(sq.h, 1)
                            act.wait_ge(sq.h, sq.base + t + 1)
                        for t in range(NT):
                            for b in range(2):
                                act.wait_ge(tr.h, tr.at(2 * t + b + 1))
                                act.activation(XT[:, 4 * b:4 * b + 4, t * P:(t + 1) * P],
                                               bank[(2 * t + b) % 4][:, :].rearrange("p (k n) -> p k n", k=4),
                                               ACT.Copy).then_inc(ev.h, 1)

                    @block.vector
                    def _(dve):
                        if src_load or zero_rows:
                            dve.memset(X[DEC:P, 4, :], 0.0).then_inc(xz.h, 1)
                        dve.wait_ge(loaded.h, loaded.at(16 * nload[0]))
                        dve.wait_ge(sq.h, sq.at(NT))
                        roots.ask(dve, dve.tensor_scalar(ss[:, 0:NT], ss[:, 0:NT], 1.0 / D, EPS, ALU.mult, ALU.add))
                        for t in range(NT):
                            dve.scalar_tensor_tensor(XN[:, t, :], X[:, t, :], ss[:, t:t + 1], gB[:, :],
                                                     ALU.mult, ALU.mult).then_inc(xn.h, 1)

                    @block.gpsimd
                    def _(pool):
                        roots.give(pool, 0, ss[:, 0:NT])

                    @block.tensor
                    def _(pe):
                        for t in range(NT):
                            pe.wait_ge(xn.h, xn.at(t + 1))
                            for b in range(2):
                                if t >= 2:
                                    pe.wait_ge(ev.h, ev.at(2 * (t - 2) + b + 1))
                                for k in range(4):
                                    mm = pe.transpose(bank[(2 * t + b) % 4][:, k * P:(k + 1) * P],
                                                      XN[:, t, (4 * b + k) * P:(4 * b + k + 1) * P], ident)
                                mm.then_inc(tr.h, 1)
                loaded.end(16 * nload[0])
                if src_load or zero_rows:
                    xz.end(1)
                roots.end()
                sq.end(NT), xn.end(NT), tr.end(2 * NT), ev.end(2 * NT)

        def attention(tag, rows, QT, key_of, V_of, SEL, scale, OUT):
            with ExitStack() as st:
                S = sb(st, f"S{tag}", [P, 3, 512])
                E = sb(st, f"E{tag}", [P, 3, 512])
                ET = sb(st, f"ET{tag}", [P, 2, 512])
                nmx = sb(st, f"nmx{tag}", [P, 3, 1])
                den = sb(st, f"den{tag}", [P, 3, 1])
                rden = sb(st, f"rden{tag}", [P, 2, 1])
                sc, so, mx, ex, tr, pt, rd, pv, fi = (sig(n) for n in (
                    "scores", "masked", "maxima", "exped", "probs_turned", "probs_copied", "sums_inverted",
                    "weighted", "heads_out"))
                every = (sc, so, mx, ex, tr, pt, rd, pv, fi)
                units = [(h, j) for h in range(AH) for j in range(NT)]
                N = len(units)
                with nc.Block() as block:
                    @block.tensor
                    def _(pe):
                        def scores(u):
                            h, j = units[u]
                            if u >= 3:
                                pe.wait_ge(so.h, so.at(u - 2))
                            n = QT_KEYS[j] * P
                            pe.matmul(bank[u % 3][:, 0:n], QT[0:rows, h, j * P:(j + 1) * P],
                                      key_of(h // 4, h, QT_FIRST[j] * P, n), start=True, stop=True).then_inc(sc.h, 1)

                        def turn(u):
                            h, j = units[u]
                            pe.wait_ge(ex.h, ex.at(u + 1))
                            if u >= 2:
                                pe.wait_ge(pt.h, pt.at(u - 1))
                            for k in range(QT_KEYS[j]):
                                mm = pe.transpose(bank[3 + u % 2][:, k * P:(k + 1) * P],
                                                  E[:, u % 3, k * P:(k + 1) * P], ident)
                            mm.then_inc(tr.h, 1)

                        def weigh(u):
                            h, j = units[u]
                            pe.wait_ge(pt.h, pt.at(u + 1))
                            if u >= 2:
                                pe.wait_ge(fi.h, fi.at(u - 1))
                            for k in range(QT_KEYS[j]):
                                mm = pe.matmul(bank[5 + u % 2][:, 0:64], ET[:, u % 2, k * P:(k + 1) * P],
                                               V_of(h // 4, h, QT_FIRST[j] + k),
                                               start=(k == 0), stop=(k == QT_KEYS[j] - 1))
                            mm.then_inc(pv.h, 1)

                        scores(0)
                        scores(1)
                        for u in range(N):
                            if u + 2 < N:
                                scores(u + 2)
                            turn(u)
                            if u >= 1:
                                weigh(u - 1)
                        weigh(N - 1)

                    @block.vector
                    def _(dve):
                        def soft(u):
                            h, j = units[u]
                            n, s = QT_KEYS[j] * P, u % 3
                            dve.wait_ge(sc.h, sc.at(u + 1))
                            if u >= 3:
                                dve.wait_ge(ex.h, ex.at(u - 2))
                            dve.scalar_tensor_tensor(S[:, s, 0:n], bank[u % 3][:, 0:n], scale, SEL[:, j, 0:n],
                                                     ALU.mult, ALU.add).then_inc(so.h, 1)
                            dve.wait_ge(so.h, so.at(u + 1))
                            dve.tensor_reduce(nmx[:, s, :], S[:, s, 0:n], AX.X, ALU.max, negate=True).then_inc(mx.h, 1)

                        def finish(u):
                            h, j = units[u]
                            dve.wait_ge(ex.h, ex.at(u + 1))
                            dve.reciprocal(rden[:, u % 2, :], den[:, u % 3, :]).then_inc(rd.h, 1)
                            dve.wait_ge(rd.h, rd.at(u + 1))
                            dve.wait_ge(pv.h, pv.at(u + 1))
                            dve.tensor_scalar(OUT[:, j, h * 64:h * 64 + 64], bank[5 + u % 2][:, 0:64],
                                              rden[:, u % 2, :], None, ALU.mult).then_inc(fi.h, 1)

                        soft(0)
                        soft(1)
                        for u in range(N):
                            if u + 2 < N:
                                soft(u + 2)
                            if u >= 1:
                                finish(u - 1)
                        finish(N - 1)

                    @block.scalar
                    def _(act):
                        def expo(u):
                            h, j = units[u]
                            n, s = QT_KEYS[j] * P, u % 3
                            act.wait_ge(mx.h, mx.at(u + 1))
                            if u >= 3:
                                act.wait_ge(tr.h, tr.at(u - 2))
                                act.wait_ge(rd.h, rd.at(u - 2))
                            act.activation(E[:, s, 0:n], S[:, s, 0:n], ACT.Exp, bias=nmx[:, s, :],
                                           accum_out=den[:, s, :]).then_inc(ex.h, 1)

                        def copy(u):
                            h, j = units[u]
                            n = QT_KEYS[j] * P
                            act.wait_ge(tr.h, tr.at(u + 1))
                            if u >= 2:
                                act.wait_ge(pv.h, pv.at(u - 1))
                            act.activation(ET[:, u % 2, 0:n], bank[3 + u % 2][:, 0:n], ACT.Copy).then_inc(pt.h, 1)

                        expo(0)
                        for u in range(N):
                            if u + 1 < N:
                                expo(u + 1)
                            copy(u)
                for s in every:
                    s.end(N)

        OC = sb(lo, "OC", [P, NT, 512])
        OBT = sb(lo, "OBT", [P, 4, PADT])

        l0 = ExitStack()
        PA = sb(l0, "PA", [P, NT, ACOLS])
        PB = sb(l0, "PB", [P, BT, 2 + TOK])
        SH = sb(l0, "SH", [P, 3, BT])
        w_loaded = [sig(f"weights_loaded{i}") for i in range(4)]

        with ExitStack() as st:
            XT = sb(st, "XT", [P, KD, PADT])
            W = sb(st, "W0", [P, KD, ACOLS + BPROJ])
            wv = io["l0_w_in"].rearrange("(k p) n -> p k n", p=P)
            CW = [(0, ACOLS), (ACOLS, ACOLS + 640), (ACOLS + 640, ACOLS + 1280), (ACOLS + 1280, ACOLS + BPROJ)]

            def load_w(sp):
                for i, (a, b) in enumerate(CW):
                    sp.dma_start(W[:, :, a:b], wv[:, :, a:b]).then_inc(w_loaded[i].h, 16)

            norm(st, "a", io["l0_norm_mix"], True, X, XT, load_w)
            mm_, ev = sig("products"), sig("evacuated")
            border = sig("borders")
            with nc.Block() as block:
                @block.sync
                def _(sp):
                    sp.dma_start(SH[:, 0, :], io["shift_t"]).then_inc(border.h, 16)

                @block.tensor
                def _(pe):
                    n = 0
                    pe.wait_ge(w_loaded[0].h, w_loaded[0].at(16))
                    for t in range(NT):
                        if n >= 4:
                            pe.wait_ge(ev.h, ev.at(n - 3))
                        for k in range(KD):
                            m = pe.matmul(bank[n % 4][:, 0:ACOLS], XT[:, k, t * P:(t + 1) * P], W[:, k, 0:ACOLS],
                                          start=(k == 0), stop=(k == KD - 1))
                        m.then_inc(mm_.h, 1)
                        n += 1
                    for f in range(BT):
                        if f % 5 == 0:
                            pe.wait_ge(w_loaded[1 + f // 5].h, w_loaded[1 + f // 5].at(16))
                        for a, b in ((0, SEQ), (SEQ, TOK)):
                            if n >= 4:
                                pe.wait_ge(ev.h, ev.at(n - 3))
                            for k in range(KD):
                                m = pe.matmul(bank[n % 4][:, 0:b - a],
                                              W[:, k, ACOLS + f * P:ACOLS + (f + 1) * P], XT[:, k, a:b],
                                              start=(k == 0), stop=(k == KD - 1))
                            m.then_inc(mm_.h, 1)
                            n += 1

                @block.scalar
                def _(act):
                    n = 0
                    for t in range(NT):
                        act.wait_ge(mm_.h, mm_.at(n + 1))
                        act.activation(PA[:, t, :], bank[n % 4][:, 0:ACOLS], ACT.Copy).then_inc(ev.h, 1)
                        n += 1
                    for f in range(BT):
                        for a, b, o in ((0, SEQ, 1), (SEQ, TOK, 2)):
                            act.wait_ge(mm_.h, mm_.at(n + 1))
                            act.activation(PB[:, f, a + o:b + o], bank[n % 4][:, 0:b - a], ACT.Copy).then_inc(ev.h, 1)
                            n += 1

                @block.vector
                def _(dve):
                    dve.memset(PB[:, :, 0:1], 0.0)
                    dve.wait_ge(border.h, border.at(16))
                    dve.tensor_copy(PB[:, :, 1 + SEQ], SH[:, 0, :])
                    dve.wait_ge(ev.h, ev.at(NT + 2 * BT))
                    dve.tensor_copy(SH[:, 1, :], PB[:, :, SEQ])
                    dve.tensor_copy(SH[:, 2, :], PB[:, :, TOK + 1])
            for s in w_loaded:
                s.end(16)
            mm_.end(NT + 2 * BT), ev.end(NT + 2 * BT), border.end(16)

        mla(nc, io, sb, sig, bank, ident, PA, OC, attention)
        rwkv(nc, io, sb, sig, bank, CST, IDN, PA, PB, OBT, X)
        with nc.Block() as block:
            @block.sync
            def _(sp):
                load_x(sp)
                sp.wait_ge(loaded.h, loaded.at(80))
                sp.dma_start(io["out_b_shift_p"], SH[:, 1, :]).then_inc(stored.h, 16)
                sp.dma_start(io["out_b_shift_s"], SH[:, 2, :]).then_inc(stored.h, 16)
                sp.wait_ge(stored.h, stored.at(32))

            @block.vector
            def _(dve):
                dve.memset(X[DEC:P, 4, :], 0.0)
                dve.memset(OBT[:, :, TOK:PADT], 0.0)
        loaded.end(80), stored.end(32)
        l0.close()
        project_out(nc, io["l0_w_out"], sb, sig, bank, ident, OC, OBT, None, X, "0")
        lo.close()
        peer(nc, io, 0, sb, sig, bank, pairs[3], ident, X, norm)
        layer1(nc, io, sb, sig, bank, ident, X, norm, attention)
        peer(nc, io, 1, sb, sig, bank, pairs[3], ident, X, norm)
        with nc.Block() as block:
            @block.sync
            def _(sp):
                for t in range(4):
                    sp.dma_start(io["out_y_p"][0, t * P:(t + 1) * P, :], X[:, t, :]).then_inc(stored.h, 16)
                sp.dma_start(io["out_y_s"][0], X[0:DEC, 4, :]).then_inc(stored.h, 16)
                sp.wait_ge(stored.h, stored.at(80))
        stored.end(80)


def mla(nc, io, sb, sig, bank, ident, PA, OC, attention):
    st = ExitStack()
    QT = sb(st, "QT", [P, AH, PADT])
    KT = sb(st, "KT", [P, AH, KT7 * P])
    V = sb(st, "V", [P, KT7, AH, AV])
    MSK = sb(st, "MSK", [P, NT, 512])
    loaded, stored, dve_chain = sig("loaded"), sig("stored"), sig("dve_chain")
    with ExitStack() as s2:
        gq = sb(s2, "gq", [P, ACQ])
        gc = sb(s2, "gc", [P, AC])
        gains = sb(s2, "gains", [P, 2, AQK])
        wuq = sb(s2, "wuq", [P, 2, AH * AQK])
        wukv = sb(s2, "wukv", [P, AH * (ANOPE + AV)])
        CQT = sb(s2, "CQT", [P, 2, PADT])
        LT = sb(s2, "LT", [P, KT7 * P])
        KRC = sb(s2, "KRC", [P, 2, AROPE])
        RT = sb(s2, "RT", [P, KT7, 32])
        CN = sb(s2, "CN", [P, NT, ACQ + AC])
        ss = sb(s2, "ssA", [P, 2, NT])
        junk = sb(s2, "junkA", [P, ACQ])
        Y = sb(s2, "Y", [P, 2, AH, AQK])
        SQ = sb(s2, "SQ", [P, AH, AQK])
        hs = sb(s2, "hs", [P, AH])
        RC = sb(s2, "RC", [P, AH, 2, 16])
        RS = sb(s2, "RS", [P, AH, 2, 16])
        sq, cn, tr, ev = sig("squares"), sig("normed"), sig("transposed"), sig("evacuated")
        up, cp, kr, ro, t2, e2 = (sig(n) for n in (
            "lifted", "lifted_copied", "krope_copied", "rotated", "heads_turned", "heads_copied"))
        NL = 10
        units = [("q", t, [0, 1, 2, 3, 6][t]) for t in range(NT)] + [("k", k, k) for k in range(KT7)]
        NU = len(units)
        roots = Roots(sig)
        with nc.Block() as block:
            @block.sync
            def _(sp):
                for dst, src in (
                    (gq[:, :], io["a_q_norm"].partition_broadcast(P)),
                    (gc[:, :], io["a_kv_norm"].partition_broadcast(P)),
                    (gains[:, 0, :], io["a_q_gain"].partition_broadcast(P)),
                    (gains[:, 1, :], io["a_k_gain"].partition_broadcast(P)),
                    (wuq[:, :, :], io["a_w_uq"].rearrange("(k p) n -> p k n", p=P)),
                    (wukv[:, :], io["a_w_ukv"]),
                    (LT[:, 4 * P:6 * P], io["ckv_t"]),
                    (KRC[:, :, :], io["cache_a_krope"][0].rearrange("(k p) n -> p k n", p=P)),
                    (RT[:, :, :], io["rope_a"]),
                    (MSK[:, :, :], io["mask"]),
                ):
                    sp.dma_start(dst, src).then_inc(loaded.h, 16)
                sp.wait_ge(cn.h, cn.at(2 * NT))
                for t in range(4):
                    sp.dma_start(io["out_a_ckv_p"][0, t * P:(t + 1) * P, :], CN[:, t, ACQ:]).then_inc(stored.h, 16)
                    sp.dma_start(io["out_a_krope_p"][0, t * P:(t + 1) * P, :], PA[:, t, ACQ + AC:]).then_inc(stored.h, 16)
                sp.dma_start(io["out_a_ckv_s"][0], CN[0:DEC, 4, ACQ:]).then_inc(stored.h, 16)
                sp.dma_start(io["out_a_krope_s"][0], PA[0:DEC, 4, ACQ + AC:]).then_inc(stored.h, 16)
                sp.wait_ge(stored.h, stored.at(160))

            @block.scalar
            def _(act):
                for t in range(NT):
                    act.activation(junk[:, :], PA[:, t, 0:ACQ], ACT.Square, accum_out=ss[:, 0, t:t + 1]).then_inc(sq.h, 1)
                    act.wait_ge(sq.h, sq.base + 2 * t + 1)
                    act.activation(junk[:, 0:AC], PA[:, t, ACQ:ACQ + AC], ACT.Square,
                                   accum_out=ss[:, 1, t:t + 1]).then_inc(sq.h, 1)
                    act.wait_ge(sq.h, sq.base + 2 * t + 2)
                for t in range(NT):
                    act.wait_ge(tr.h, tr.at(t + 1))
                    b = bank[t % 2]
                    act.activation(CQT[:, :, t * P:(t + 1) * P], b[:, 0:256].rearrange("p (k n) -> p k n", k=2),
                                   ACT.Copy).then_inc(ev.h, 1)
                    kt = t if t < 4 else 6
                    act.activation(LT[:, kt * P:(kt + 1) * P], b[:, 256:384], ACT.Copy).then_inc(ev.h, 1)

                def take(u):
                    kind, t, kt = units[u]
                    act.wait_ge(up.h, up.at(u + 1))
                    if u >= 2:
                        act.wait_ge(t2.h, t2.at(u - 1))
                    for b in range(2):
                        src = bank[2 * (u % 2) + b]
                        y = Y[:, u % 2, 4 * b:4 * b + 4, :]
                        if kind == "q":
                            ins = act.activation(y, src[:, 0:384].rearrange("p (h n) -> p h n", h=4), ACT.Copy)
                        else:
                            s4 = src[:, :].rearrange("p (h n) -> p h n", h=4)
                            act.activation(y[:, :, 0:ANOPE], s4[:, :, 0:ANOPE], ACT.Copy)
                            ins = act.activation(V[:, t, 4 * b:4 * b + 4, :], s4[:, :, ANOPE:], ACT.Copy)
                    ins.then_inc(cp.h, 1)

                def give(u):
                    kind, t, kt = units[u]
                    act.wait_ge(t2.h, t2.at(u + 1))
                    dst = QT if kind == "q" else KT
                    for b in range(2):
                        act.activation(dst[0:AQK, 4 * b:4 * b + 4, t * P:(t + 1) * P],
                                       bank[4 + 2 * (u % 2) + b][0:AQK, :].rearrange("p (h n) -> p h n", h=4),
                                       ACT.Copy).then_inc(e2.h, 1)

                act.wait_ge(loaded.h, loaded.at(16 * NL))
                take(0)
                for u in range(NU):
                    if u + 1 < NU:
                        take(u + 1)
                    give(u)

            @block.vector
            def _(dve):
                ch = Chain(dve, dve_chain)
                dve.wait_ge(loaded.h, loaded.at(16 * NL))
                dve.wait_ge(sq.h, sq.at(2 * NT))
                for i, w in ((0, ACQ), (1, AC)):
                    roots.ask(dve, dve.tensor_scalar(ss[:, i, :], ss[:, i, :], 1.0 / w, EPS, ALU.mult, ALU.add))
                for t in range(NT):
                    dve.scalar_tensor_tensor(CN[:, t, 0:ACQ], PA[:, t, 0:ACQ], ss[:, 0, t:t + 1], gq[:, :],
                                             ALU.mult, ALU.mult).then_inc(cn.h, 1)
                    dve.scalar_tensor_tensor(CN[:, t, ACQ:], PA[:, t, ACQ:ACQ + AC], ss[:, 1, t:t + 1], gc[:, :],
                                             ALU.mult, ALU.mult).then_inc(cn.h, 1)
                for u, (kind, t, kt) in enumerate(units):
                    y = Y[:, u % 2, :, :]
                    if kind == "k":
                        if u >= 2:
                            dve.wait_ge(t2.h, t2.at(u - 1))
                        src = PA[:, t, ACQ + AC:] if t < 4 else PA[:, 4, ACQ + AC:] if t == 6 else KRC[:, t - 4, :]
                        ch(dve.tensor_copy(y[:, :, ANOPE:], src.unsqueeze(1).broadcast_to([P, AH, AROPE])))
                    dve.wait_ge(cp.h, cp.at(u + 1))
                    rms_heads(dve, ch, roots, y, SQ[:, :, :], hs[:, :], AH, AQK)
                    ch(dve.tensor_tensor(y, y, gains[:, int(kind == "k"), :].unsqueeze(1).broadcast_to([P, AH, AQK]), ALU.mult))
                    rotate(dve, ch, y[:, :, ANOPE:], RT[:, kt, :], RC[:, :, :, :], RS[:, :, :, :], AH, 16, ro)
                dve_chain.end(ch.n)

            @block.gpsimd
            def _(pool):
                for i in range(2):
                    roots.give(pool, i, ss[:, i, :])
                for u in range(NU):
                    roots.give(pool, 2 + u, hs[:, :])

            @block.tensor
            def _(pe):
                for t in range(NT):
                    pe.wait_ge(cn.h, cn.at(2 * t + 2))
                    if t >= 2:
                        pe.wait_ge(ev.h, ev.at(2 * t - 2))
                    for k in range(3):
                        m = pe.transpose(bank[t % 2][:, k * P:(k + 1) * P], CN[:, t, k * P:(k + 1) * P], ident)
                    m.then_inc(tr.h, 1)

                def lift(u):
                    kind, t, kt = units[u]
                    if u >= 2:
                        pe.wait_ge(cp.h, cp.at(u - 1))
                    for b in range(2):
                        dst = bank[2 * (u % 2) + b]
                        if kind == "q":
                            for k in range(2):
                                m = pe.matmul(dst[:, 0:384], CQT[:, k, t * P:(t + 1) * P],
                                              wuq[:, k, b * 384:(b + 1) * 384], start=(k == 0), stop=(k == 1))
                        else:
                            m = pe.matmul(dst[:, :], LT[:, t * P:(t + 1) * P], wukv[:, b * 512:(b + 1) * 512],
                                          start=True, stop=True)
                    m.then_inc(up.h, 1)

                pe.wait_ge(ev.h, ev.at(2 * NT))
                pe.wait_ge(loaded.h, loaded.at(16 * NL))
                lift(0)
                for u in range(NU):
                    if u + 1 < NU:
                        lift(u + 1)
                    pe.wait_ge(ro.h, ro.at(u + 1))
                    if u >= 2:
                        pe.wait_ge(e2.h, e2.at(2 * (u - 1)))
                    for h in range(AH):
                        m = pe.transpose(bank[4 + 2 * (u % 2) + h // 4][0:AQK, (h % 4) * P:(h % 4 + 1) * P],
                                         Y[:, u % 2, h, :], ident)
                    m.then_inc(t2.h, 1)
        loaded.end(16 * NL), stored.end(160), sq.end(2 * NT), cn.end(2 * NT), tr.end(NT), ev.end(2 * NT)
        roots.end()
        up.end(NU), cp.end(NU), ro.end(NU), t2.end(NU), e2.end(2 * NU)
    attention("A", AQK, QT, lambda a, h, c, n: KT[0:AQK, h, c:c + n], lambda a, h, k: V[:, k, h, :],
              MSK, float(AQK) ** -0.5, OC)
    st.close()


def rms_heads(dve, ch, roots, y, sq, hs, heads, width):
    ch(dve.tensor_tensor(sq, y, y, ALU.mult))
    ch(dve.tensor_reduce(hs, sq, AX.X, ALU.add))
    roots.ask(dve, dve.tensor_scalar(hs, hs, 1.0 / width, EPS, ALU.mult, ALU.add))
    ch(dve.tensor_tensor(y, y, hs.unsqueeze(2).broadcast_to([P, heads, width]), ALU.mult))


def rotate(dve, ch, y, cs, rc, rs, heads, half, done):
    y4 = y.rearrange("p h (a n) -> p h a n", a=2)
    cos = cs[:, 0:half].unsqueeze(1)
    sin = cs[:, half:2 * half].unsqueeze(1)
    for a in range(2):
        ch(dve.tensor_tensor(rc[:, :, a, :], y4[:, :, a, :], cos.broadcast_to([P, heads, half]), ALU.mult))
        ch(dve.tensor_tensor(rs[:, :, a, :], y4[:, :, 1 - a, :], sin.broadcast_to([P, heads, half]), ALU.mult))
    ch(dve.tensor_tensor(y4[:, :, 0, :], rc[:, :, 0, :], rs[:, :, 0, :], ALU.subtract))
    ins = dve.tensor_tensor(y4[:, :, 1, :], rc[:, :, 1, :], rs[:, :, 1, :], ALU.add)
    if done is None:
        ch(ins)
    else:
        ins.then_inc(done.h, 1)


def project_out(nc, w_dram, sb, sig, bank, ident, OC, OBT, OD, X, tag):
    loaded, tr, ev, mm_, ad = (sig(n) for n in ("loaded", "transposed", "evacuated", "products", "added"))
    with ExitStack() as st:
        W = sb(st, f"WO{tag}", [P, KD, D])
        OT = sb(st, f"OT{tag}", [P, 2, KD, P])
        nb = 1 if OD is None else 2
        with nc.Block() as block:
            @block.sync
            def _(sp):
                wv = w_dram.rearrange("(k p) n -> p k n", p=P)
                for i in range(2):
                    sp.dma_start(W[:, 4 * i:4 * i + 4, :], wv[:, 4 * i:4 * i + 4, :]).then_inc(loaded.h, 16)

            @block.tensor
            def _(pe):
                def turn(t):
                    if t >= 1:
                        pe.wait_ge(ev.h, ev.at(nb * t))
                    for b in range(nb):
                        src = (OC, OD)[b]
                        for k in range(4):
                            m = pe.transpose(bank[b][:, k * P:(k + 1) * P], src[:, t, k * P:(k + 1) * P], ident)
                        m.then_inc(tr.h, 1)

                def product(t):
                    pe.wait_ge(ev.h, ev.at(nb * (t + 1)))
                    if t >= 2:
                        pe.wait_ge(ad.h, ad.at(2 * (t - 1)))
                    for b in range(2):
                        for k in range(KD):
                            lhs = OT[:, t % 2, k, :] if k < 4 or OBT is None else OBT[:, k - 4, t * P:(t + 1) * P]
                            m = pe.matmul(bank[2 + 2 * (t % 2) + b][:, :], lhs, W[:, k, b * 512:(b + 1) * 512],
                                          start=(k == 0), stop=(k == KD - 1))
                        m.then_inc(mm_.h, 1)

                turn(0)
                pe.wait_ge(loaded.h, loaded.at(32))
                for t in range(NT):
                    if t + 1 < NT:
                        turn(t + 1)
                    product(t)

            @block.scalar
            def _(act):
                for t in range(NT):
                    for b in range(nb):
                        act.wait_ge(tr.h, tr.at(nb * t + b + 1))
                        if t >= 2:
                            act.wait_ge(mm_.h, mm_.at(2 * (t - 1)))
                        act.activation(OT[:, t % 2, 4 * b:4 * b + 4, :],
                                       bank[b][:, :].rearrange("p (k n) -> p k n", k=4), ACT.Copy).then_inc(ev.h, 1)

            @block.vector
            def _(dve):
                for t in range(NT):
                    for b in range(2):
                        dve.wait_ge(mm_.h, mm_.at(2 * t + b + 1))
                        x = X[:, t, b * 512:(b + 1) * 512]
                        dve.tensor_tensor(x, bank[2 + 2 * (t % 2) + b][:, :], x, ALU.add).then_inc(ad.h, 1)
        loaded.end(32), tr.end(nb * NT), ev.end(nb * NT), mm_.end(2 * NT), ad.end(2 * NT)


V_W0, V_A0, V_KK, V_KA, V_RK, V_LG, V_LB, V_MU = 0, 4, 8, 12, 16, 20, 24, 28


def rwkv(nc, io, sb, sig, bank, CST, IDN, PA, PB, OBT, X):
    ident, eps = IDN[:, 0:128], IDN[:, 129:130]
    onesbd, maskSI, mask16, maskO, mask16L = (
        CST[:, 0:128], CST[:, 128:384], CST[:, 384:512], CST[:, 512:640], CST[:, 640:768])
    stackI = CST[:, 768:832]
    scanm = CST[:, 832:1408]
    loaded, stored, dve_chain, act_chain = sig("loaded"), sig("stored"), sig("dve_chain"), sig("act_chain")
    st = ExitStack()
    AR = sb(st, "AR", [P, NCH, 4, 2, P])
    BB = sb(st, "BB", [P, NCH, 4, P])
    KB = sb(st, "KB", [P, NCH, 4, P])
    VC = sb(st, "VC", [P, NCH, 4, 64])
    PC = sb(st, "PCe", [P, NCH, 4])
    XV = X[:, :, :].rearrange("p t d -> p (t d)").rearrange("p (s n) -> p s n", s=8)
    G = XV[:, 0:4, :]
    with ExitStack() as s2:
        XS = sb(s2, "XS", [P, 5, TOK])
        W2A = sb(s2, "W2A", [P, 2, BW])
        G2 = sb(s2, "G2", [P, BW])
        BV = sb(s2, "BV", [P, V_MU + BT])
        oka = sb(s2, "oka", [P, 4])
        T4 = sb(s2, "T4", [P, TOK])
        T5 = sb(s2, "T5", [P, TOK])
        VB = sb(s2, "VB", [P, NCH, P])
        T0, T1, T2, T3 = (XV[:, 4 + i, 0:TOK] for i in range(4))
        R, K, V, LW, LG = (XS[:, i, :] for i in range(5))
        sh, tn, za, zg, zc, d1, e1, d2, sp1, d3, d4, sp2, d5, vb, vm, vcp = (sig(n) for n in (
            "shifted", "lora_in", "lora_out", "gates_taken", "zeroed", "summed", "exps", "kk_squared", "kk_sums",
            "kk_done", "bonus_in", "bonus_sums", "bonus_done", "v_blocks", "v_turned", "v_copied"))
        rt = sig("kk_norms")
        with nc.Block() as block:
            @block.sync
            def _(sp):
                sp.wait_ge(zc.h, zc.at(1))
                for dst, src in ((W2A[0:64, 0, :], io["b_w2"]), (W2A[64:P, 1, :], io["b_a2"]), (G2[:, :], io["b_g2"]),
                                 (BV[:, :], io["bvec"])):
                    sp.dma_start(dst, src).then_inc(loaded.h, 16)
                sp.wait_ge(loaded.h, loaded.at(64))

            @block.gpsimd
            def _(pool):
                pool.memset(W2A[:, :, :], 0.0).then_inc(zc.h, 1)
                pool.memset(AR[:, :, :, :, :], 0.0).then_inc(zc.h, 1)
                pool.memset(BB[:, :, :, :], 0.0).then_inc(zc.h, 1)
                pool.memset(KB[:, :, :, :], 0.0).then_inc(zc.h, 1)
                pool.memset(VB[:, :, :], 0.0).then_inc(zc.h, 1)

            @block.vector
            def _(dve):
                ch = Chain(dve, dve_chain)

                def shift(slot, ft):
                    x = XS[:, slot, :]
                    ch(dve.tensor_tensor(x[:, 0:SEQ], PB[:, ft, 0:SEQ], PB[:, ft, 1:SEQ + 1], ALU.subtract))
                    ch(dve.tensor_tensor(x[:, SEQ:], PB[:, ft, SEQ + 1:TOK + 1], PB[:, ft, SEQ + 2:], ALU.subtract))
                    mu = BV[:, V_MU + ft:V_MU + ft + 1]
                    ch(dve.scalar_tensor_tensor(x[:, 0:SEQ], x[:, 0:SEQ], mu, PB[:, ft, 1:SEQ + 1], ALU.mult, ALU.add))
                    ch(dve.scalar_tensor_tensor(x[:, SEQ:], x[:, SEQ:], mu, PB[:, ft, SEQ + 2:], ALU.mult, ALU.add))

                def blocks(dst, in0, in1, scalar=None):
                    for h in range(2):
                        q = slice(64 * h, 64 * h + 64)
                        o = dst[q, :, 64 * h:64 * h + 64]
                        a = in0[q, :].rearrange("p (c n) -> p c n", c=NCH)
                        b = in1[q, :].rearrange("p (c n) -> p c n", c=NCH)
                        if scalar is None:
                            ch(dve.tensor_tensor(o, a, b, ALU.mult))
                        else:
                            ch(dve.scalar_tensor_tensor(o, a, scalar, b, ALU.mult, ALU.mult))

                dve.wait_ge(loaded.h, loaded.at(64))
                dve.wait_ge(zc.h, zc.at(5))
                shift(3, 12)
                shift(4, 13)
                ch(dve.tensor_scalar(oka[:, :], BV[:, V_KA:V_KA + 4], -1.0, 1.0, ALU.mult, ALU.add))
                dve.engine_nop().then_inc(sh.h, 1)
                for p in range(4):
                    shift(0, p)
                    shift(1, 4 + p)
                    shift(2, 8 + p)
                    dve.wait_ge(zg.h, zg.at(3 * p + 2))
                    ch(dve.tensor_tensor_scan(T1, scanm, T0, 0.0, ALU.mult, ALU.add))
                    dve.tensor_tensor(T2, T1, T0, ALU.subtract).then_inc(d1.h, 1)
                    dve.wait_ge(e1.h, e1.at(3 * p + 3))
                    ch(dve.tensor_scalar(T1, K, BV[:, V_KK + p:V_KK + p + 1], None, ALU.mult))
                    dve.tensor_tensor(T2, T1, T1, ALU.mult).then_inc(d2.h, 1)
                    dve.wait_ge(rt.h, rt.at(p + 1))
                    ch(dve.reciprocal(T2, T2))
                    ch(dve.tensor_tensor(T1, T1, T2, ALU.mult))
                    blocks(AR[:, :, p, 0, :], T1, T0, -1.0)
                    ch(dve.tensor_scalar(T2, T3, BV[:, V_KA + p:V_KA + p + 1], oka[:, p:p + 1], ALU.mult, ALU.add))
                    ch(dve.tensor_tensor(K, K, T2, ALU.mult))
                    ch(dve.tensor_tensor(T3, T1, T3, ALU.mult))
                    blocks(BB[:, :, p, :], T3, T5)
                    blocks(KB[:, :, p, :], K, T5)
                    blocks(AR[:, :, p, 1, :], R, T4)
                    ch(dve.tensor_copy(PC[:, :, p], T4[:, 63:TOK:64]))
                    dve.scalar_tensor_tensor(T1, R, BV[:, V_RK + p:V_RK + p + 1], K, ALU.mult, ALU.mult).then_inc(d4.h, 1)
                    if p >= 1:
                        dve.wait_ge(vm.h, vm.at(p))
                    for h in range(2):
                        q = slice(64 * h, 64 * h + 64)
                        ins = dve.tensor_copy(VB[q, :, 64 * h:64 * h + 64], V[q, :].rearrange("p (c n) -> p c n", c=NCH))
                        ins.then_inc(vb.h, 1)
                    dve.wait_ge(sp2.h, sp2.at(p + 1))
                    dve.tensor_tensor(OBT[:, p, 0:512], bank[6][:, :], V[:, 0:512], ALU.mult).then_inc(d5.h, 1)
                    dve.tensor_tensor(OBT[:, p, 512:TOK], bank[7][:, 0:64], V[:, 512:], ALU.mult).then_inc(d5.h, 1)
                    dve.wait_ge(d5.h, d5.at(2 * p + 2))
                    dve.wait_ge(vb.h, vb.at(2 * p + 2))
                dve_chain.end(ch.n)

            @block.scalar
            def _(act):
                act.wait_ge(sh.h, sh.at(1))
                act.activation(LW[0:64, :], LW[0:64, :], ACT.Tanh).then_inc(tn.h, 1)
                act.activation(LG, LG, ACT.Sigmoid).then_inc(tn.h, 1)
                for p in range(4):
                    act.wait_ge(za.h, za.at(p + 1))
                    if p >= 1:
                        act.wait_ge(d5.h, d5.at(2 * p))
                    for i, (dst, col) in enumerate(((T0, V_W0), (T3, V_A0))):
                        act.activation(dst[:, 0:512], bank[2 * i][:, :], ACT.Sigmoid, bias=BV[:, col + p:col + p + 1])
                        act.activation(dst[:, 512:], bank[2 * i + 1][:, 0:64], ACT.Sigmoid,
                                       bias=BV[:, col + p:col + p + 1]).then_inc(zg.h, 1)
                    act.activation(G[:, p, 0:512], bank[4][:, :], ACT.Copy)
                    act.activation(G[:, p, 512:TOK], bank[5][:, 0:64], ACT.Copy).then_inc(zg.h, 1)
                    act.wait_ge(d1.h, d1.at(p + 1))
                    act.activation(T0, T2, ACT.Exp, scale=-DECAY).then_inc(e1.h, 1)
                    act.activation(T4[:, :], T1, ACT.Exp, scale=-DECAY).then_inc(e1.h, 1)
                    act.activation(T5[:, :], T1, ACT.Exp, scale=DECAY).then_inc(e1.h, 1)
                    act.wait_ge(sp1.h, sp1.at(p + 1))
                    act.activation(T2[:, 0:512], bank[6][:, :], ACT.Sqrt, bias=eps)
                    act.activation(T2[:, 512:], bank[7][:, 0:64], ACT.Sqrt, bias=eps).then_inc(rt.h, 1)
                    act.wait_ge(vm.h, vm.at(p + 1))
                    act.activation(VC[:, 0:8, p, :], bank[0][:, :].rearrange("p (c n) -> p c n", c=8), ACT.Copy)
                    act.activation(VC[:, 8, p, :], bank[1][:, 0:64], ACT.Copy).then_inc(vcp.h, 1)

            @block.tensor
            def _(pe):
                pe.wait_ge(tn.h, tn.at(2))
                for p in range(4):
                    if p >= 1:
                        pe.wait_ge(vcp.h, vcp.at(p))
                    w = slice(p * P, (p + 1) * P)
                    for i, (lhs, rhs) in enumerate(((W2A[:, 0, w], LW), (W2A[:, 1, w], LW), (G2[:, w], LG))):
                        pe.matmul(bank[2 * i][:, :], lhs, rhs[:, 0:512], start=True, stop=True)
                        m = pe.matmul(bank[2 * i + 1][:, 0:64], lhs, rhs[:, 512:], start=True, stop=True)
                    m.then_inc(za.h, 1)
                    pe.wait_ge(d2.h, d2.at(p + 1))
                    pe.matmul(bank[6][:, :], onesbd, T2[:, 0:512], start=True, stop=True)
                    pe.matmul(bank[7][:, 0:64], onesbd, T2[:, 512:], start=True, stop=True).then_inc(sp1.h, 1)
                    pe.wait_ge(d4.h, d4.at(p + 1))
                    pe.matmul(bank[6][:, :], onesbd, T1[:, 0:512], start=True, stop=True)
                    pe.matmul(bank[7][:, 0:64], onesbd, T1[:, 512:], start=True, stop=True).then_inc(sp2.h, 1)
                    pe.wait_ge(vb.h, vb.at(2 * p + 2))
                    pe.wait_ge(zg.h, zg.at(3 * p + 3))
                    for c in range(NCH):
                        m = pe.matmul(bank[c // 8][:, (c % 8) * 64:(c % 8) * 64 + 64], VB[:, c, :], stackI,
                                      start=True, stop=True)
                    m.then_inc(vm.h, 1)
        rt.end(4)
        loaded.end(64), zc.end(5), sh.end(1), tn.end(2), za.end(4), zg.end(12), d1.end(4), e1.end(12), d2.end(4)
        sp1.end(4), d4.end(4), sp2.end(4), d5.end(8), vb.end(8), vm.end(4), vcp.end(4)

    with ExitStack() as s2:
        BV = sb(s2, "BV2", [P, V_MU + BT])
        XF = X[:, :, :].rearrange("p t d -> p (t d)")
        PF = PB[:, :, :].rearrange("p f n -> p (f n)")
        MORE = sb(s2, "chunk_more", [P, 19 * 512])
        AF = PA[:, :, :].rearrange("p t n -> p (t n)")
        cut = lambda buf, n, first=0: [buf[:, first + 512 * i:first + 512 * i + 512] for i in range(n)]
        wide = lambda buf, first: buf[:, first:first + 1024].rearrange("p (q a n) -> p q a n", q=4, a=2)
        lanes = [(XF, 2560, cut(XF, 1, 4608) + cut(MORE, 9)),
                 (PF, 0, cut(PF, 10, 2048)),
                 (AF, 0, cut(MORE, 10, 9 * 512))]

        class Work:

            def __init__(self, lane):
                buf, first, slabs = lanes[lane]
                self.M1 = wide(buf, first)
                self.M2 = wide(buf, first + 1024)
                (self.Bt, self.Kt, self.Dt, self.Dg, self.O, self.ID, self.D2, self.D2T, self.W1, self.W2) = (
                    x.rearrange("p (q n) -> p q n", q=4) for x in slabs)
                self.D4, self.D4T, self.D8T = self.Dt, self.Dg, self.ID
                self.WT, self.NT = self.D2, self.D2T
                self.YC, self.YQ = (slabs[8][:, 256 * i:256 * i + 256].rearrange("p (q n) -> p q n", q=4)
                                    for i in range(2))
                self.b = bank[2 * lane:2 * lane + 2]

        LANES = 3
        work = [Work(i) for i in range(LANES)]
        ST = sb(s2, "STr", [P, 4, 64])
        TMP = sb(s2, "TMP", [P, 4, 64])
        four_of = lambda x: x.rearrange("p (q n) -> p q n", q=4)
        YB, SA = four_of(PF[:, 7168:7680]), four_of(PF[:, 7680:7936])
        ys = sb(s2, "ys", [P, 2, 4])
        made = [sig(f"stage_products{i}") for i in range(LANES)]
        taken = [sig(f"stage_taken{i}") for i in range(LANES)]
        st_sig, y_sig = sig("state_stored"), sig("y_blocks")
        NS, LAG, PRODUCTS = 18, 6, 17
        last = NCH - 1

        def count(c, k):
            return c // LANES * PRODUCTS + min(k, 16)

        roots = Roots(sig)
        turns = [(c, tau - LAG * c) for tau in range(LAG * last + NS) for c in range(NCH) if 0 <= tau - LAG * c < NS]

        def v4(b):
            return b[:, :].rearrange("p (q n) -> p q n", q=4)

        def v64(b):
            return b[:, 0:256].rearrange("p (q n) -> p q n", q=4)

        def four(pe, b, lhs, rhs, n=P):
            for p in range(4):
                m = pe.matmul(b[:, p * n:(p + 1) * n], lhs[:, p, :], rhs[:, p, :], start=True, stop=True)
            return m

        def pe_stage(pe, c, k):
            lane, w = c % LANES, work[c % LANES]
            b = w.b
            if k == 16:
                return
            if count(c, k):
                pe.wait_ge(taken[lane].h, taken[lane].at(2 * count(c, k)))
            if k in (0, 1):
                for p in range(4):
                    m = pe.matmul(b[p // 2][:, (p % 2) * 256:(p % 2) * 256 + 256], (BB, KB)[k][:, c, p, :],
                                  AR[:, c, p, :, :].rearrange("p a n -> p (a n)"), start=True, stop=True)
            elif k == 2:
                for p in range(4):
                    pe.matmul(b[0][:, p * P:(p + 1) * P], AR[:, c, p, 0, :], BB[:, c, p, :], start=True, stop=True)
                    m = pe.transpose(b[1][:, p * P:(p + 1) * P], BB[:, c, p, :], ident)
            elif k == 3:
                four(pe, b[0], w.Dt, w.Dg)
                m = four(pe, b[1], w.Dg, w.Dt)
            elif k == 4:
                four(pe, b[0], w.D2, w.D2T)
                m = four(pe, b[1], w.D2T, w.ID)
            elif k == 5:
                four(pe, b[0], w.D2T, w.D2)
                m = four(pe, b[1], w.D4T, w.W1)
            elif k == 6:
                four(pe, b[0], w.D4, w.D4T)
                for p in range(4):
                    m = pe.transpose(b[1][:, p * P:(p + 1) * P], KB[:, c, p, :], ident)
            elif k == 7:
                m = four(pe, b[0], w.D8T, w.W2)
            elif k == 8:
                for p in range(4):
                    m = pe.transpose(b[1][:, p * P:(p + 1) * P], w.W1[:, p, :], ident)
            elif k == 9:
                m = four(pe, b[0], w.O, w.WT)
            elif k == 10:
                m = four(pe, b[1], w.NT, w.W1)
            elif k in (11, 12):
                m = four(pe, b[(k + 1) % 2], w.NT, w.W2)
            elif k == 13:
                if c:
                    pe.wait_ge(st_sig.h, st_sig.at(c))
                if c == last:
                    pe.wait_ge(loaded.h, loaded.at(32))
                for p in range(4):
                    o = b[0][:, p * 64:(p + 1) * 64]
                    pe.matmul(o, AR[:, c, p, 0, :], ST[:, p, :], start=True, stop=False)
                    m = pe.matmul(o, w.M2[:, p, 0, :], VC[:, c, p, :], start=False, stop=True)
            elif k == 14:
                m = four(pe, b[1], w.W2, TMP, 64)
            elif k == 15:
                for p in range(4):
                    o = b[1][:, p * 64:(p + 1) * 64]
                    pe.matmul(o, w.Bt[:, p, :], SA[:, p, :], start=True, stop=False)
                    pe.matmul(o, w.Kt[:, p, :], VC[:, c, p, :], start=False, stop=True)
                    o = b[0][:, p * 64:(p + 1) * 64]
                    pe.matmul(o, AR[:, c, p, 1, :], ST[:, p, :], start=True, stop=False)
                    pe.matmul(o, w.M1[:, p, 1, :], SA[:, p, :], start=False, stop=False)
                    m = pe.matmul(o, w.M2[:, p, 1, :], VC[:, c, p, :], start=False, stop=True)
            else:
                pe.wait_ge(y_sig.h, y_sig.at(c + 1))
                for p in range(4):
                    m = pe.matmul(b[1][:, p * 64:(p + 1) * 64], YB[:, p, :], stackI, start=True, stop=True)
            m.then_inc(made[lane].h, 1)

        def act_stage(act, c, k):
            lane, w = c % LANES, work[c % LANES]
            b = w.b
            copies = {2: [(w.Bt, v4(b[1]))], 3: [(w.D2, v4(b[0])), (w.D2T, v4(b[1]))], 4: [(w.D4T, v4(b[0]))],
                      5: [(w.D4, v4(b[0]))], 6: [(w.D8T, v4(b[0])), (w.Kt, v4(b[1]))],
                      8: [(w.WT, v4(b[1]))], 9: [(w.NT, v4(b[0]))],
                      13: [(TMP[:, :, :], v64(b[0]))], 14: [(SA, v64(b[1]))]}.get(k, [])
            if copies:
                act.wait_ge(made[lane].h, made[lane].at(count(c, k) + 1))
                for dst, src in copies:
                    ins = act.activation(dst, src, ACT.Copy)
                ins.then_inc(taken[lane].h, 1 if k in (2, 4, 5) else 2)

        def dve_stage(dve, ch, c, k):
            lane, w = c % LANES, work[c % LANES]
            b, tt = w.b, dve.tensor_tensor
            if k in (3, 6, 8, 9, 13, 14):
                return
            bc4 = lambda m: m.unsqueeze(1).broadcast_to([P, 4, P])
            parts = 1 if k in (2, 4, 5) else 2
            if k == 16:
                roots.get(dve)
                for h in range(2):
                    q = slice(64 * h, 64 * h + 64)
                    ins = tt(YB[q, :, 64 * h:64 * h + 64], w.YC[q, :, :],
                             ys[q, 1, :].unsqueeze(2).broadcast_to([64, 4, 64]), ALU.mult)
                    if h == 0:
                        ch(ins)
                ins.then_inc(y_sig.h, 1)
                return
            dve.wait_ge(made[lane].h, made[lane].at(count(c, k) + 1))
            if k in (0, 1):
                for q in range(2):
                    ins = tt((w.M1, w.M2)[k][:, 2 * q:2 * q + 2, :, :].rearrange("p q a n -> p q (a n)"),
                             b[q][:, :].rearrange("p (q n) -> p q n", q=2),
                             maskSI.unsqueeze(1).broadcast_to([P, 2, 256]), ALU.mult)
                    if q == 0:
                        ch(ins)
            elif k == 2:
                ch(tt(w.Dg, w.M1[:, :, 0, :], bc4(mask16), ALU.mult))
                ch(tt(w.O, w.M1[:, :, 0, :], bc4(maskO), ALU.mult))
                ch(tt(w.ID, w.Dg, bc4(ident), ALU.add))
                ins = tt(w.Dt, v4(b[0]), bc4(mask16L), ALU.mult)
            elif k == 4:
                ins = tt(w.W1, v4(b[1]), w.ID, ALU.add)
            elif k == 5:
                ins = tt(w.W2, v4(b[1]), w.W1, ALU.add)
            elif k == 7:
                ins = tt(w.W1, v4(b[0]), w.W2, ALU.add)
            elif k == 10:
                ins = tt(w.W2, v4(b[1]), w.W1, ALU.add)
            elif k in (11, 12):
                ins = tt(w.W2, v4(b[(k + 1) % 2]), w.W1, ALU.add)
            elif k == 15:
                ch(tt(ST[:, :, :], v64(b[1]), ST[:, :, :], ALU.add))
                tt(ST[:, :, :], ST[:, :, :], PC[:, c, :].unsqueeze(2).broadcast_to([P, 4, 64]),
                   ALU.mult).then_inc(st_sig.h, 1)
                ch(dve.tensor_reduce(ys[:, 0, :], v64(b[0]), AX.X, ALU.add))
                ch(dve.tensor_scalar(ys[:, 0, :], ys[:, 0, :], 1.0 / BHD, None, ALU.mult))
                tt(w.YC, v64(b[0]), ys[:, 0, :].unsqueeze(2).broadcast_to([P, 4, 64]),
                   ALU.subtract).then_inc(taken[lane].h, 2)
                dve.wait_ge(taken[lane].h, taken[lane].at(2 * count(c, k) + 2))
                ch(tt(w.YQ, w.YC, w.YC, ALU.mult))
                ch(dve.tensor_reduce(ys[:, 1, :], w.YQ, AX.X, ALU.add))
                roots.send(dve.tensor_scalar(ys[:, 1, :], ys[:, 1, :], 1.0 / BHD, BLN_EPS, ALU.mult, ALU.add))
                return
            else:
                for p in range(4):
                    ins = dve.tensor_scalar(w.YQ[:, p, :], b[1][:, p * 64:(p + 1) * 64], BV[:, V_LG + p:V_LG + p + 1],
                                            BV[:, V_LB + p:V_LB + p + 1], ALU.mult, ALU.add)
                    if p < 3:
                        ch(ins)
                ins.then_inc(taken[lane].h, 2)
                dve.wait_ge(taken[lane].h, taken[lane].at(2 * count(c, k) + 2))
                o = OBT[:, :, c * 64:c * 64 + 64]
                ch(tt(o, o, w.YQ, ALU.add))
                ch(tt(o, o, G[:, :, c * 64:c * 64 + 64], ALU.mult))
                return
            ins.then_inc(taken[lane].h, parts)

        zs = sig("state_zeroed")
        with nc.Block() as block:
            @block.sync
            def _(sp):
                sp.dma_start(BV[:, :], io["bvec"]).then_inc(loaded.h, 16)
                sp.wait_ge(st_sig.h, st_sig.at(last))
                sp.dma_start(io["out_b_wkv_p"], ST[:, :, :]).then_inc(stored.h, 16)
                sp.wait_ge(made[(last - 1) % LANES].h,
                           made[(last - 1) % LANES].at(count(last - 1, 15) + 1))
                sp.wait_ge(stored.h, stored.at(16))
                sp.dma_start(ST[:, :, :], io["wkv_t"]).then_inc(loaded.h, 16)
                sp.wait_ge(st_sig.h, st_sig.at(NCH))
                sp.dma_start(io["out_b_wkv_s"], ST[:, :, :]).then_inc(stored.h, 16)
                sp.wait_ge(stored.h, stored.at(32))

            @block.tensor
            def _(pe):
                pe.wait_ge(zs.h, zs.at(2))
                for c, k in turns:
                    pe_stage(pe, c, k)

            @block.scalar
            def _(act):
                for c, k in turns:
                    act_stage(act, c, k)

            @block.gpsimd
            def _(pool):
                for c in range(NCH):
                    roots.give(pool, c, ys[:, 1, :])

            @block.vector
            def _(dve):
                ch = Chain(dve, dve_chain)
                dve.memset(ST[:, :, :], 0.0).then_inc(zs.h, 1)
                dve.memset(YB, 0.0).then_inc(zs.h, 1)
                dve.wait_ge(zs.h, zs.at(2))
                dve.wait_ge(loaded.h, loaded.at(16))
                for c, k in turns:
                    if (c, k) == (last, 15):
                        dve.wait_ge(loaded.h, loaded.at(32))
                    dve_stage(dve, ch, c, k)
                dve_chain.end(ch.n)
        roots.end()
        for lane in range(LANES):
            n = len(range(lane, NCH, LANES)) * PRODUCTS
            made[lane].end(n), taken[lane].end(2 * n)
        y_sig.end(NCH)
        loaded.end(32), stored.end(32), zs.end(2), st_sig.end(NCH)
    st.close()


def peer(nc, io, layer, sb, sig, bank, junk, ident, X, norm):
    loaded, dve_chain = sig("loaded"), sig("dve_chain")
    st = ExitStack()
    L = f"l{layer}"
    XN = sb(st, f"XN{L}", [P, NT, D])
    QP = sb(st, f"QP{L}", [P, NT, PH, P])
    KB = sb(st, f"KY{L}", [P, PH + 1, 2 * NK])
    IOT = sb(st, f"IOT{L}", [P, PK])
    FOLD = sb(st, f"FOLD{L}", [P, DEC])
    ring = sb(st, f"ring{L}", [P, RING, 2 * D])
    flat = ring[:, :, :].rearrange("p s n -> p (s n)")
    at = [2 * D * RING // 2]

    def in_ring(n):
        at[0] += n
        assert at[0] <= 2 * D * RING
        return flat[:, at[0] - n:at[0]]

    WQ = in_ring(KD * D).rearrange("p (k n) -> p k n", k=KD)
    XT = in_ring(KD * PADT).rearrange("p (k n) -> p k n", k=KD)
    wl, kz, kl, fo = sig("weights_loaded0"), sig("keys_zeroed"), sig("keys_loaded"), sig("fold_ready")
    mm_, ev = sig("products"), sig("evacuated")
    QUERIES = 2 * PH

    def load_w(sp):
        sp.dma_start(WQ, io[f"l{layer}_peer_wq"].rearrange("(k p) n -> p k n", p=P)).then_inc(wl.h, 16)

    norm(st, L, io[f"l{layer}_norm_ffn"], False, XN, XT, load_w, zero_rows=True, place=in_ring)

    def sp_start(sp):
        sp.wait_ge(kz.h, kz.at(1))
        kv = io[f"keys_t{layer}"]
        for half in range(2):
            q, n = slice(64 * half, 64 * half + 64), slice(NK * half, NK * half + NK)
            sp.dma_start(KB[q, 0:PH, n], kv[:, half].rearrange("h d n -> d h n")).then_inc(kl.h, 16)
            sp.dma_start(KB[q, PH, n], kv[0, half]).then_inc(kl.h, 16)
        sp.dma_start(XN[DEC:P, NT - 1, :], XN[0:DEC, NT - 1, :]).then_inc(kl.h, 16)
        sp.wait_ge(kl.h, kl.at(80))

    def pool_start(pool):
        pool.memset(KB[:, :, :], 0.0).then_inc(kz.h, 1)
        pool.iota(IOT[:, :], [[1, PK]], base=0, channel_multiplier=0,
                  allow_small_or_imprecise_dtypes=True).then_inc(kz.h, 1)

    def pe_start(pe):
        pe.wait_ge(wl.h, wl.at(16))
        n = 0
        for h in range(PH):
            for a, b in ((0, 512), (512, PADT)):
                if n >= 3:
                    pe.wait_ge(ev.h, ev.at(n - 2))
                for k in range(KD):
                    m = pe.matmul(bank[3 + n % 3][:, 0:b - a], WQ[:, k, h * P:(h + 1) * P], XT[:, k, a:b],
                                  start=(k == 0), stop=(k == KD - 1))
                m.then_inc(mm_.h, 1)
                n += 1
            if h == 0:
                pe.wait_ge(kl.h, kl.at(80))
                pe.wait_ge(ev.h, ev.at(2))
                pe.matmul(bank[0][:, 0:2 * NK], QP[:, 0, 0, :], KB[:, 0, :], start=True, stop=True).then_inc(rp.h, 1)
        pe.wait_ge(ev.h, ev.at(QUERIES))

    def act_start(act):
        n = 0
        for h in range(PH):
            for t0, t1 in ((0, 4), (4, 5)):
                act.wait_ge(mm_.h, mm_.at(n + 1))
                src = bank[3 + n % 3]
                if t0 == 4 and h % 2:
                    act.activation(QP[:, 4, h, 0:DEC], src[:, DEC:P], ACT.Copy)
                    ins = act.activation(QP[:, 4, h, DEC:P], src[:, 0:DEC], ACT.Copy)
                else:
                    ins = act.activation(QP[:, t0:t1, h, :],
                                         src[:, 0:(t1 - t0) * P].rearrange("p (t n) -> p t n", n=P), ACT.Copy)
                ins.then_inc(ev.h, 1)
                n += 1
            if h == 0:
                act.wait_ge(rp.h, rp.at(1))
                act.activation(SC[:, :, :].rearrange("p a n -> p (a n)"), bank[0][:, 0:2 * NK],
                               ACT.Copy).then_inc(rc.h, 1)
            if h == 2:
                act_route_exp(act, 0)
        act.wait_ge(ev.h, ev.at(QUERIES))

    QS = sb(st, f"QS{L}", [P, P])
    QPF = QP[:, :, :, :].rearrange("p t h n -> p (t h n)")
    SC = sb(st, f"SC{L}", [P, 2, NK])
    SW = sb(st, f"SW{L}", [P, 2, NK])
    TS_ = sb(st, f"TS{L}", [P, 2, PK])
    TI = sb(st, f"TI{L}", [P, 2, PK], U32)
    TF = sb(st, f"TF{L}", [P, 2, PK])
    CA = sb(st, f"CA{L}", [P, PK, PK])
    CW = sb(st, f"CW{L}", [P, PK * PK])
    BS = sb(st, f"BS{L}", [P, PK])
    BP = sb(st, f"BP{L}", [P, PK], U32)
    BQ = sb(st, f"BQ{L}", [P, 2, PK], U32)
    BF = sb(st, f"BF{L}", [P, 2, PK])
    OH = sb(st, f"OH{L}", [P, PK, PK])
    SEL = sb(st, f"SEL{L}", [P, 2, PK])
    EF = sb(st, f"EF{L}", [P, PK])
    EI = sb(st, f"EI{L}", [P, 2, PK], U32)
    NM = sb(st, f"NM{L}", [P, 1])
    GX = sb(st, f"GX{L}", [P, PK])
    GS = sb(st, f"GS{L}", [P, 2])
    GT = sb(st, f"GT{L}", [P, 2, PK])
    HD = sb(st, f"HD{L}", [P, 2, PK])
    HG = sb(st, f"HG{L}", [P, 2, PK])
    HW = sb(st, f"HW{L}", [P, 1])
    DG = sb(st, f"DG{L}", [P, 4, P])
    rp, rc, rm, rx, ri, ud, ge, vd = (sig(n) for n in (
        "key_scores", "key_scores_copied", "best_known", "gate_exps", "experts_known", "u_dots", "gelus", "v_added"))
    dg, xa, hw, va = sig("diagonals"), sig("sums_added"), sig("weights_known"), sig("v_added_here")
    G = 4 * PH + PH // 2

    def two_heads(g):
        return isinstance(g, int) and g >= 4 * PH

    SV = SLOTS // 4
    SP = SLOTS - SV
    passed, passed_v = sig("slot_waits_passed"), sig("score_waits_passed")
    qs, steps = sig("queries_placed"), sig("route_steps")
    gd = [sig(f"gathered{i}") for i in range(RING)]
    rows = io[f"uv{layer}"]

    def pe_route(pe, g, kh):
        if two_heads(g):
            pe.wait_ge(rc.h, rc.at(g))
            for odd in range(2):
                h = 2 * (g - 4 * PH) + odd
                m = pe.matmul(bank[0][:, 0:2 * NK], QP[:, NT - 1, h, :], KB[:, h, :], start=(odd == 0), stop=(odd == 1))
            m.then_inc(rp.h, 1)
            return
        pe.wait_ge(qs.h, qs.at(g))
        pe.wait_ge(rc.h, rc.at(g))
        pe.matmul(bank[0][:, 0:2 * NK], QS[:, :],
                  KB[:, kh, :], start=True, stop=True).then_inc(rp.h, 1)

    def act_route_in(act, g):
        if not two_heads(g):
            act.wait_ge(rp.h, rp.at(g))
            act.activation(QS[:, :], QPF[:, bass.ds(g * P, P)], ACT.Copy).then_inc(qs.h, 1)
        act.wait_ge(rp.h, rp.at(g + 1))
        act.wait_ge(ri.h, ri.at(g))
        act.activation(SC[:, :, :].rearrange("p a n -> p (a n)"), bank[0][:, 0:2 * NK], ACT.Copy).then_inc(rc.h, 1)

    def act_route_exp(act, g):
        act.wait_ge(rm.h, rm.at(g + 1))
        act.activation(GX[:, :], BS[:, :], ACT.Exp, bias=NM[:, :], accum_out=GS[:, 0:1]).then_inc(rx.h, 1)

    def dve_route(dve, g, par):
        dve.sem_clear(steps.h)
        ch = Chain(dve, steps)
        dve.wait_ge(rc.h, rc.at(g + 1))
        dve.sem_inc(passed_v.h, 1)
        for a in range(2):
            ch(dve.max(TS_[:, a, 0:8], SC[:, a, :]))
            ch(dve.match_replace(SW[:, a, :], TS_[:, a, 0:8], SC[:, a, :], -3e38))
            ch(dve.max(TS_[:, a, 8:16], SW[:, a, :]))
            ch(dve.max_index(TI[:, a, 0:8], TS_[:, a, 0:8], SC[:, a, :]))
            ch(dve.max_index(TI[:, a, 8:16], TS_[:, a, 8:16], SW[:, a, :]))
        ch(dve.tensor_copy(TF[:, :, :], TI[:, :, :]))
        ch(dve.tensor_tensor(CA[:, :, :], TS_[:, 0, :].unsqueeze(2).broadcast_to([P, PK, PK]),
                             TS_[:, 1, :].unsqueeze(1).broadcast_to([P, PK, PK]), ALU.add))
        cf = CA[:, :, :].rearrange("p a b -> p (a b)")
        ch(dve.max(BS[:, 0:8], cf))
        ch(dve.match_replace(CW[:, :], BS[:, 0:8], cf, -3e38))
        ch(dve.max(BS[:, 8:16], CW[:, :]))
        dve.tensor_scalar(NM[:, :], BS[:, 0:1], -1.0, None, ALU.mult).then_inc(rm.h, 1)
        ch(dve.max_index(BP[:, 0:8], BS[:, 0:8], cf))
        ch(dve.max_index(BP[:, 8:16], BS[:, 8:16], CW[:, :]))
        ch(dve.tensor_single_scalar(BQ[:, 0, :], BP[:, :], 4, op=ALU.logical_shift_right))
        ch(dve.tensor_single_scalar(BQ[:, 1, :], BP[:, :], 15, op=ALU.bitwise_and))
        ch(dve.tensor_copy(BF[:, :, :], BQ[:, :, :]))
        for a in range(2):
            ch(dve.tensor_tensor(OH[:, :, :], BF[:, a, :].unsqueeze(2).broadcast_to([P, PK, PK]),
                                 IOT[:, :].unsqueeze(1).broadcast_to([P, PK, PK]), ALU.is_equal))
            ch(dve.tensor_tensor(OH[:, :, :], OH[:, :, :], TF[:, a, :].unsqueeze(1).broadcast_to([P, PK, PK]),
                                 ALU.mult))
            ch(dve.tensor_reduce(SEL[:, a, :], OH[:, :, :], AX.X, ALU.add))
        ch(dve.scalar_tensor_tensor(EF[:, :], SEL[:, 0, :], float(NK), SEL[:, 1, :], ALU.mult, ALU.add))
        ch(dve.tensor_copy(EI[:, par, :], EF[:, :]))
        dve.wait_ge(rx.h, rx.at(g + 1))
        ch(dve.reciprocal(GS[:, 1:2], GS[:, 0:1]))
        dve.tensor_scalar(GT[:, par, :], GX[:, :], GS[:, 1:2], None, ALU.mult).then_inc(ri.h, 1)

    def use(g, k):
        return g * (SLOTS // RING) + k // RING + 1

    def pool_group(pool, g, par):
        pool.wait_ge(ri.h, ri.at(g + 1))
        for k in range(SLOTS):
            if k % 4 == 3:
                pool.wait_ge(va.h, va.at(g * SV + k // 4 + 1))
            else:
                pool.wait_ge(vd.h, vd.at(g * SP + k - k // 4 + 1))
            if k == RING // 2:
                pool.wait_ge(mm_.h, mm_.at(QUERIES))
            pool.sem_inc(passed.h, 1)
            pool.indirect_dma_start(ring[:, k % RING, :], None, rows,
                                    bass.IndirectOffsetOnAxis(ap=EI[:, par, k:k + 1], axis=0)
                                    ).then_inc(gd[k % RING].h, 16)

    def act_group(act, g, par):
        for b in range(SLOTS // 2):
            act.wait_ge(ud.h, ud.at(g * SLOTS + 2 * b + 2 + 2))
            act.activation(HG[:, par, 2 * b:2 * b + 2], HD[:, par, 2 * b:2 * b + 2], ACT.Gelu).then_inc(ge.h, 1)

    def dve_group(dve, g, t, par, route=None):

        def dot(k):
            dve.wait_ge(gd[k % RING].h, gd[k % RING].at(16 * use(g, k)))
            dve.wait_ge(ud.h, ud.at(g * SLOTS + k + 2))
            dve.scalar_tensor_tensor(junk[:, :], ring[:, k % RING, 0:D], 1.0, XN[:, t, :], ALU.mult, ALU.mult,
                                     accum_out=HD[:, par, k:k + 1]).then_inc(ud.h, 1)

        def weigh(k):
            if k % 2 == 0:
                dve.wait_ge(ge.h, ge.at(g * (SLOTS // 2) + k // 2 + 1))
            if k % 4 != 3:
                i = k - k // 4
                dve.wait_ge(vd.h, vd.at(g * SP + i + SP - 3))
                on, cols = (FOLD, DEC) if two_heads(g) else (ident, P)
                dve.tensor_scalar(DG[:, i % 4, 0:cols], on[:, :], HG[:, par, k:k + 1], GT[:, par, k:k + 1],
                                  ALU.mult, ALU.mult).then_inc(dg.h, 1)
            else:
                i = g * SV + k // 4
                dve.tensor_tensor(HW[:, :], HG[:, par, k:k + 1], GT[:, par, k:k + 1], ALU.mult).then_inc(hw.h, 1)
                dve.wait_ge(hw.h, hw.at(i + 1))
                dve.wait_ge(va.h, va.at(i + SV))
                dve.wait_ge(xa.h, xa.at(2 * g + 2))
                dve.scalar_tensor_tensor(X[:, t, :], ring[:, k, D:2 * D], HW[:, :], X[:, t, :],
                                         ALU.mult, ALU.add).then_inc(va.h, 1)

        for b in range(SLOTS // 2):
            for k in (2 * b, 2 * b + 1):
                dot(k)
                if b:
                    weigh(k - 2)
            if b == 1 and route is not None:
                route()
        weigh(SLOTS - 2)
        weigh(SLOTS - 1)
        dve.wait_ge(va.h, va.at((g + 1) * SV + SV))
        for half in range(2):
            q = slice(512 * half, 512 * half + 512)
            dve.wait_ge(vd.h, vd.at((g + 1) * SP + SP))
            n = DEC if two_heads(g) else P
            dve.tensor_tensor(X[0:n, t, q], bank[1 + 2 * par + half][0:n, :], X[0:n, t, q],
                              ALU.add).then_inc(xa.h, 1)

    def pe_group(pe, g, par):
        n = DEC if two_heads(g) else P
        pe.wait_ge(xa.h, xa.at(2 * g))
        for k in range(SLOTS):
            if k % 4 == 3:
                continue
            i = k - k // 4
            pe.wait_ge(dg.h, dg.at(g * SP + i + 1))
            for half in range(2):
                m = pe.matmul(bank[1 + 2 * par + half][0:n, :], DG[:, i % 4, 0:n],
                              ring[:, k, D + 512 * half:D + 512 * half + 512],
                              start=(i == 0), stop=(i == SP - 1))
            m.then_inc(vd.h, 1)

    def groups(eng, body):
        with eng.Fori(0, 3) as t, eng.Fori(0, PH // 2) as j:
            for par in range(2):
                body(t * PH + j * 2 + par, t, par, j * 2 + par + 1, False)
        with eng.Fori(0, PH // 2 - 1) as j:
            for par in range(2):
                body(3 * PH + j * 2 + par, 3, par, j * 2 + par + 1, False)
        for g in range(4 * PH - 2, G):
            body(g, min(g // PH, 4), g % 2, g % PH + 1, g == G - 1)

    with nc.Block() as block:
        @block.sync
        def _(sp):
            sp_start(sp)

        @block.gpsimd
        def _(pool):
            pool_start(pool)
            groups(pool, lambda g, t, par, hn, last: pool_group(pool, g, par))

        @block.tensor
        def _(pe):
            pe_start(pe)

            def body(g, t, par, hn, last):
                if not last:
                    pe_route(pe, g + 1, hn)
                pe_group(pe, g, par)
            groups(pe, body)
            pe.wait_ge(xa.h, xa.at(2 * G + 2))
            pe.wait_ge(va.h, va.at(G * SV + SV))
            for half in range(2):
                pe.matmul(bank[1 + half][0:DEC, :], ident[:, DEC:P], X[:, NT - 1, 512 * half:512 * half + 512],
                          start=True, stop=True).then_inc(mm_.h, 1)

        @block.scalar
        def _(act):
            act_start(act)

            def body(g, t, par, hn, last):
                if last:
                    act_group(act, g, par)
                    return
                act_route_in(act, g + 1)
                for b in range(SLOTS // 2):
                    act.wait_ge(ud.h, ud.at(g * SLOTS + 2 * b + 2 + 2))
                    act.activation(HG[:, par, 2 * b:2 * b + 2], HD[:, par, 2 * b:2 * b + 2],
                                   ACT.Gelu).then_inc(ge.h, 1)
                    if b == 1:
                        act_route_exp(act, g + 1)
            groups(act, body)

        @block.vector
        def _(dve):
            dve.engine_nop().then_inc(vd.h, SP)
            dve.engine_nop().then_inc(va.h, SV)
            dve.engine_nop().then_inc(ud.h, 2)
            dve.engine_nop().then_inc(xa.h, 2)
            dve.tensor_tensor(FOLD[:, :], ident[:, 0:DEC], ident[:, DEC:P], ALU.add).then_inc(fo.h, 1)
            dve.wait_ge(fo.h, fo.at(1))
            dve.wait_ge(kz.h, kz.at(2))
            dve_route(dve, 0, 0)

            def body(g, t, par, hn, last):
                dve_group(dve, g, t, par, None if last else lambda: dve_route(dve, g + 1, 1 - par))
            groups(dve, body)
            for half in range(2):
                q = slice(512 * half, 512 * half + 512)
                dve.wait_ge(mm_.h, mm_.at(QUERIES + half + 1))
                dve.tensor_tensor(X[0:DEC, NT - 1, q], bank[1 + half][0:DEC, :], X[0:DEC, NT - 1, q], ALU.add)
    mm_.end(QUERIES + 2), ev.end(QUERIES), wl.end(16), kz.end(2), kl.end(80), fo.end(1)
    dg.end(G * SP), xa.end(2 + 2 * G), hw.end(G * SV), va.end(SV + G * SV)
    passed.end(G * SLOTS), passed_v.end(G)
    qs.end(4 * PH - 1), rp.end(G), rc.end(G), rm.end(G), rx.end(G), ri.end(G), ud.end(2 + G * SLOTS), ge.end(G * SLOTS // 2)
    vd.end(SP + G * SP)
    for s in gd:
        s.end(16 * G * SLOTS // RING)
    st.close()


def layer1(nc, io, sb, sig, bank, ident, X, norm, attention):
    loaded, stored, dve_chain = sig("loaded"), sig("stored"), sig("dve_chain")
    st = ExitStack()
    PCm = sb(st, "PCm", [P, NT, CCOLS])
    OD = sb(st, "OD", [P, NT, 2 * DW])
    with ExitStack() as s2:
        XT = sb(s2, "XT1", [P, KD, PADT])
        XN = sb(s2, "XN1", [P, NT, D])
        W = sb(s2, "W1", [P, KD, 1024 + 512])
        CW = [(0, 512, 0), (512, 1024, 512), (1024, CCOLS, 1024), (CCOLS, CCOLS + 512, 0), (CCOLS + 512, CCOLS + 1024, 512)]
        wv = io["l1_w_in"].rearrange("(k p) n -> p k n", p=P)
        wl = [sig(f"weights_loaded{i}") for i in range(5)]
        mm_, ev = sig("products"), sig("evacuated")

        def load_w(sp):
            for i in range(3):
                a, b, o = CW[i]
                sp.dma_start(W[:, :, o:o + b - a], wv[:, :, a:b]).then_inc(wl[i].h, 16)

        norm(s2, "c", io["l1_norm_mix"], False, XN, XT, load_w)
        with nc.Block() as block:
            @block.sync
            def _(sp):
                for i in (3, 4):
                    a, b, o = CW[i]
                    sp.wait_ge(mm_.h, mm_.at(NT * (i - 2)))
                    sp.dma_start(W[:, :, o:o + b - a], wv[:, :, a:b]).then_inc(wl[i].h, 16)

            @block.tensor
            def _(pe):
                n = 0
                for i, (a, b, o) in enumerate(CW):
                    pe.wait_ge(wl[i].h, wl[i].at(16))
                    for t in range(NT):
                        if n >= 4:
                            pe.wait_ge(ev.h, ev.at(n - 3))
                        for k in range(KD):
                            m = pe.matmul(bank[n % 4][:, 0:b - a], XT[:, k, t * P:(t + 1) * P], W[:, k, o:o + b - a],
                                          start=(k == 0), stop=(k == KD - 1))
                        m.then_inc(mm_.h, 1)
                        n += 1

            @block.scalar
            def _(act):
                n = 0
                for i, (a, b, o) in enumerate(CW):
                    for t in range(NT):
                        act.wait_ge(mm_.h, mm_.at(n + 1))
                        src = bank[n % 4][:, 0:b - a]
                        if i < 3:
                            ins = act.activation(PCm[:, t, a:b], src, ACT.Copy)
                        else:
                            ins = act.activation(OD[:, t, a - CCOLS:b - CCOLS], src, ACT.Gelu)
                        ins.then_inc(ev.h, 1)
                        n += 1
        for s in wl:
            s.end(16)
        mm_.end(5 * NT), ev.end(5 * NT)

    with ExitStack() as s2:
        lg = sb(s2, "dlg", [P, DW])
        lb = sb(s2, "dlb", [P, DW])
        WT = sb(s2, "dwt", [P, 4, P])
        DB = sb(s2, "dbs", [P, 4])
        VN = sb(s2, "VN", [P, NT, DW])
        JQ = sb(s2, "JQ", [P, DW])
        ms = sb(s2, "ms", [P, NT, 2])
        roots = Roots(sig)
        wm, vn, mm_, dd = sig("mix_masked"), sig("normed"), sig("products"), sig("added")
        with nc.Block() as block:
            @block.sync
            def _(sp):
                for dst, src in ((lg[:, :], io["d_ln_g"].partition_broadcast(P)),
                                 (lb[:, :], io["d_ln_b"].partition_broadcast(P)),
                                 (WT[:, :, :], io["dws_t"]), (DB[:, :], io["dbs_t"])):
                    sp.dma_start(dst, src).then_inc(loaded.h, 16)
                sp.wait_ge(vn.h, vn.at(NT))
                sp.dma_start(io["out_d_v_s"][0], VN[0:DEC, 4, :]).then_inc(stored.h, 16)
                sp.wait_ge(stored.h, stored.at(16))

            @block.gpsimd
            def _(pool):
                pool.wait_ge(loaded.h, loaded.at(64))
                pool.affine_select(out=WT[:, :, :], in_=WT[:, :, :], compare_op=ALU.is_ge, fill=0.0, base=0,
                                   pattern=[[0, 4], [1, P]], channel_multiplier=-1).then_inc(wm.h, 1)
                for t in range(NT):
                    roots.give(pool, t, ms[:, t, 1:2])

            @block.vector
            def _(dve):
                ch = Chain(dve, dve_chain)
                dve.wait_ge(loaded.h, loaded.at(64))
                for t in range(NT):
                    v = OD[:, t, DW:]
                    mean, var = ms[:, t, 0:1], ms[:, t, 1:2]
                    ch(dve.tensor_reduce(mean, v, AX.X, ALU.add))
                    ch(dve.tensor_scalar(mean, mean, 1.0 / DW, None, ALU.mult))
                    ch(dve.tensor_scalar(VN[:, t, :], v, mean, None, ALU.subtract))
                    ch(dve.tensor_tensor(JQ[:, :], VN[:, t, :], VN[:, t, :], ALU.mult))
                    ch(dve.tensor_reduce(var, JQ[:, :], AX.X, ALU.add))
                    roots.ask(dve, dve.tensor_scalar(var, var, 1.0 / DW, EPS, ALU.mult, ALU.add))
                    ch(dve.scalar_tensor_tensor(VN[:, t, :], VN[:, t, :], var, lg[:, :], ALU.mult, ALU.mult))
                    dve.tensor_tensor(VN[:, t, :], VN[:, t, :], lb[:, :], ALU.add).then_inc(vn.h, 1)
                for t in range(NT):
                    dve.wait_ge(mm_.h, mm_.at(t + 1))
                    for g in range(4):
                        q = slice(g * P, (g + 1) * P)
                        ins = dve.scalar_tensor_tensor(OD[:, t, q], bank[t % 2][:, q], DB[:, g:g + 1], OD[:, t, q],
                                                       ALU.add, ALU.mult)
                    ins.then_inc(dd.h, 1)
                dve_chain.end(ch.n)

            @block.tensor
            def _(pe):
                pe.wait_ge(wm.h, wm.at(1))
                for t in range(NT):
                    pe.wait_ge(vn.h, vn.at(t + 1))
                    if t >= 2:
                        pe.wait_ge(dd.h, dd.at(t - 1))
                    for g in range(4):
                        q = slice(g * P, (g + 1) * P)
                        m = pe.matmul(bank[t % 2][:, q], WT[:, g, :], VN[:, t, q], start=True, stop=True)
                    m.then_inc(mm_.h, 1)
        roots.end()
        loaded.end(64), stored.end(16), wm.end(1), vn.end(NT), mm_.end(NT), dd.end(NT)

    s3 = ExitStack()
    OC = sb(st, "OC1", [P, NT, 512])
    QT = sb(s3, "QTc", [P, CH_, PADT])
    KT = sb(s3, "KTc", [P, CKV, KT7 * P])
    VV = sb(s3, "VVc", [P, KT7, CKV, CHD])
    MSK = sb(s3, "MSKc", [P, NT, 512])
    with ExitStack() as s2:
        IQT = sb(s2, "IQT", [P, 8, PADT])
        IKT = sb(s2, "IKT", [P, KT7 * P])
        gn = sb(s2, "gnc", [P, 3, CHD])
        RT = sb(s2, "RTc", [P, NT, 64])
        SQ = sb(s2, "SQc", [P, 10, CHD])
        hs = sb(s2, "hsc", [P, 11])
        RC = sb(s2, "RCc", [P, 10, 2, 32])
        RS = sb(s2, "RSc", [P, 10, 2, 32])
        IW = sb(s2, "IWc", [P, NT, 8])
        LG = sb(s2, "LGc", [P, 2, 512])
        SCO = sb(s2, "SCO", [P, 512])
        WK = sb(s2, "WKc", [P, 512])
        M8 = sb(s2, "M8c", [P, 8])
        roots = Roots(sig)
        kz, ro, tr, ev = sig("keys_zeroed"), sig("rotated"), sig("heads_turned"), sig("heads_copied")
        ix, rl, ac = sig("index_scores"), sig("index_relu"), sig("index_added")
        cols = [h * 64 for h in range(8)] + [768 + h * 64 for h in range(8)] + [512, 576, 1280]
        with nc.Block() as block:
            @block.gpsimd
            def _(pool):
                for buf in (QT, IQT, KT):
                    pool.memset(buf[64:P, :, :], 0.0).then_inc(kz.h, 1)
                pool.memset(IKT[64:P, :], 0.0).then_inc(kz.h, 1)
                pool.wait_ge(kz.h, kz.at(4))
                for t in range(NT):
                    roots.give(pool, 2 * t, hs[:, 0:10])
                    roots.give(pool, 2 * t + 1, hs[:, 10:11])

            @block.sync
            def _(sp):
                kvw = io["cache_c_v"][0].rearrange("(k p) h n -> p k h n", p=P)
                for dst, src in (
                    (gn[:, 0, :], io["c_q_gain"].partition_broadcast(P)),
                    (gn[:, 1, :], io["c_k_gain"].partition_broadcast(P)),
                    (gn[:, 2, :], io["c_kidx_gain"].partition_broadcast(P)),
                    (RT[:, :, :], io["rope_c"]), (MSK[:, :, :], io["mask"]),
                    (KT[0:64, :, 4 * P:6 * P], io["ck_t"]), (IKT[0:64, 4 * P:6 * P], io["kidx_t"]),
                    (VV[:, 4:6, :, :].rearrange("p k h n -> p k (h n)"), kvw.rearrange("p k h n -> p k (h n)")),
                ):
                    sp.dma_start(dst, src).then_inc(loaded.h, 16)
                ns = 0
                for t in range(NT):
                    sp.wait_ge(ro.h, ro.at(t + 1))
                    n = P if t < 4 else DEC
                    for name, a, b in (("c_k", 512, 640), ("c_v", 640, 768), ("c_kidx", 1280, 1344)):
                        o = io[f"out_{name}_{'p' if t < 4 else 's'}"][0]
                        if name != "c_kidx":
                            o = o.rearrange("s h n -> s (h n)")
                        sp.dma_start(o[t % 4 * P:t % 4 * P + n, :], PCm[0:n, t, a:b]).then_inc(stored.h, 16)
                        ns += 1
                sp.wait_ge(stored.h, stored.at(16 * ns))

            @block.vector
            def _(dve):
                ch = Chain(dve, dve_chain)
                dve.wait_ge(loaded.h, loaded.at(128))
                for t in range(NT):
                    qk = PCm[:, t, 0:640].rearrange("p (h n) -> p h n", h=10)
                    ik = PCm[:, t, 1280:1344].unsqueeze(1)
                    rms_heads(dve, ch, roots, qk, SQ[:, :, :], hs[:, 0:10], 10, CHD)
                    rms_heads(dve, ch, roots, ik, SQ[:, 0:1, :], hs[:, 10:11], 1, CHD)
                    for a, n, g in ((0, 8, 0), (8, 2, 1)):
                        y = qk[:, a:a + n, :]
                        ch(dve.tensor_tensor(y, y, gn[:, g, :].unsqueeze(1).broadcast_to([P, n, CHD]), ALU.mult))
                    ch(dve.tensor_tensor(ik[:, 0, :], ik[:, 0, :], gn[:, 2, :], ALU.mult))
                    rotate(dve, ch, qk, RT[:, t, :], RC[:, :, :, :], RS[:, :, :, :], 10, 32, None)
                    ch(dve.tensor_copy(VV[:, t if t < 4 else 6, :, :].rearrange("p h n -> p (h n)"), PCm[:, t, 640:768]))
                    ch(dve.tensor_scalar(IW[:, t, :], PCm[:, t, 1344:1352], float(8 ** -0.5) * 0.125, None, ALU.mult))
                    iqk = PCm[:, t, 768:1344].rearrange("p (h n) -> p h n", h=9)
                    rotate(dve, ch, iqk, RT[:, t, :], RC[:, 0:9, :, :], RS[:, 0:9, :, :], 9, 32, ro)
                for t in range(NT):
                    n = QT_KEYS[t] * P
                    for h in range(8):
                        i = t * 8 + h
                        dve.wait_ge(rl.h, rl.at(i + 1))
                        w = IW[:, t, h:h + 1]
                        prev = MSK[:, t, 0:n] if h == 0 else SCO[:, 0:n]
                        ch(dve.scalar_tensor_tensor(SCO[:, 0:n], LG[:, i % 2, 0:n], w, prev, ALU.mult, ALU.add))
                        dve.engine_nop().then_inc(ac.h, 1)
                    if SEL_KEYS[t]:
                        for r in range(SEL_KEYS[t] // 8):
                            src = SCO if r == 0 else WK
                            ch(dve.max(M8[:, :], src[:, 0:n]))
                            ch(dve.match_replace(WK[:, 0:n], M8[:, :], src[:, 0:n], -3e38))
                        ch(dve.tensor_scalar(WK[:, 0:n], WK[:, 0:n], -1e38, NEG, ALU.is_ge, ALU.mult))
                        ch(dve.tensor_tensor(MSK[:, t, 0:n], MSK[:, t, 0:n], WK[:, 0:n], ALU.min))
                dve_chain.end(ch.n)

            @block.tensor
            def _(pe):
                for t in range(NT):
                    pe.wait_ge(ro.h, ro.at(t + 1))
                    for i, c in enumerate(cols):
                        b, o = i // 4, (i % 4) * P
                        if i % 4 == 0 and t >= 1:
                            pe.wait_ge(ev.h, ev.at(5 * (t - 1) + b + 1))
                        m = pe.transpose(bank[b][0:64, o:o + P], PCm[:, t, c:c + 64], ident)
                        if i % 4 == 3 or i == len(cols) - 1:
                            m.then_inc(tr.h, 1)
                pe.wait_ge(kz.h, kz.at(4))
                pe.wait_ge(loaded.h, loaded.at(128))
                pe.wait_ge(ev.h, ev.at(5 * NT))
                for t in range(NT):
                    n, f = QT_KEYS[t] * P, QT_FIRST[t] * P
                    for h in range(8):
                        i = t * 8 + h
                        if i >= 2:
                            pe.wait_ge(rl.h, rl.at(i - 1))
                        pe.matmul(bank[6 + i % 2][:, 0:n], IQT[:, h, t * P:(t + 1) * P], IKT[:, f:f + n],
                                  start=True, stop=True).then_inc(ix.h, 1)

            @block.scalar
            def _(act):
                for t in range(NT):
                    kt = t if t < 4 else 6
                    s = slice(t * P, (t + 1) * P)
                    kk = slice(kt * P, (kt + 1) * P)
                    v = lambda b, n: bank[b][0:64, 0:n * P].rearrange("p (h n) -> p h n", h=n)
                    for b, dst in enumerate((QT[0:64, 0:4, s], QT[0:64, 4:8, s], IQT[0:64, 0:4, s], IQT[0:64, 4:8, s])):
                        act.wait_ge(tr.h, tr.at(5 * t + b + 1))
                        act.activation(dst, v(b, 4), ACT.Copy).then_inc(ev.h, 1)
                    act.wait_ge(tr.h, tr.at(5 * t + 5))
                    act.activation(KT[0:64, :, kk], v(4, 2), ACT.Copy)
                    act.activation(IKT[0:64, kk], bank[4][0:64, 256:384], ACT.Copy).then_inc(ev.h, 1)
                for t in range(NT):
                    n = QT_KEYS[t] * P
                    for h in range(8):
                        i = t * 8 + h
                        act.wait_ge(ix.h, ix.at(i + 1))
                        if i >= 2:
                            act.wait_ge(ac.h, ac.at(i - 1))
                        act.activation(LG[:, i % 2, 0:n], bank[6 + i % 2][:, 0:n], ACT.Relu).then_inc(rl.h, 1)
        roots.end()
        loaded.end(128), stored.end(16 * 15), kz.end(4), ro.end(NT), tr.end(5 * NT), ev.end(5 * NT)
        ix.end(40), rl.end(40), ac.end(40)
    attention("C", P, QT, lambda a, h, c, n: KT[:, a, c:c + n], lambda a, h, k: VV[:, k, a, :],
              MSK, 0.125, OC)
    s3.close()
    project_out(nc, io["l1_w_out"], sb, sig, bank, ident, OC, None, OD, X, "1")
    st.close()


_OUTS = [
    ("y_p", (1, SEQ, D)), ("y_s", (1, DEC, D)),
    ("a_ckv_p", (1, SEQ, AC)), ("a_krope_p", (1, SEQ, AROPE)), ("b_wkv_p", (P, 4, 64)), ("b_shift_p", (P, BT)),
    ("c_k_p", (1, SEQ, CKV, CHD)), ("c_v_p", (1, SEQ, CKV, CHD)), ("c_kidx_p", (1, SEQ, 64)),
    ("a_ckv_s", (1, DEC, AC)), ("a_krope_s", (1, DEC, AROPE)), ("b_wkv_s", (P, 4, 64)), ("b_shift_s", (P, BT)),
    ("c_k_s", (1, DEC, CKV, CHD)), ("c_v_s", (1, DEC, CKV, CHD)), ("c_kidx_s", (1, DEC, 64)),
    ("d_v_s", (1, DEC, DW)),
]
_AS_THEY_ARE = [
    "x_prompt", "x_sample", "cache_a_krope", "cache_c_v", "l0_norm_mix", "l0_w_in", "a_q_norm", "a_w_uq",
    "a_kv_norm", "a_w_ukv", "a_q_gain", "a_k_gain", "b_w2", "b_a2", "b_g2", "l0_w_out", "l0_norm_ffn",
    "l0_peer_wq", "l1_norm_mix", "l1_w_in", "c_q_gain", "c_k_gain", "c_kidx_gain", "d_ln_g", "d_ln_b",
    "l1_w_out", "l1_norm_ffn", "l1_peer_wq",
]


def _constants():
    i = np.arange(P)
    blk = (i[:, None] // 64) == (i[None, :] // 64)
    b16 = (i[:, None] // 16) == (i[None, :] // 16)
    lt, le = i[:, None] < i[None, :], i[:, None] <= i[None, :]
    scan = np.ones(TOK)
    scan[::CHK] = 0
    cst = np.concatenate([
        blk, blk & lt, blk & le, b16, ~b16, b16 & (i[:, None] > i[None, :]),
        (i[:, None] % 64) == np.arange(64)[None, :], np.broadcast_to(scan, (P, TOK))], axis=1).astype(np.float32)
    idn = np.concatenate([np.eye(P), np.full((P, 1), -0.5), np.full((P, 1), 1e-12)], axis=1).astype(np.float32)
    mask = np.zeros((P, NT, 512), np.float32)
    for t in range(4):
        mask[0:64, t, t * P + 64:] = NEG
        mask[:, t, (t + 1) * P:] = NEG
    mask[:, 4, PAST + DEC:] = NEG

    def rope(pos, half):
        f = (np.float32(10000.0) ** (-np.arange(half, dtype=np.float32) / np.float32(half))).astype(np.float32)
        ang = (pos.astype(np.float32)[:, None] * f[None, :]).astype(np.float32)
        t = np.concatenate([np.cos(ang), np.sin(ang)], axis=1).astype(np.float32)
        return np.ascontiguousarray(t.reshape(-1, P, 2 * half).transpose(1, 0, 2))

    own = np.concatenate([np.arange(SEQ), PAST + np.arange(P)])
    keys = np.concatenate([np.arange(SEQ), np.arange(PAST + P)])
    return {"cst": cst, "idn": idn, "mask": mask, "rope_a": rope(keys, 16), "rope_c": rope(own, 32)}


def kernel(**inputs):
    import concourse.bacc as _bacc
    from concourse.bass_utils import run_bass_kernel_spmd as _run

    a = {k: np.asarray(v) for k, v in inputs.items()}
    col = lambda v: v.reshape(-1, P).T
    ins = {k: a[k] for k in _AS_THEY_ARE}
    ins |= _constants()
    ins["bvec"] = np.concatenate([col(a[k]) for k in ("b_w0", "b_a0", "b_kk", "b_ka")] + [col(a["b_rk"].reshape(-1))]
                                 + [col(a[k]) for k in ("b_ln_g", "b_ln_b", "b_mu")], axis=1)
    ins["shift_t"] = col(a["state_b_shift"][0])
    ins["wkv_t"] = a["state_b_wkv"][0].transpose(0, 2, 1).reshape(4, P, 64).transpose(1, 0, 2)
    ins["ckv_t"] = a["cache_a_ckv"][0].T
    ins["ck_t"] = a["cache_c_k"][0].transpose(2, 1, 0)
    ins["kidx_t"] = a["cache_c_kidx"][0].T
    ins["dws_t"] = a["d_ws"].transpose(2, 0, 1)
    ins["dbs_t"] = a["d_bs"].T
    for i in range(2):
        ins[f"keys_t{i}"] = a[f"l{i}_peer_keys"].transpose(0, 1, 3, 2)
        ins[f"uv{i}"] = np.concatenate([a[f"l{i}_peer_u"], a[f"l{i}_peer_v"]], axis=1)

    nc = _bacc.Bacc("TRN2", target_bir_lowering=False, num_devices=1)
    arrays, io = {}, {}
    for name, v in ins.items():
        v = np.ascontiguousarray(v)
        arrays[f"in_{name}"] = v
        io[name] = nc.dram_tensor(f"in_{name}", v.shape, mybir.dt.from_np(v.dtype), kind="ExternalInput").ap()
    for name, shape in _OUTS:
        io[f"out_{name}"] = nc.dram_tensor(f"out_{name}", shape, F32, kind="ExternalOutput").ap()
    encoder(nc, io)
    got = _run(nc, [arrays], core_ids=[0]).results[0]
    res = []
    for name, _ in _OUTS:
        v = got[f"out_{name}"]
        if "wkv" in name:
            v = v.reshape(2, 64, 4, 64).transpose(2, 0, 3, 1).reshape(1, BH, BHD, BHD)
        elif "shift" in name:
            v = v.T.reshape(1, BPROJ)
        res.append(np.ascontiguousarray(v))
    return tuple(res)
```

```python
from contextlib import ExitStack

import numpy as np

import concourse.bass as bass
from concourse import mybir

P = 128
F32 = mybir.dt.float32
U32 = mybir.dt.uint32
ALU = mybir.AluOpType
ACT = mybir.ActivationFunctionType
AX = mybir.AxisListType

D = 1024
KD = D // P
SEQ, DEC, PAST = 512, 64, 256
NT = 5
TOK = SEQ + DEC
PADT = NT * P
KT7 = 7
EPS = 1e-6
NEG = -1e30

AH, ANOPE, AROPE, AQK, AV = 8, 64, 32, 96, 64
ACQ, AC = 256, 128
ACOLS = ACQ + AC + AROPE
BH, BHD, BW = 8, 64, 512
BT = 14
BPROJ = BT * P
BLN_EPS = 64e-5
DECAY = float(np.exp(-0.5))
CHK = 64
NCH = TOK // CHK
CH_, CKV, CHD = 8, 2, 64
CCOLS = 1352
DW = 512
NK = 128
PH, PK = 8, 16
QT_KEYS = [1, 2, 3, 4, 3]
QT_FIRST = [0, 0, 0, 0, 4]
SEL_KEYS = [0, 128, 128, 128, 80]
RING = 16
SLOTS = 16


class Signal:

    def __init__(self, handle):
        self.h, self.base = handle, 0

    def at(self, n):
        return self.base + n

    def end(self, n):
        self.base += n


class Chain:

    def __init__(self, eng, signal, base=0):
        self.eng, self.s, self.base, self.n = eng, signal, base, 0

    def add(self, ins):
        ins.then_inc(self.s.h, 1)
        self.n += 1

    def __call__(self, ins):
        ins.then_inc(self.s.h, 1)
        self.n += 1
        self.eng.wait_ge(self.s.h, self.s.at(self.base + self.n))


class Roots:

    half = None

    def __init__(self, sig):
        self.asked, self.done, self.n = sig("roots_asked"), sig("roots_done"), 0

    def send(self, ins):
        ins.then_inc(self.asked.h, 1)
        self.n += 1
        return self.n

    def get(self, dve, n=None):
        dve.wait_ge(self.done.h, self.done.at(n or self.n))

    def ask(self, dve, ins):
        self.send(ins)
        self.get(dve)

    def give(self, pool, i, ap):
        pool.wait_ge(self.asked.h, self.asked.at(i + 1))
        half = self.half[:, 0:1]
        half = half.broadcast_to(list(ap.shape)) if len(ap.shape) == 2 else half
        pool.tensor_tensor(ap, ap, half, ALU.pow).then_inc(self.done.h, 1)

    def end(self):
        self.asked.end(self.n), self.done.end(self.n)


def encoder(nc, io):
    ctx = ExitStack()
    with ctx:
        def sb(stack, name, shape, dt=F32):
            return stack.enter_context(nc.sbuf_tensor(name, shape, dt))

        names = {}

        def sig(name):
            if name not in names:
                names[name] = Signal(ctx.enter_context(nc.semaphore(name)))
            return names[name]

        pairs = [ctx.enter_context(nc.psum_tensor(f"banks{i}", [P, 1024], F32)) for i in range(4)]
        bank = [pairs[i // 2][:, 512 * (i % 2):512 * (i % 2) + 512] for i in range(8)]

        X = sb(ctx, "X", [P, NT, D])
        IDN = sb(ctx, "IDN", [P, 130])
        ident = IDN[:, 0:128]
        Roots.half = IDN[:, 128:129]
        lo = ExitStack()
        CST = sb(lo, "CST", [P, 1408])

        dve_chain = sig("dve_chain")
        loaded = sig("loaded")
        stored = sig("stored")

        def load_x(eng):
            for t in range(4):
                eng.dma_start(X[:, t, :], io["x_prompt"][0, t * P:(t + 1) * P, :]).then_inc(loaded.h, 16)
            eng.dma_start(X[0:DEC, 4, :], io["x_sample"][0]).then_inc(loaded.h, 16)

        def norm(stack, tag, gain, src_load, XN, XT, more_loads=None, zero_rows=False, place=None):
            with ExitStack() as st:
                gB = place(D) if place else sb(st, f"gB{tag}", [P, D])
                junk = place(D) if place else sb(st, f"junk{tag}", [P, D])
                ss = sb(st, f"ss{tag}", [P, 8])
                xz, sq, xn, tr, ev = (sig(n) for n in ("x_zeroed", "squares", "normed", "transposed", "evacuated"))
                nload = [0]
                roots = Roots(sig)
                with nc.Block() as block:
                    @block.sync
                    def _(sp):
                        sp.dma_start(gB[:, 0:D], gain.partition_broadcast(P)).then_inc(loaded.h, 16)
                        nload[0] += 1
                        if src_load:
                            load_x(sp)
                            nload[0] += 5
                            sp.dma_start(CST[:, :], io["cst"]).then_inc(loaded.h, 16)
                            sp.dma_start(IDN[:, :], io["idn"]).then_inc(loaded.h, 16)
                            nload[0] += 2
                        if more_loads:
                            more_loads(sp)

                    @block.scalar
                    def _(act):
                        act.wait_ge(loaded.h, loaded.at(16 * nload[0]))
                        if src_load or zero_rows:
                            act.wait_ge(xz.h, xz.at(1))
                        for t in range(NT):
                            act.activation(junk[:, :], X[:, t, :], ACT.Square,
                                           accum_out=ss[:, t:t + 1]).then_inc(sq.h, 1)
                            act.wait_ge(sq.h, sq.base + t + 1)
                        for t in range(NT):
                            for b in range(2):
                                act.wait_ge(tr.h, tr.at(2 * t + b + 1))
                                act.activation(XT[:, 4 * b:4 * b + 4, t * P:(t + 1) * P],
                                               bank[(2 * t + b) % 4][:, :].rearrange("p (k n) -> p k n", k=4),
                                               ACT.Copy).then_inc(ev.h, 1)

                    @block.vector
                    def _(dve):
                        if src_load or zero_rows:
                            dve.memset(X[DEC:P, 4, :], 0.0).then_inc(xz.h, 1)
                        dve.wait_ge(loaded.h, loaded.at(16 * nload[0]))
                        asked = []

                        def mean(t):
                            dve.wait_ge(sq.h, sq.at(t + 1))
                            asked.append(roots.send(dve.tensor_scalar(ss[:, t:t + 1], ss[:, t:t + 1], 1.0 / D, EPS,
                                                                      ALU.mult, ALU.add)))
                        mean(0)
                        for t in range(NT):
                            if t + 1 < NT:
                                mean(t + 1)
                            roots.get(dve, asked[t])
                            dve.scalar_tensor_tensor(XN[:, t, :], X[:, t, :], ss[:, t:t + 1], gB[:, :],
                                                     ALU.mult, ALU.mult).then_inc(xn.h, 1)

                    @block.gpsimd
                    def _(pool):
                        for t in range(NT):
                            roots.give(pool, t, ss[:, t:t + 1])

                    @block.tensor
                    def _(pe):
                        for t in range(NT):
                            pe.wait_ge(xn.h, xn.at(t + 1))
                            for b in range(2):
                                if t >= 2:
                                    pe.wait_ge(ev.h, ev.at(2 * (t - 2) + b + 1))
                                for k in range(4):
                                    mm = pe.transpose(bank[(2 * t + b) % 4][:, k * P:(k + 1) * P],
                                                      XN[:, t, (4 * b + k) * P:(4 * b + k + 1) * P], ident)
                                mm.then_inc(tr.h, 1)
                loaded.end(16 * nload[0])
                if src_load or zero_rows:
                    xz.end(1)
                roots.end()
                sq.end(NT), xn.end(NT), tr.end(2 * NT), ev.end(2 * NT)

        def attention(tag, rows, QT, key_of, V_of, SEL, scale, OUT, prefetch=None):
            with ExitStack() as st:
                S = sb(st, f"S{tag}", [P, 3, 512])
                E = sb(st, f"E{tag}", [P, 3, 512])
                ET = sb(st, f"ET{tag}", [P, 2, 512])
                nmx = sb(st, f"nmx{tag}", [P, 3, 1])
                den = sb(st, f"den{tag}", [P, 3, 1])
                rden = sb(st, f"rden{tag}", [P, 2, 1])
                sc, so, mx, ex, tr, pt, rd, pv, fi = (sig(n) for n in (
                    "scores", "masked", "maxima", "exped", "probs_turned", "probs_copied", "sums_inverted",
                    "weighted", "heads_out"))
                every = (sc, so, mx, ex, tr, pt, rd, pv, fi)
                units = [(h, j) for h in range(AH) for j in range(NT)]
                N = len(units)
                with nc.Block() as block:
                    if prefetch:
                        @block.sync
                        def _(sp):
                            prefetch(sp)

                    @block.tensor
                    def _(pe):
                        def scores(u):
                            h, j = units[u]
                            if u >= 3:
                                pe.wait_ge(so.h, so.at(u - 2))
                            n = QT_KEYS[j] * P
                            pe.matmul(bank[u % 3][:, 0:n], QT[0:rows, h, j * P:(j + 1) * P],
                                      key_of(h // 4, h, QT_FIRST[j] * P, n), start=True, stop=True).then_inc(sc.h, 1)

                        def turn(u):
                            h, j = units[u]
                            pe.wait_ge(ex.h, ex.at(u + 1))
                            if u >= 2:
                                pe.wait_ge(pt.h, pt.at(u - 1))
                            for k in range(QT_KEYS[j]):
                                mm = pe.transpose(bank[3 + u % 2][:, k * P:(k + 1) * P],
                                                  E[:, u % 3, k * P:(k + 1) * P], ident)
                            mm.then_inc(tr.h, 1)

                        def weigh(u):
                            h, j = units[u]
                            pe.wait_ge(pt.h, pt.at(u + 1))
                            if u >= 2:
                                pe.wait_ge(fi.h, fi.at(u - 1))
                            for k in range(QT_KEYS[j]):
                                mm = pe.matmul(bank[5 + u % 2][:, 0:64], ET[:, u % 2, k * P:(k + 1) * P],
                                               V_of(h // 4, h, QT_FIRST[j] + k),
                                               start=(k == 0), stop=(k == QT_KEYS[j] - 1))
                            mm.then_inc(pv.h, 1)

                        scores(0)
                        scores(1)
                        for u in range(N):
                            if u + 2 < N:
                                scores(u + 2)
                            turn(u)
                            if u >= 1:
                                weigh(u - 1)
                        weigh(N - 1)

                    @block.vector
                    def _(dve):
                        def soft(u):
                            h, j = units[u]
                            n, s = QT_KEYS[j] * P, u % 3
                            dve.wait_ge(sc.h, sc.at(u + 1))
                            if u >= 3:
                                dve.wait_ge(ex.h, ex.at(u - 2))
                            dve.scalar_tensor_tensor(S[:, s, 0:n], bank[u % 3][:, 0:n], scale, SEL[:, j, 0:n],
                                                     ALU.mult, ALU.add).then_inc(so.h, 1)
                            dve.wait_ge(so.h, so.at(u + 1))
                            dve.tensor_reduce(nmx[:, s, :], S[:, s, 0:n], AX.X, ALU.max, negate=True).then_inc(mx.h, 1)

                        def finish(u):
                            h, j = units[u]
                            dve.wait_ge(ex.h, ex.at(u + 1))
                            dve.reciprocal(rden[:, u % 2, :], den[:, u % 3, :]).then_inc(rd.h, 1)
                            dve.wait_ge(rd.h, rd.at(u + 1))
                            dve.wait_ge(pv.h, pv.at(u + 1))
                            dve.tensor_scalar(OUT[:, j, h * 64:h * 64 + 64], bank[5 + u % 2][:, 0:64],
                                              rden[:, u % 2, :], None, ALU.mult).then_inc(fi.h, 1)

                        soft(0)
                        soft(1)
                        for u in range(N):
                            if u + 2 < N:
                                soft(u + 2)
                            if u >= 1:
                                finish(u - 1)
                        finish(N - 1)

                    @block.scalar
                    def _(act):
                        def expo(u):
                            h, j = units[u]
                            n, s = QT_KEYS[j] * P, u % 3
                            act.wait_ge(mx.h, mx.at(u + 1))
                            if u >= 3:
                                act.wait_ge(tr.h, tr.at(u - 2))
                                act.wait_ge(rd.h, rd.at(u - 2))
                            act.activation(E[:, s, 0:n], S[:, s, 0:n], ACT.Exp, bias=nmx[:, s, :],
                                           accum_out=den[:, s, :]).then_inc(ex.h, 1)

                        def copy(u):
                            h, j = units[u]
                            n = QT_KEYS[j] * P
                            act.wait_ge(tr.h, tr.at(u + 1))
                            if u >= 2:
                                act.wait_ge(pv.h, pv.at(u - 1))
                            act.activation(ET[:, u % 2, 0:n], bank[3 + u % 2][:, 0:n], ACT.Copy).then_inc(pt.h, 1)

                        expo(0)
                        for u in range(N):
                            if u + 1 < N:
                                expo(u + 1)
                            copy(u)
                for s in every:
                    s.end(N)

        OC = sb(lo, "OC", [P, NT, 512])
        OBT = sb(lo, "OBT", [P, 4, PADT])

        SH = sb(lo, "SH", [P, 3, BT])

        l0 = ExitStack()
        PA = sb(l0, "PA", [P, NT, ACOLS])
        PB = sb(l0, "PB", [P, BT, 2 + TOK])
        w_loaded = [sig(f"weights_loaded{i}") for i in range(4)]

        with ExitStack() as st:
            XT = sb(st, "XT", [P, KD, PADT])
            W = sb(st, "W0", [P, KD, ACOLS + BPROJ])
            wv = io["l0_w_in"].rearrange("(k p) n -> p k n", p=P)
            CW = [(0, ACOLS), (ACOLS, ACOLS + 640), (ACOLS + 640, ACOLS + 1280), (ACOLS + 1280, ACOLS + BPROJ)]

            def load_w(sp):
                for i, (a, b) in enumerate(CW):
                    sp.dma_start(W[:, :, a:b], wv[:, :, a:b]).then_inc(w_loaded[i].h, 16)

            norm(st, "a", io["l0_norm_mix"], True, X, XT, load_w)
            mm_, ev = sig("products"), sig("evacuated")
            border = sig("borders")
            with nc.Block() as block:
                @block.sync
                def _(sp):
                    sp.dma_start(SH[:, 0, :], io["shift_t"]).then_inc(border.h, 16)
                    sp.wait_ge(border.h, border.at(48))
                    sp.dma_start(io["out_b_shift_p"], SH[:, 1, :]).then_inc(stored.h, 16)
                    sp.dma_start(io["out_b_shift_s"], SH[:, 2, :]).then_inc(stored.h, 16)
                    sp.wait_ge(stored.h, stored.at(32))

                @block.tensor
                def _(pe):
                    n = 0
                    pe.wait_ge(w_loaded[0].h, w_loaded[0].at(16))
                    for t in range(NT):
                        if n >= 4:
                            pe.wait_ge(ev.h, ev.at(n - 3))
                        for k in range(KD):
                            m = pe.matmul(bank[n % 4][:, 0:ACOLS], XT[:, k, t * P:(t + 1) * P], W[:, k, 0:ACOLS],
                                          start=(k == 0), stop=(k == KD - 1))
                        m.then_inc(mm_.h, 1)
                        n += 1
                    for f in range(BT):
                        if f % 5 == 0:
                            pe.wait_ge(w_loaded[1 + f // 5].h, w_loaded[1 + f // 5].at(16))
                        for a, b in ((0, SEQ), (SEQ, TOK)):
                            if n >= 4:
                                pe.wait_ge(ev.h, ev.at(n - 3))
                            for k in range(KD):
                                m = pe.matmul(bank[n % 4][:, 0:b - a],
                                              W[:, k, ACOLS + f * P:ACOLS + (f + 1) * P], XT[:, k, a:b],
                                              start=(k == 0), stop=(k == KD - 1))
                            m.then_inc(mm_.h, 1)
                            n += 1

                @block.scalar
                def _(act):
                    n = 0
                    for t in range(NT):
                        act.wait_ge(mm_.h, mm_.at(n + 1))
                        act.activation(PA[:, t, :], bank[n % 4][:, 0:ACOLS], ACT.Copy).then_inc(ev.h, 1)
                        n += 1
                    for f in range(BT):
                        for a, b, o in ((0, SEQ, 1), (SEQ, TOK, 2)):
                            act.wait_ge(mm_.h, mm_.at(n + 1))
                            act.activation(PB[:, f, a + o:b + o], bank[n % 4][:, 0:b - a], ACT.Copy).then_inc(ev.h, 1)
                            n += 1

                @block.vector
                def _(dve):
                    dve.memset(PB[:, :, 0:1], 0.0)
                    dve.wait_ge(border.h, border.at(16))
                    dve.tensor_copy(PB[:, :, 1 + SEQ], SH[:, 0, :])
                    dve.wait_ge(ev.h, ev.at(NT + 2 * BT))
                    dve.tensor_copy(SH[:, 1, :], PB[:, :, SEQ]).then_inc(border.h, 16)
                    dve.tensor_copy(SH[:, 2, :], PB[:, :, TOK + 1]).then_inc(border.h, 16)
            for s in w_loaded:
                s.end(16)
            mm_.end(NT + 2 * BT), ev.end(NT + 2 * BT), border.end(48), stored.end(32)

        mla(nc, io, sb, sig, bank, ident, PA, OC, attention)
        rwkv(nc, io, sb, sig, bank, CST, IDN, PA, PB, OBT, X)
        l0.close()
        project_out(nc, io["l0_w_out"], sb, sig, bank, ident, OC, OBT, None, X, "0", load_x=load_x)
        lo.close()
        peer(nc, io, 0, sb, sig, bank, pairs[3], ident, X, norm)
        layer1(nc, io, sb, sig, bank, ident, X, norm, attention)
        peer(nc, io, 1, sb, sig, bank, pairs[3], ident, X, norm)


def mla(nc, io, sb, sig, bank, ident, PA, OC, attention):
    st = ExitStack()
    QT = sb(st, "QT", [P, AH, PADT])
    KT = sb(st, "KT", [P, AH, KT7 * P])
    V = sb(st, "V", [P, KT7, AH, AV])
    MSK = sb(st, "MSK", [P, NT, 512])
    loaded, stored, dve_chain = sig("loaded"), sig("stored"), sig("dve_chain")
    with ExitStack() as s2:
        gq = sb(s2, "gq", [P, ACQ])
        gc = sb(s2, "gc", [P, AC])
        gains = sb(s2, "gains", [P, 2, AQK])
        wuq = sb(s2, "wuq", [P, 2, AH * AQK])
        wukv = sb(s2, "wukv", [P, AH * (ANOPE + AV)])
        CQT = sb(s2, "CQT", [P, 2, PADT])
        LT = sb(s2, "LT", [P, KT7 * P])
        KRC = sb(s2, "KRC", [P, 2, AROPE])
        RT = sb(s2, "RT", [P, KT7, 32])
        CN = sb(s2, "CN", [P, NT, ACQ + AC])
        ss = sb(s2, "ssA", [P, 2, NT])
        junk = sb(s2, "junkA", [P, ACQ])
        Y = sb(s2, "Y", [P, 3, AH, AQK])
        SQ = sb(s2, "SQ", [P, AH, AQK])
        hs = sb(s2, "hs", [P, 2, AH])
        RC = sb(s2, "RC", [P, AH, 2, 16])
        RS = sb(s2, "RS", [P, AH, 2, 16])
        sq, cn, tr, ev = sig("squares"), sig("normed"), sig("transposed"), sig("evacuated")
        up, cp, ro, t2, e2 = (sig(n) for n in (
            "lifted", "lifted_copied", "rotated", "heads_turned", "heads_copied"))
        NL = 5
        gl, ml = sig("gains_loaded"), sig("masks_loaded")
        units = [("q", t, [0, 1, 2, 3, 6][t]) for t in range(NT)] + [("k", k, k) for k in range(KT7)]
        NU = len(units)
        roots = Roots(sig)
        with nc.Block() as block:
            @block.sync
            def _(sp):
                for dst, src in (
                    (gq[:, :], io["a_q_norm"].partition_broadcast(P)),
                    (gc[:, :], io["a_kv_norm"].partition_broadcast(P)),
                    (gains[:, 0, :], io["a_q_gain"].partition_broadcast(P)),
                    (gains[:, 1, :], io["a_k_gain"].partition_broadcast(P)),
                ):
                    sp.dma_start(dst, src).then_inc(gl.h, 16)
                for dst, src in (
                    (wuq[:, :, :], io["a_w_uq"].rearrange("(k p) n -> p k n", p=P)),
                    (RT[:, :, :], io["rope_a"]),
                    (wukv[:, :], io["a_w_ukv"]),
                    (LT[:, 4 * P:6 * P], io["ckv_t"]),
                    (KRC[:, :, :], io["cache_a_krope"][0].rearrange("(k p) n -> p k n", p=P)),
                ):
                    sp.dma_start(dst, src).then_inc(loaded.h, 16)
                sp.dma_start(MSK[:, :, :], io["mask"]).then_inc(ml.h, 16)
                sp.wait_ge(cn.h, cn.at(2 * NT))
                for t in range(4):
                    sp.dma_start(io["out_a_ckv_p"][0, t * P:(t + 1) * P, :], CN[:, t, ACQ:]).then_inc(stored.h, 16)
                    sp.dma_start(io["out_a_krope_p"][0, t * P:(t + 1) * P, :], PA[:, t, ACQ + AC:]).then_inc(stored.h, 16)
                sp.dma_start(io["out_a_ckv_s"][0], CN[0:DEC, 4, ACQ:]).then_inc(stored.h, 16)
                sp.dma_start(io["out_a_krope_s"][0], PA[0:DEC, 4, ACQ + AC:]).then_inc(stored.h, 16)
                sp.wait_ge(ml.h, ml.at(16))
                sp.wait_ge(stored.h, stored.at(160))

            @block.scalar
            def _(act):
                for t in range(NT):
                    act.activation(junk[:, :], PA[:, t, 0:ACQ], ACT.Square, accum_out=ss[:, 0, t:t + 1]).then_inc(sq.h, 1)
                    act.wait_ge(sq.h, sq.base + 2 * t + 1)
                    act.activation(junk[:, 0:AC], PA[:, t, ACQ:ACQ + AC], ACT.Square,
                                   accum_out=ss[:, 1, t:t + 1]).then_inc(sq.h, 1)
                    act.wait_ge(sq.h, sq.base + 2 * t + 2)
                for t in range(NT):
                    act.wait_ge(tr.h, tr.at(t + 1))
                    b = bank[t % 2]
                    act.activation(CQT[:, :, t * P:(t + 1) * P], b[:, 0:256].rearrange("p (k n) -> p k n", k=2),
                                   ACT.Copy).then_inc(ev.h, 1)
                    kt = t if t < 4 else 6
                    act.activation(LT[:, kt * P:(kt + 1) * P], b[:, 256:384], ACT.Copy).then_inc(ev.h, 1)

                def take(u):
                    kind, t, kt = units[u]
                    act.wait_ge(up.h, up.at(u + 1))
                    if u >= 3:
                        act.wait_ge(t2.h, t2.at(u - 2))
                    for b in range(2):
                        src = bank[2 * (u % 2) + b]
                        y = Y[:, u % 3, 4 * b:4 * b + 4, :]
                        if kind == "q":
                            ins = act.activation(y, src[:, 0:384].rearrange("p (h n) -> p h n", h=4), ACT.Copy)
                        else:
                            s4 = src[:, :].rearrange("p (h n) -> p h n", h=4)
                            act.activation(y[:, :, 0:ANOPE], s4[:, :, 0:ANOPE], ACT.Copy)
                            ins = act.activation(V[:, t, 4 * b:4 * b + 4, :], s4[:, :, ANOPE:], ACT.Copy)
                    ins.then_inc(cp.h, 1)

                def give(u):
                    kind, t, kt = units[u]
                    act.wait_ge(t2.h, t2.at(u + 1))
                    dst = QT if kind == "q" else KT
                    for b in range(2):
                        act.activation(dst[0:AQK, 4 * b:4 * b + 4, t * P:(t + 1) * P],
                                       bank[4 + 2 * (u % 2) + b][0:AQK, :].rearrange("p (h n) -> p h n", h=4),
                                       ACT.Copy).then_inc(e2.h, 1)

                act.wait_ge(loaded.h, loaded.at(16 * NL))
                take(0)
                take(1)
                for u in range(NU):
                    if u + 2 < NU:
                        take(u + 2)
                    give(u)

            @block.vector
            def _(dve):
                ch = Chain(dve, dve_chain)
                dve.wait_ge(gl.h, gl.at(64))
                dve.wait_ge(sq.h, sq.at(2 * NT))
                for i, w in ((0, ACQ), (1, AC)):
                    roots.ask(dve, dve.tensor_scalar(ss[:, i, :], ss[:, i, :], 1.0 / w, EPS, ALU.mult, ALU.add))
                for t in range(NT):
                    dve.scalar_tensor_tensor(CN[:, t, 0:ACQ], PA[:, t, 0:ACQ], ss[:, 0, t:t + 1], gq[:, :],
                                             ALU.mult, ALU.mult).then_inc(cn.h, 1)
                    dve.scalar_tensor_tensor(CN[:, t, ACQ:], PA[:, t, ACQ:ACQ + AC], ss[:, 1, t:t + 1], gc[:, :],
                                             ALU.mult, ALU.mult).then_inc(cn.h, 1)
                def squares(u):
                    kind, t, kt = units[u]
                    y = Y[:, u % 3, :, :]
                    if kind == "k":
                        if u >= 3:
                            dve.wait_ge(t2.h, t2.at(u - 2))
                        src = PA[:, t, ACQ + AC:] if t < 4 else PA[:, 4, ACQ + AC:] if t == 6 else KRC[:, t - 4, :]
                        ch(dve.tensor_copy(y[:, :, ANOPE:], src.unsqueeze(1).broadcast_to([P, AH, AROPE])))
                    dve.wait_ge(cp.h, cp.at(u + 1))
                    square_heads(dve, ch, y, SQ[:, :, :], hs[:, u % 2, :])
                    asked.append(roots.send(mean_heads(dve, hs[:, u % 2, :], AQK)))

                asked = []
                dve.wait_ge(loaded.h, loaded.at(16 * NL))
                squares(0)
                for u, (kind, t, kt) in enumerate(units):
                    if u + 1 < NU:
                        squares(u + 1)
                    y = Y[:, u % 3, :, :]
                    roots.get(dve, asked[u])
                    ch(dve.tensor_tensor(y, y, hs[:, u % 2, :].unsqueeze(2).broadcast_to([P, AH, AQK]), ALU.mult))
                    ch(dve.tensor_tensor(y, y, gains[:, int(kind == "k"), :].unsqueeze(1).broadcast_to([P, AH, AQK]), ALU.mult))
                    rotate(dve, ch, y[:, :, ANOPE:], RT[:, kt, :], RC[:, :, :, :], RS[:, :, :, :], AH, 16, ro)
                dve_chain.end(ch.n)

            @block.gpsimd
            def _(pool):
                for i in range(2):
                    roots.give(pool, i, ss[:, i, :])
                for u in range(NU):
                    roots.give(pool, 2 + u, hs[:, u % 2, :])

            @block.tensor
            def _(pe):
                for t in range(NT):
                    pe.wait_ge(cn.h, cn.at(2 * t + 2))
                    if t >= 2:
                        pe.wait_ge(ev.h, ev.at(2 * t - 2))
                    for k in range(3):
                        m = pe.transpose(bank[t % 2][:, k * P:(k + 1) * P], CN[:, t, k * P:(k + 1) * P], ident)
                    m.then_inc(tr.h, 1)

                def lift(u):
                    kind, t, kt = units[u]
                    if u >= 2:
                        pe.wait_ge(cp.h, cp.at(u - 1))
                    for b in range(2):
                        dst = bank[2 * (u % 2) + b]
                        if kind == "q":
                            for k in range(2):
                                m = pe.matmul(dst[:, 0:384], CQT[:, k, t * P:(t + 1) * P],
                                              wuq[:, k, b * 384:(b + 1) * 384], start=(k == 0), stop=(k == 1))
                        else:
                            m = pe.matmul(dst[:, :], LT[:, t * P:(t + 1) * P], wukv[:, b * 512:(b + 1) * 512],
                                          start=True, stop=True)
                    m.then_inc(up.h, 1)

                pe.wait_ge(ev.h, ev.at(2 * NT))
                pe.wait_ge(loaded.h, loaded.at(16 * NL))
                lift(0)
                lift(1)
                for u in range(NU):
                    if u + 2 < NU:
                        lift(u + 2)
                    pe.wait_ge(ro.h, ro.at(u + 1))
                    if u >= 2:
                        pe.wait_ge(e2.h, e2.at(2 * (u - 1)))
                    for h in range(AH):
                        m = pe.transpose(bank[4 + 2 * (u % 2) + h // 4][0:AQK, (h % 4) * P:(h % 4 + 1) * P],
                                         Y[:, u % 3, h, :], ident)
                    m.then_inc(t2.h, 1)
        gl.end(64), ml.end(16), loaded.end(16 * NL), stored.end(160), sq.end(2 * NT), cn.end(2 * NT), tr.end(NT), ev.end(2 * NT)
        roots.end()
        up.end(NU), cp.end(NU), ro.end(NU), t2.end(NU), e2.end(2 * NU)
    attention("A", AQK, QT, lambda a, h, c, n: KT[0:AQK, h, c:c + n], lambda a, h, k: V[:, k, h, :],
              MSK, float(AQK) ** -0.5, OC)
    st.close()


def square_heads(dve, ch, y, sq, hs):
    ch(dve.tensor_tensor(sq, y, y, ALU.mult))
    ch(dve.tensor_reduce(hs, sq, AX.X, ALU.add))


def mean_heads(dve, hs, width):
    return dve.tensor_scalar(hs, hs, 1.0 / width, EPS, ALU.mult, ALU.add)


def rotate(dve, ch, y, cs, rc, rs, heads, half, done):
    y4 = y.rearrange("p h (a n) -> p h a n", a=2)
    cos = cs[:, 0:half].unsqueeze(1)
    sin = cs[:, half:2 * half].unsqueeze(1)
    for a in range(2):
        ch.add(dve.tensor_tensor(rc[:, :, a, :], y4[:, :, a, :], cos.broadcast_to([P, heads, half]), ALU.mult))
        (ch if a else ch.add)(dve.tensor_tensor(rs[:, :, a, :], y4[:, :, 1 - a, :],
                                                sin.broadcast_to([P, heads, half]), ALU.mult))
    ch.add(dve.tensor_tensor(y4[:, :, 0, :], rc[:, :, 0, :], rs[:, :, 0, :], ALU.subtract))
    ins = dve.tensor_tensor(y4[:, :, 1, :], rc[:, :, 1, :], rs[:, :, 1, :], ALU.add)
    if done is None:
        ch(ins)
    else:
        ins.then_inc(done.h, 1)


def load_out(sp, w_dram, W, wl):
    wv = w_dram.rearrange("(k p) n -> p k n", p=P)
    for i in range(4):
        q = slice(D // 4 * i, D // 4 * i + D // 4)
        sp.dma_start(W[:, :, q], wv[:, :, q]).then_inc(wl[i].h, 16)


def project_out(nc, w_dram, sb, sig, bank, ident, OC, OBT, OD, X, tag, W=None, load_x=None):
    tr, ev, mm_, ad = (sig(n) for n in ("transposed", "evacuated", "products", "added"))
    loaded, xz = sig("loaded"), sig("x_zeroed")
    wl = [sig(f"weights_loaded{i}") for i in range(4)]
    with ExitStack() as st:
        fetched = W is not None
        W = W if fetched else sb(st, f"WO{tag}", [P, KD, D])
        OT = sb(st, f"OT{tag}", [P, 2, KD, P])
        nb = 1 if OD is None else 2
        with nc.Block() as block:
            @block.sync
            def _(sp):
                if not fetched:
                    load_out(sp, w_dram, W, wl)
                if load_x:
                    load_x(sp)

            @block.tensor
            def _(pe):
                def turn(t):
                    if t >= 1:
                        pe.wait_ge(ev.h, ev.at(nb * t))
                    for b in range(nb):
                        src = (OC, OD)[b]
                        for k in range(4):
                            m = pe.transpose(bank[b][:, k * P:(k + 1) * P], src[:, t, k * P:(k + 1) * P], ident)
                        m.then_inc(tr.h, 1)

                def product(t):
                    pe.wait_ge(ev.h, ev.at(nb * (t + 1)))
                    if t >= 2:
                        pe.wait_ge(ad.h, ad.at(2 * (t - 1)))
                    for b in range(2):
                        if t == 0:
                            pe.wait_ge(wl[2 * b].h, wl[2 * b].at(16))
                            pe.wait_ge(wl[2 * b + 1].h, wl[2 * b + 1].at(16))
                        for k in range(KD):
                            lhs = OT[:, t % 2, k, :] if k < 4 or OBT is None else OBT[:, k - 4, t * P:(t + 1) * P]
                            m = pe.matmul(bank[2 + 2 * (t % 2) + b][:, :], lhs, W[:, k, b * 512:(b + 1) * 512],
                                          start=(k == 0), stop=(k == KD - 1))
                        m.then_inc(mm_.h, 1)

                turn(0)
                for t in range(NT):
                    if t + 1 < NT:
                        turn(t + 1)
                    product(t)

            @block.scalar
            def _(act):
                for t in range(NT):
                    for b in range(nb):
                        act.wait_ge(tr.h, tr.at(nb * t + b + 1))
                        if t >= 2:
                            act.wait_ge(mm_.h, mm_.at(2 * (t - 1)))
                        act.activation(OT[:, t % 2, 4 * b:4 * b + 4, :],
                                       bank[b][:, :].rearrange("p (k n) -> p k n", k=4), ACT.Copy).then_inc(ev.h, 1)

            @block.vector
            def _(dve):
                if load_x:
                    dve.memset(X[DEC:P, NT - 1, :], 0.0).then_inc(xz.h, 1)
                    dve.wait_ge(xz.h, xz.at(1))
                    dve.wait_ge(loaded.h, loaded.at(80))
                for t in range(NT):
                    for b in range(2):
                        dve.wait_ge(mm_.h, mm_.at(2 * t + b + 1))
                        x = X[:, t, b * 512:(b + 1) * 512]
                        dve.tensor_tensor(x, bank[2 + 2 * (t % 2) + b][:, :], x, ALU.add).then_inc(ad.h, 1)
        for s in wl:
            s.end(16)
        if load_x:
            loaded.end(80), xz.end(1)
        tr.end(nb * NT), ev.end(nb * NT), mm_.end(2 * NT), ad.end(2 * NT)


V_W0, V_A0, V_KK, V_KA, V_RK, V_LG, V_LB, V_MU = 0, 4, 8, 12, 16, 20, 24, 28


def rwkv(nc, io, sb, sig, bank, CST, IDN, PA, PB, OBT, X):
    ident, eps = IDN[:, 0:128], IDN[:, 129:130]
    onesbd, maskSI, mask16, maskO, mask16L = (
        CST[:, 0:128], CST[:, 128:384], CST[:, 384:512], CST[:, 512:640], CST[:, 640:768])
    stackI = CST[:, 768:832]
    scanm = CST[:, 832:1408]
    loaded, stored, dve_chain = sig("loaded"), sig("stored"), sig("dve_chain")
    st = ExitStack()
    AR = sb(st, "AR", [P, NCH, 4, 2, P])
    BB = sb(st, "BB", [P, NCH, 4, P])
    KB = sb(st, "KB", [P, NCH, 4, P])
    VC = sb(st, "VC", [P, NCH, 4, 64])
    PC = sb(st, "PCe", [P, NCH, 4])
    XV = X[:, :, :].rearrange("p t d -> p (t d)").rearrange("p (s n) -> p s n", s=8)
    G = XV[:, 0:4, :]
    with ExitStack() as s2:
        XS = sb(s2, "XS", [P, 8, TOK])
        W2A = sb(s2, "W2A", [P, 2, BW])
        G2 = sb(s2, "G2", [P, BW])
        BV = sb(s2, "BV", [P, V_MU + BT])
        oka = sb(s2, "oka", [P, 4])
        T4 = sb(s2, "T4", [P, TOK])
        T5 = sb(s2, "T5", [P, TOK])
        VB = sb(s2, "VB", [P, NCH, P])
        T0N = sb(s2, "T0N", [P, TOK])
        T3N = sb(s2, "T3N", [P, TOK])
        T1, T2 = XV[:, 4, 0:TOK], XV[:, 5, 0:TOK]
        T0S, T3S = (XV[:, 6, 0:TOK], T0N[:, :]), (XV[:, 7, 0:TOK], T3N[:, :])
        LW, LG = XS[:, 6, :], XS[:, 7, :]
        sh, tn, za, zg, zc, d1, e1, d2, sp1, d4, sp2, d5, vb, vm, vcp = (sig(n) for n in (
            "shifted", "lora_in", "lora_out", "gates_taken", "zeroed", "summed", "exps", "kk_squared", "kk_sums",
            "bonus_in", "bonus_sums", "bonus_done", "v_blocks", "v_turned", "v_copied"))
        rt = sig("kk_norms")
        with nc.Block() as block:
            @block.sync
            def _(sp):
                sp.wait_ge(zc.h, zc.at(1))
                for dst, src in ((W2A[0:64, 0, :], io["b_w2"]), (W2A[64:P, 1, :], io["b_a2"]), (G2[:, :], io["b_g2"]),
                                 (BV[:, :], io["bvec"])):
                    sp.dma_start(dst, src).then_inc(loaded.h, 16)
                sp.wait_ge(loaded.h, loaded.at(64))

            @block.gpsimd
            def _(pool):
                pool.memset(W2A[:, :, :], 0.0).then_inc(zc.h, 1)
                pool.memset(AR[:, :, :, :, :], 0.0).then_inc(zc.h, 1)
                pool.memset(BB[:, :, :, :], 0.0).then_inc(zc.h, 1)
                pool.memset(KB[:, :, :, :], 0.0).then_inc(zc.h, 1)
                pool.memset(VB[:, :, :], 0.0).then_inc(zc.h, 1)

            @block.vector
            def _(dve):
                ch = Chain(dve, dve_chain)

                def shift(slot, ft):
                    x = XS[:, slot, :]
                    ch.add(dve.tensor_tensor(x[:, 0:SEQ], PB[:, ft, 0:SEQ], PB[:, ft, 1:SEQ + 1], ALU.subtract))
                    ch(dve.tensor_tensor(x[:, SEQ:], PB[:, ft, SEQ + 1:TOK + 1], PB[:, ft, SEQ + 2:], ALU.subtract))
                    mu = BV[:, V_MU + ft:V_MU + ft + 1]
                    ch.add(dve.scalar_tensor_tensor(x[:, 0:SEQ], x[:, 0:SEQ], mu, PB[:, ft, 1:SEQ + 1], ALU.mult, ALU.add))
                    ch(dve.scalar_tensor_tensor(x[:, SEQ:], x[:, SEQ:], mu, PB[:, ft, SEQ + 2:], ALU.mult, ALU.add))

                def blocks(dst, in0, in1, scalar=None):
                    for h in range(2):
                        q = slice(64 * h, 64 * h + 64)
                        o = dst[q, :, 64 * h:64 * h + 64]
                        a = in0[q, :].rearrange("p (c n) -> p c n", c=NCH)
                        b = in1[q, :].rearrange("p (c n) -> p c n", c=NCH)
                        if scalar is None:
                            ch.add(dve.tensor_tensor(o, a, b, ALU.mult))
                        else:
                            ch.add(dve.scalar_tensor_tensor(o, a, scalar, b, ALU.mult, ALU.mult))

                dve.wait_ge(loaded.h, loaded.at(64))
                def ahead(i, p):
                    if p < 4:
                        shift(3 * (p % 2) + i, 4 * i + p)

                shift(6, 12)
                shift(7, 13)
                dve.engine_nop().then_inc(sh.h, 1)
                ch(dve.tensor_scalar(oka[:, :], BV[:, V_KA:V_KA + 4], -1.0, 1.0, ALU.mult, ALU.add))
                for i in range(3):
                    ahead(i, 0)
                for p in range(4):
                    R, K, V = (XS[:, 3 * (p % 2) + i, :] for i in range(3))
                    T0, T3 = T0S[p % 2], T3S[p % 2]
                    dve.wait_ge(zg.h, zg.at(3 * p + 2))
                    ch(dve.tensor_tensor_scan(T1, scanm, T0, 0.0, ALU.mult, ALU.add))
                    dve.tensor_tensor(T2, T1, T0, ALU.subtract).then_inc(d1.h, 1)
                    ahead(0, p + 1)
                    ahead(1, p + 1)
                    dve.wait_ge(e1.h, e1.at(3 * p + 3))
                    ch(dve.tensor_scalar(T1, K, BV[:, V_KK + p:V_KK + p + 1], None, ALU.mult))
                    dve.tensor_tensor(T2, T1, T1, ALU.mult).then_inc(d2.h, 1)
                    if p == 0:
                        dve.wait_ge(zc.h, zc.at(5))
                    blocks(AR[:, :, p, 1, :], R, T4)
                    ch(dve.tensor_copy(PC[:, :, p], T4[:, 63:TOK:64]))
                    if p >= 1:
                        dve.wait_ge(vm.h, vm.at(p))
                    for h in range(2):
                        q = slice(64 * h, 64 * h + 64)
                        ins = dve.tensor_copy(VB[q, :, 64 * h:64 * h + 64], V[q, :].rearrange("p (c n) -> p c n", c=NCH))
                        ins.then_inc(vb.h, 1)
                    dve.wait_ge(rt.h, rt.at(p + 1))
                    ch(dve.reciprocal(T2, T2))
                    ch(dve.tensor_tensor(T1, T1, T2, ALU.mult))
                    blocks(AR[:, :, p, 0, :], T1, T0, -1.0)
                    ch(dve.tensor_scalar(T2, T3, BV[:, V_KA + p:V_KA + p + 1], oka[:, p:p + 1], ALU.mult, ALU.add))
                    ch.add(dve.tensor_tensor(K, K, T2, ALU.mult))
                    ch(dve.tensor_tensor(T3, T1, T3, ALU.mult))
                    blocks(BB[:, :, p, :], T3, T5)
                    blocks(KB[:, :, p, :], K, T5)
                    dve.wait_ge(dve_chain.h, dve_chain.at(ch.n))
                    dve.scalar_tensor_tensor(T1, R, BV[:, V_RK + p:V_RK + p + 1], K, ALU.mult, ALU.mult).then_inc(d4.h, 1)
                    ahead(2, p + 1)
                    dve.wait_ge(sp2.h, sp2.at(p + 1))
                    dve.tensor_tensor(OBT[:, p, 0:512], bank[6][:, :], V[:, 0:512], ALU.mult).then_inc(d5.h, 1)
                    dve.tensor_tensor(OBT[:, p, 512:TOK], bank[7][:, 0:64], V[:, 512:], ALU.mult).then_inc(d5.h, 1)
                    dve.wait_ge(d5.h, d5.at(2 * p + 2))
                    dve.wait_ge(vb.h, vb.at(2 * p + 2))
                dve_chain.end(ch.n)

            @block.scalar
            def _(act):
                act.wait_ge(sh.h, sh.at(1))
                act.activation(LW[0:64, :], LW[0:64, :], ACT.Tanh).then_inc(tn.h, 1)
                act.activation(LG, LG, ACT.Sigmoid).then_inc(tn.h, 1)

                def lora_out(p):
                    T0, T3 = T0S[p % 2], T3S[p % 2]
                    act.wait_ge(za.h, za.at(p + 1))
                    if p >= 2:
                        act.wait_ge(d5.h, d5.at(2 * (p - 1)))
                    for i, (dst, col) in enumerate(((T0, V_W0), (T3, V_A0))):
                        act.activation(dst[:, 0:512], bank[2 * i][:, :], ACT.Sigmoid, bias=BV[:, col + p:col + p + 1])
                        act.activation(dst[:, 512:], bank[2 * i + 1][:, 0:64], ACT.Sigmoid,
                                       bias=BV[:, col + p:col + p + 1]).then_inc(zg.h, 1)
                    act.activation(G[:, p, 0:512], bank[4][:, :], ACT.Copy)
                    act.activation(G[:, p, 512:TOK], bank[5][:, 0:64], ACT.Copy).then_inc(zg.h, 1)

                lora_out(0)
                for p in range(4):
                    act.wait_ge(d1.h, d1.at(p + 1))
                    act.activation(T0S[p % 2], T2, ACT.Exp, scale=-DECAY).then_inc(e1.h, 1)
                    act.activation(T4[:, :], T1, ACT.Exp, scale=-DECAY).then_inc(e1.h, 1)
                    act.activation(T5[:, :], T1, ACT.Exp, scale=DECAY).then_inc(e1.h, 1)
                    act.wait_ge(sp1.h, sp1.at(p + 1))
                    act.activation(T2[:, 0:512], bank[6][:, :], ACT.Sqrt, bias=eps)
                    act.activation(T2[:, 512:], bank[7][:, 0:64], ACT.Sqrt, bias=eps).then_inc(rt.h, 1)
                    if p + 1 < 4:
                        lora_out(p + 1)
                    act.wait_ge(vm.h, vm.at(p + 1))
                    act.activation(VC[:, 0:8, p, :], bank[6][:, :].rearrange("p (c n) -> p c n", c=8), ACT.Copy)
                    act.activation(VC[:, 8, p, :], bank[7][:, 0:64], ACT.Copy).then_inc(vcp.h, 1)

            @block.tensor
            def _(pe):
                def lora(p):
                    w = slice(p * P, (p + 1) * P)
                    if p >= 1:
                        pe.wait_ge(zg.h, zg.at(3 * p))
                    for i, (lhs, rhs) in enumerate(((W2A[:, 0, w], LW), (W2A[:, 1, w], LW), (G2[:, w], LG))):
                        pe.matmul(bank[2 * i][:, :], lhs, rhs[:, 0:512], start=True, stop=True)
                        m = pe.matmul(bank[2 * i + 1][:, 0:64], lhs, rhs[:, 512:], start=True, stop=True)
                    m.then_inc(za.h, 1)

                pe.wait_ge(tn.h, tn.at(2))
                lora(0)
                for p in range(4):
                    if p + 1 < 4:
                        lora(p + 1)
                    if p >= 1:
                        pe.wait_ge(vcp.h, vcp.at(p))
                    pe.wait_ge(d2.h, d2.at(p + 1))
                    pe.matmul(bank[6][:, :], onesbd, T2[:, 0:512], start=True, stop=True)
                    pe.matmul(bank[7][:, 0:64], onesbd, T2[:, 512:], start=True, stop=True).then_inc(sp1.h, 1)
                    pe.wait_ge(d4.h, d4.at(p + 1))
                    pe.matmul(bank[6][:, :], onesbd, T1[:, 0:512], start=True, stop=True)
                    pe.matmul(bank[7][:, 0:64], onesbd, T1[:, 512:], start=True, stop=True).then_inc(sp2.h, 1)
                    pe.wait_ge(vb.h, vb.at(2 * p + 2))
                    pe.wait_ge(d5.h, d5.at(2 * p + 2))
                    for c in range(NCH):
                        m = pe.matmul(bank[6 + c // 8][:, (c % 8) * 64:(c % 8) * 64 + 64], VB[:, c, :], stackI,
                                      start=True, stop=True)
                    m.then_inc(vm.h, 1)
        rt.end(4)
        loaded.end(64), zc.end(5), sh.end(1), tn.end(2), za.end(4), zg.end(12), d1.end(4), e1.end(12), d2.end(4)
        sp1.end(4), d4.end(4), sp2.end(4), d5.end(8), vb.end(8), vm.end(4), vcp.end(4)

    with ExitStack() as s2:
        BV = sb(s2, "BV2", [P, V_MU + BT])
        XF = X[:, :, :].rearrange("p t d -> p (t d)")
        PF = PB[:, :, :].rearrange("p f n -> p (f n)")
        MORE = sb(s2, "chunk_more", [P, 19 * 512])
        AF = PA[:, :, :].rearrange("p t n -> p (t n)")
        cut = lambda buf, n, first=0: [buf[:, first + 512 * i:first + 512 * i + 512] for i in range(n)]
        wide = lambda buf, first: buf[:, first:first + 1024].rearrange("p (q a n) -> p q a n", q=4, a=2)
        lanes = [(XF, 2560, cut(XF, 1, 4608) + cut(MORE, 9)),
                 (PF, 0, cut(PF, 10, 2048)),
                 (AF, 0, cut(MORE, 10, 9 * 512))]

        class Work:

            def __init__(self, lane):
                buf, first, slabs = lanes[lane]
                self.M1 = wide(buf, first)
                self.M2 = wide(buf, first + 1024)
                (self.Bt, self.Kt, self.Dt, self.Dg, self.O, self.ID, self.D2, self.D2T, self.W1, self.W2) = (
                    x.rearrange("p (q n) -> p q n", q=4) for x in slabs)
                self.D4, self.D4T, self.D8T = self.Dt, self.Dg, self.ID
                self.WT, self.NT = self.D2, self.D2T
                self.YC, self.YQ = (slabs[8][:, 256 * i:256 * i + 256].rearrange("p (q n) -> p q n", q=4)
                                    for i in range(2))
                self.b = bank[2 * lane:2 * lane + 2]

        LANES = 3
        work = [Work(i) for i in range(LANES)]
        ST = sb(s2, "STr", [P, 4, 64])
        TMP = sb(s2, "TMP", [P, 4, 64])
        four_of = lambda x: x.rearrange("p (q n) -> p q n", q=4)
        YB, SA = four_of(PF[:, 7168:7680]), four_of(PF[:, 7680:7936])
        ys = sb(s2, "ys", [P, 2, 4])
        made = [sig(f"stage_products{i}") for i in range(LANES)]
        taken = [sig(f"stage_taken{i}") for i in range(LANES)]
        st_sig, y_sig = sig("state_stored"), sig("y_blocks")
        NS, LAG, PRODUCTS = 18, 6, 17
        last = NCH - 1

        def count(c, k):
            return c // LANES * PRODUCTS + min(k, 16)

        roots = Roots(sig)
        turns = [(c, tau - LAG * c) for tau in range(LAG * last + NS) for c in range(NCH) if 0 <= tau - LAG * c < NS]

        def v4(b):
            return b[:, :].rearrange("p (q n) -> p q n", q=4)

        def v64(b):
            return b[:, 0:256].rearrange("p (q n) -> p q n", q=4)

        def four(pe, b, lhs, rhs, n=P):
            for p in range(4):
                m = pe.matmul(b[:, p * n:(p + 1) * n], lhs[:, p, :], rhs[:, p, :], start=True, stop=True)
            return m

        def pe_stage(pe, c, k):
            lane, w = c % LANES, work[c % LANES]
            b = w.b
            if k == 16:
                return
            if count(c, k):
                pe.wait_ge(taken[lane].h, taken[lane].at(2 * count(c, k)))
            if k in (0, 1):
                for p in range(4):
                    m = pe.matmul(b[p // 2][:, (p % 2) * 256:(p % 2) * 256 + 256], (BB, KB)[k][:, c, p, :],
                                  AR[:, c, p, :, :].rearrange("p a n -> p (a n)"), start=True, stop=True)
            elif k == 2:
                for p in range(4):
                    pe.matmul(b[0][:, p * P:(p + 1) * P], AR[:, c, p, 0, :], BB[:, c, p, :], start=True, stop=True)
                    m = pe.transpose(b[1][:, p * P:(p + 1) * P], BB[:, c, p, :], ident)
            elif k == 3:
                four(pe, b[0], w.Dt, w.Dg)
                m = four(pe, b[1], w.Dg, w.Dt)
            elif k == 4:
                four(pe, b[0], w.D2, w.D2T)
                m = four(pe, b[1], w.D2T, w.ID)
            elif k == 5:
                four(pe, b[0], w.D2T, w.D2)
                m = four(pe, b[1], w.D4T, w.W1)
            elif k == 6:
                four(pe, b[0], w.D4, w.D4T)
                for p in range(4):
                    m = pe.transpose(b[1][:, p * P:(p + 1) * P], KB[:, c, p, :], ident)
            elif k == 7:
                m = four(pe, b[0], w.D8T, w.W2)
            elif k == 8:
                for p in range(4):
                    m = pe.transpose(b[1][:, p * P:(p + 1) * P], w.W1[:, p, :], ident)
            elif k == 9:
                m = four(pe, b[0], w.O, w.WT)
            elif k == 10:
                m = four(pe, b[1], w.NT, w.W1)
            elif k in (11, 12):
                m = four(pe, b[(k + 1) % 2], w.NT, w.W2)
            elif k == 13:
                if c:
                    pe.wait_ge(st_sig.h, st_sig.at(c))
                if c == last:
                    pe.wait_ge(loaded.h, loaded.at(32))
                for p in range(4):
                    o = b[0][:, p * 64:(p + 1) * 64]
                    pe.matmul(o, AR[:, c, p, 0, :], ST[:, p, :], start=True, stop=False)
                    m = pe.matmul(o, w.M2[:, p, 0, :], VC[:, c, p, :], start=False, stop=True)
            elif k == 14:
                m = four(pe, b[1], w.W2, TMP, 64)
            elif k == 15:
                for p in range(4):
                    o = b[1][:, p * 64:(p + 1) * 64]
                    pe.matmul(o, w.Bt[:, p, :], SA[:, p, :], start=True, stop=False)
                    pe.matmul(o, w.Kt[:, p, :], VC[:, c, p, :], start=False, stop=True)
                    o = b[0][:, p * 64:(p + 1) * 64]
                    pe.matmul(o, AR[:, c, p, 1, :], ST[:, p, :], start=True, stop=False)
                    pe.matmul(o, w.M1[:, p, 1, :], SA[:, p, :], start=False, stop=False)
                    m = pe.matmul(o, w.M2[:, p, 1, :], VC[:, c, p, :], start=False, stop=True)
            else:
                pe.wait_ge(y_sig.h, y_sig.at(c + 1))
                for p in range(4):
                    m = pe.matmul(b[1][:, p * 64:(p + 1) * 64], YB[:, p, :], stackI, start=True, stop=True)
            m.then_inc(made[lane].h, 1)

        def act_stage(act, c, k):
            lane, w = c % LANES, work[c % LANES]
            b = w.b
            copies = {2: [(w.Bt, v4(b[1]))], 3: [(w.D2, v4(b[0])), (w.D2T, v4(b[1]))], 4: [(w.D4T, v4(b[0]))],
                      5: [(w.D4, v4(b[0]))], 6: [(w.D8T, v4(b[0])), (w.Kt, v4(b[1]))],
                      8: [(w.WT, v4(b[1]))], 9: [(w.NT, v4(b[0]))],
                      13: [(TMP[:, :, :], v64(b[0]))], 14: [(SA, v64(b[1]))]}.get(k, [])
            if copies:
                act.wait_ge(made[lane].h, made[lane].at(count(c, k) + 1))
                for dst, src in copies:
                    ins = act.activation(dst, src, ACT.Copy)
                ins.then_inc(taken[lane].h, 1 if k in (2, 4, 5) else 2)

        def dve_stage(dve, ch, c, k):
            lane, w = c % LANES, work[c % LANES]
            b, tt = w.b, dve.tensor_tensor
            if k in (3, 6, 8, 9, 13, 14):
                return
            bc4 = lambda m: m.unsqueeze(1).broadcast_to([P, 4, P])
            parts = 1 if k in (2, 4, 5) else 2
            if k == 16:
                roots.get(dve)
                for h in range(2):
                    q = slice(64 * h, 64 * h + 64)
                    ins = tt(YB[q, :, 64 * h:64 * h + 64], w.YC[q, :, :],
                             ys[q, 1, :].unsqueeze(2).broadcast_to([64, 4, 64]), ALU.mult)
                    if h == 0:
                        ch(ins)
                ins.then_inc(y_sig.h, 1)
                return
            dve.wait_ge(made[lane].h, made[lane].at(count(c, k) + 1))
            if k in (0, 1):
                for q in range(2):
                    ins = tt((w.M1, w.M2)[k][:, 2 * q:2 * q + 2, :, :].rearrange("p q a n -> p q (a n)"),
                             b[q][:, :].rearrange("p (q n) -> p q n", q=2),
                             maskSI.unsqueeze(1).broadcast_to([P, 2, 256]), ALU.mult)
                    if q == 0:
                        ch(ins)
            elif k == 2:
                ch(tt(w.Dg, w.M1[:, :, 0, :], bc4(mask16), ALU.mult))
                ch(tt(w.O, w.M1[:, :, 0, :], bc4(maskO), ALU.mult))
                ch(tt(w.ID, w.Dg, bc4(ident), ALU.add))
                ins = tt(w.Dt, v4(b[0]), bc4(mask16L), ALU.mult)
            elif k == 4:
                ins = tt(w.W1, v4(b[1]), w.ID, ALU.add)
            elif k == 5:
                ins = tt(w.W2, v4(b[1]), w.W1, ALU.add)
            elif k == 7:
                ins = tt(w.W1, v4(b[0]), w.W2, ALU.add)
            elif k == 10:
                ins = tt(w.W2, v4(b[1]), w.W1, ALU.add)
            elif k in (11, 12):
                ins = tt(w.W2, v4(b[(k + 1) % 2]), w.W1, ALU.add)
            elif k == 15:
                ch(tt(ST[:, :, :], v64(b[1]), ST[:, :, :], ALU.add))
                tt(ST[:, :, :], ST[:, :, :], PC[:, c, :].unsqueeze(2).broadcast_to([P, 4, 64]),
                   ALU.mult).then_inc(st_sig.h, 1)
                ch(dve.tensor_reduce(ys[:, 0, :], v64(b[0]), AX.X, ALU.add))
                ch(dve.tensor_scalar(ys[:, 0, :], ys[:, 0, :], 1.0 / BHD, None, ALU.mult))
                tt(w.YC, v64(b[0]), ys[:, 0, :].unsqueeze(2).broadcast_to([P, 4, 64]),
                   ALU.subtract).then_inc(taken[lane].h, 2)
                dve.wait_ge(taken[lane].h, taken[lane].at(2 * count(c, k) + 2))
                ch(tt(w.YQ, w.YC, w.YC, ALU.mult))
                ch(dve.tensor_reduce(ys[:, 1, :], w.YQ, AX.X, ALU.add))
                roots.send(dve.tensor_scalar(ys[:, 1, :], ys[:, 1, :], 1.0 / BHD, BLN_EPS, ALU.mult, ALU.add))
                return
            else:
                for p in range(4):
                    ins = dve.tensor_scalar(w.YQ[:, p, :], b[1][:, p * 64:(p + 1) * 64], BV[:, V_LG + p:V_LG + p + 1],
                                            BV[:, V_LB + p:V_LB + p + 1], ALU.mult, ALU.add)
                    if p < 3:
                        ch(ins)
                ins.then_inc(taken[lane].h, 2)
                dve.wait_ge(taken[lane].h, taken[lane].at(2 * count(c, k) + 2))
                o = OBT[:, :, c * 64:c * 64 + 64]
                ch(tt(o, o, w.YQ, ALU.add))
                ch(tt(o, o, G[:, :, c * 64:c * 64 + 64], ALU.mult))
                return
            ins.then_inc(taken[lane].h, parts)

        zs = sig("state_zeroed")
        with nc.Block() as block:
            @block.sync
            def _(sp):
                sp.dma_start(BV[:, :], io["bvec"]).then_inc(loaded.h, 16)
                sp.wait_ge(st_sig.h, st_sig.at(last))
                sp.dma_start(io["out_b_wkv_p"], ST[:, :, :]).then_inc(stored.h, 16)
                sp.wait_ge(made[(last - 1) % LANES].h,
                           made[(last - 1) % LANES].at(count(last - 1, 15) + 1))
                sp.wait_ge(stored.h, stored.at(16))
                sp.dma_start(ST[:, :, :], io["wkv_t"]).then_inc(loaded.h, 16)
                sp.wait_ge(st_sig.h, st_sig.at(NCH))
                sp.dma_start(io["out_b_wkv_s"], ST[:, :, :]).then_inc(stored.h, 16)
                sp.wait_ge(stored.h, stored.at(32))

            @block.tensor
            def _(pe):
                pe.wait_ge(zs.h, zs.at(2))
                for c, k in turns:
                    pe_stage(pe, c, k)

            @block.scalar
            def _(act):
                for c, k in turns:
                    act_stage(act, c, k)

            @block.gpsimd
            def _(pool):
                for c in range(NCH):
                    roots.give(pool, c, ys[:, 1, :])

            @block.vector
            def _(dve):
                ch = Chain(dve, dve_chain)
                dve.memset(ST[:, :, :], 0.0).then_inc(zs.h, 1)
                dve.memset(OBT[:, :, TOK:PADT], 0.0)
                dve.memset(YB, 0.0).then_inc(zs.h, 1)
                dve.wait_ge(zs.h, zs.at(2))
                dve.wait_ge(loaded.h, loaded.at(16))
                for c, k in turns:
                    if (c, k) == (last, 15):
                        dve.wait_ge(loaded.h, loaded.at(32))
                    dve_stage(dve, ch, c, k)
                dve_chain.end(ch.n)
        roots.end()
        for lane in range(LANES):
            n = len(range(lane, NCH, LANES)) * PRODUCTS
            made[lane].end(n), taken[lane].end(2 * n)
        y_sig.end(NCH)
        loaded.end(32), stored.end(32), zs.end(2), st_sig.end(NCH)
    st.close()


def peer(nc, io, layer, sb, sig, bank, junk, ident, X, norm):
    stored, xd = sig("stored"), sig("sample_done")
    st = ExitStack()
    L = f"l{layer}"
    XN = sb(st, f"XN{L}", [P, NT, D])
    QP = sb(st, f"QP{L}", [P, NT, PH, P])
    KB = sb(st, f"KY{L}", [P, PH + 1, 2 * NK])
    IOT = sb(st, f"IOT{L}", [P, PK])
    FOLD = sb(st, f"FOLD{L}", [P, DEC])
    ring = sb(st, f"ring{L}", [P, RING, 2 * D])
    flat = ring[:, :, :].rearrange("p s n -> p (s n)")
    at = [2 * D * RING // 2]

    def in_ring(n):
        at[0] += n
        assert at[0] <= 2 * D * RING
        return flat[:, at[0] - n:at[0]]

    norm_rows = [in_ring(D), in_ring(D)]
    WQ = [in_ring(KD * D // 2).rearrange("p (k n) -> p k n", k=KD) for _ in range(2)]
    XT = in_ring(KD * PADT).rearrange("p (k n) -> p k n", k=KD)
    wl, kz, kl, fo = sig("weights_loaded0"), sig("keys_zeroed"), sig("keys_loaded"), sig("fold_ready")
    mm_, ev = sig("products"), sig("evacuated")
    QUERIES = 2 * PH

    def load_w(sp):
        wv = io[f"l{layer}_peer_wq"].rearrange("(k p) n -> p k n", p=P)
        for i in range(2):
            sp.dma_start(WQ[i], wv[:, :, 512 * i:512 * i + 512]).then_inc(wl.h, 16)

    norm(st, L, io[f"l{layer}_norm_ffn"], False, XN, XT, load_w, zero_rows=True, place=lambda n: norm_rows.pop())

    def sp_store(sp):
        for t in range(NT - 1):
            sp.wait_ge(xa.h, xa.at(2 + 2 * PH * (t + 1)))
            sp.dma_start(io["out_y_p"][0, t * P:(t + 1) * P, :], X[:, t, :]).then_inc(stored.h, 16)
        sp.wait_ge(xd.h, xd.at(2))
        sp.dma_start(io["out_y_s"][0], X[0:DEC, NT - 1, :]).then_inc(stored.h, 16)
        sp.wait_ge(stored.h, stored.at(16 * NT))

    def sp_start(sp):
        sp.wait_ge(kz.h, kz.at(1))
        kv = io[f"keys_t{layer}"]
        for half in range(2):
            q, n = slice(64 * half, 64 * half + 64), slice(NK * half, NK * half + NK)
            sp.dma_start(KB[q, 0:PH, n], kv[:, half].rearrange("h d n -> d h n")).then_inc(kl.h, 16)
            sp.dma_start(KB[q, PH, n], kv[0, half]).then_inc(kl.h, 16)
        sp.dma_start(XN[DEC:P, NT - 1, :], XN[0:DEC, NT - 1, :]).then_inc(kl.h, 16)
        sp.wait_ge(kl.h, kl.at(80))

    def pool_start(pool):
        pool.memset(KB[:, :, :], 0.0).then_inc(kz.h, 1)
        pool.iota(IOT[:, :], [[1, PK]], base=0, channel_multiplier=0,
                  allow_small_or_imprecise_dtypes=True).then_inc(kz.h, 1)
        pool.memset(QP[:, NT - 1, :, :], 0.0).then_inc(kz.h, 1)

    def pe_start(pe):
        pe.wait_ge(wl.h, wl.at(32))
        n = 0
        for h in range(PH):
            for a, b in ((0, SEQ), (SEQ, TOK)):
                if n >= 3:
                    pe.wait_ge(ev.h, ev.at(n - 2))
                for k in range(KD):
                    m = pe.matmul(bank[3 + n % 3][:, 0:b - a], WQ[h // 4][:, k, h % 4 * P:h % 4 * P + P], XT[:, k, a:b],
                                  start=(k == 0), stop=(k == KD - 1))
                m.then_inc(mm_.h, 1)
                n += 1
            if h == 0:
                pe.wait_ge(kl.h, kl.at(80))
                pe.wait_ge(ev.h, ev.at(2))
                pe.matmul(bank[0][:, 0:2 * NK], QP[:, 0, 0, :], KB[:, 0, :], start=True, stop=True).then_inc(rp.h, 1)
        pe.wait_ge(ev.h, ev.at(QUERIES))

    def act_start(act):
        n = 0
        for h in range(PH):
            for t0, t1 in ((0, 4), (4, 5)):
                act.wait_ge(mm_.h, mm_.at(n + 1))
                src = bank[3 + n % 3]
                if t0 == 4:
                    if h == 0:
                        act.wait_ge(kz.h, kz.at(3))
                    a = DEC * (h % 2)
                    ins = act.activation(QP[:, 4, h, a:a + DEC], src[:, 0:DEC], ACT.Copy)
                else:
                    ins = act.activation(QP[:, t0:t1, h, :],
                                         src[:, 0:(t1 - t0) * P].rearrange("p (t n) -> p t n", n=P), ACT.Copy)
                ins.then_inc(ev.h, 1)
                n += 1
            if h == 0:
                act.wait_ge(rp.h, rp.at(1))
                act.activation(SC[:, :, :].rearrange("p a n -> p (a n)"), bank[0][:, 0:2 * NK],
                               ACT.Copy).then_inc(rc.h, 1)
            if h == 1:
                act_route_exp(act, 0)
        act.wait_ge(ev.h, ev.at(QUERIES))

    QS = sb(st, f"QS{L}", [P, P])
    QPF = QP[:, :, :, :].rearrange("p t h n -> p (t h n)")
    SC = sb(st, f"SC{L}", [P, 2, NK])
    SW = sb(st, f"SW{L}", [P, 2, NK])
    TS_ = sb(st, f"TS{L}", [P, 2, PK])
    TI = sb(st, f"TI{L}", [P, 2, PK], U32)
    TF = sb(st, f"TF{L}", [P, 2, PK])
    CA = sb(st, f"CA{L}", [P, PK, PK])
    CW = sb(st, f"CW{L}", [P, PK * PK])
    BS = sb(st, f"BS{L}", [P, PK])
    BP = sb(st, f"BP{L}", [P, PK], U32)
    BQ = sb(st, f"BQ{L}", [P, 2, PK], U32)
    BF = sb(st, f"BF{L}", [P, 2, PK])
    OH = sb(st, f"OH{L}", [P, PK, PK])
    SEL = sb(st, f"SEL{L}", [P, 2, PK])
    EF = sb(st, f"EF{L}", [P, PK])
    EI = sb(st, f"EI{L}", [P, 2, PK], U32)
    NM = sb(st, f"NM{L}", [P, 1])
    GX = sb(st, f"GX{L}", [P, PK])
    GS = sb(st, f"GS{L}", [P, 2])
    GT = sb(st, f"GT{L}", [P, 2, PK])
    HD = sb(st, f"HD{L}", [P, 2, PK])
    HG = sb(st, f"HG{L}", [P, 2, PK])
    HW = sb(st, f"HW{L}", [P, 1])
    DG = sb(st, f"DG{L}", [P, 4, P])
    rp, rc, rm, rx, ri, ud, ge, vd = (sig(n) for n in (
        "key_scores", "key_scores_copied", "best_known", "gate_exps", "experts_known", "u_dots", "gelus", "v_added"))
    dg, xa, hw, va = sig("diagonals"), sig("sums_added"), sig("weights_known"), sig("v_added_here")
    G = 4 * PH + PH // 2

    def two_heads(g):
        return isinstance(g, int) and g >= 4 * PH

    SV = SLOTS // 4
    SP = SLOTS - SV
    passed, passed_v = sig("slot_waits_passed"), sig("score_waits_passed")
    qs, steps = sig("queries_placed"), sig("route_steps")
    gd = [sig(f"gathered{i}") for i in range(RING)]
    rows = io[f"uv{layer}"]

    def pe_route(pe, g, kh):
        if two_heads(g):
            pe.wait_ge(rc.h, rc.at(g))
            for odd in range(2):
                h = 2 * (g - 4 * PH) + odd
                m = pe.matmul(bank[0][:, 0:2 * NK], QP[:, NT - 1, h, :], KB[:, h, :], start=(odd == 0), stop=(odd == 1))
            m.then_inc(rp.h, 1)
            return
        pe.wait_ge(qs.h, qs.at(g))
        pe.wait_ge(rc.h, rc.at(g))
        pe.matmul(bank[0][:, 0:2 * NK], QS[:, :],
                  KB[:, kh, :], start=True, stop=True).then_inc(rp.h, 1)

    def act_route_in(act, g):
        if not two_heads(g):
            act.wait_ge(rp.h, rp.at(g))
            act.activation(QS[:, :], QPF[:, bass.ds(g * P, P)], ACT.Copy).then_inc(qs.h, 1)
        act.wait_ge(rp.h, rp.at(g + 1))
        act.wait_ge(ri.h, ri.at(g))
        act.activation(SC[:, :, :].rearrange("p a n -> p (a n)"), bank[0][:, 0:2 * NK], ACT.Copy).then_inc(rc.h, 1)

    def act_route_exp(act, g):
        act.wait_ge(rm.h, rm.at(g + 1))
        act.activation(GX[:, :], BS[:, :], ACT.Exp, bias=NM[:, :], accum_out=GS[:, 0:1]).then_inc(rx.h, 1)

    def dve_route(dve, g, par):
        dve.sem_clear(steps.h)
        ch = Chain(dve, steps)
        dve.wait_ge(rc.h, rc.at(g + 1))
        dve.sem_inc(passed_v.h, 1)
        for a in range(2):
            ch(dve.max(TS_[:, a, 0:8], SC[:, a, :]))
            ch(dve.match_replace(SW[:, a, :], TS_[:, a, 0:8], SC[:, a, :], -3e38))
            ch(dve.max(TS_[:, a, 8:16], SW[:, a, :]))
            ch(dve.max_index(TI[:, a, 0:8], TS_[:, a, 0:8], SC[:, a, :]))
            ch(dve.max_index(TI[:, a, 8:16], TS_[:, a, 8:16], SW[:, a, :]))
        ch(dve.tensor_copy(TF[:, :, :], TI[:, :, :]))
        ch(dve.tensor_tensor(CA[:, :, :], TS_[:, 0, :].unsqueeze(2).broadcast_to([P, PK, PK]),
                             TS_[:, 1, :].unsqueeze(1).broadcast_to([P, PK, PK]), ALU.add))
        cf = CA[:, :, :].rearrange("p a b -> p (a b)")
        ch(dve.max(BS[:, 0:8], cf))
        ch(dve.match_replace(CW[:, :], BS[:, 0:8], cf, -3e38))
        ch(dve.max(BS[:, 8:16], CW[:, :]))
        dve.tensor_scalar(NM[:, :], BS[:, 0:1], -1.0, None, ALU.mult).then_inc(rm.h, 1)
        ch(dve.max_index(BP[:, 0:8], BS[:, 0:8], cf))
        ch(dve.max_index(BP[:, 8:16], BS[:, 8:16], CW[:, :]))
        ch(dve.tensor_single_scalar(BQ[:, 0, :], BP[:, :], 4, op=ALU.logical_shift_right))
        ch(dve.tensor_single_scalar(BQ[:, 1, :], BP[:, :], 15, op=ALU.bitwise_and))
        ch(dve.tensor_copy(BF[:, :, :], BQ[:, :, :]))
        for a in range(2):
            ch(dve.tensor_tensor(OH[:, :, :], BF[:, a, :].unsqueeze(2).broadcast_to([P, PK, PK]),
                                 IOT[:, :].unsqueeze(1).broadcast_to([P, PK, PK]), ALU.is_equal))
            ch(dve.tensor_tensor(OH[:, :, :], OH[:, :, :], TF[:, a, :].unsqueeze(1).broadcast_to([P, PK, PK]),
                                 ALU.mult))
            ch(dve.tensor_reduce(SEL[:, a, :], OH[:, :, :], AX.X, ALU.add))
        ch(dve.scalar_tensor_tensor(EF[:, :], SEL[:, 0, :], float(NK), SEL[:, 1, :], ALU.mult, ALU.add))
        dve.tensor_copy(EI[:, par, :], EF[:, :]).then_inc(ri.h, 1)
        dve.wait_ge(rx.h, rx.at(g + 1))
        ch(dve.reciprocal(GS[:, 1:2], GS[:, 0:1]))
        ch(dve.tensor_scalar(GT[:, par, :], GX[:, :], GS[:, 1:2], None, ALU.mult))

    def use(g, k):
        return g * (SLOTS // RING) + k // RING + 1

    def pool_group(pool, g, par):
        pool.wait_ge(ri.h, ri.at(g + 1))
        for k in range(SLOTS):
            if k % 4 == 3:
                pool.wait_ge(va.h, va.at(g * SV + k // 4 + 1))
            else:
                pool.wait_ge(vd.h, vd.at(g * SP + k - k // 4 + 1))
            if k == RING // 2 + 1:
                pool.wait_ge(mm_.h, mm_.at(QUERIES // 2))
            if k == RING // 2 + 3:
                pool.wait_ge(mm_.h, mm_.at(QUERIES))
            pool.sem_inc(passed.h, 1)
            pool.indirect_dma_start(ring[:, k % RING, :], None, rows,
                                    bass.IndirectOffsetOnAxis(ap=EI[:, par, k:k + 1], axis=0)
                                    ).then_inc(gd[k % RING].h, 16)

    def act_group(act, g, par):
        for b in range(SLOTS // 2):
            act.wait_ge(ud.h, ud.at(g * SLOTS + 2 * b + 2 + 2))
            act.activation(HG[:, par, 2 * b:2 * b + 2], HD[:, par, 2 * b:2 * b + 2], ACT.Gelu).then_inc(ge.h, 1)

    def dve_group(dve, g, t, par, route=None):

        def dot(k):
            dve.wait_ge(gd[k % RING].h, gd[k % RING].at(16 * use(g, k)))
            dve.wait_ge(ud.h, ud.at(g * SLOTS + k + 2))
            dve.scalar_tensor_tensor(junk[:, :], ring[:, k % RING, 0:D], 1.0, XN[:, t, :], ALU.mult, ALU.mult,
                                     accum_out=HD[:, par, k:k + 1]).then_inc(ud.h, 1)

        def weigh(k):
            if k % 2 == 0:
                dve.wait_ge(ge.h, ge.at(g * (SLOTS // 2) + k // 2 + 1))
            if k % 4 != 3:
                i = k - k // 4
                dve.wait_ge(vd.h, vd.at(g * SP + i + SP - 3))
                on, cols = (FOLD, DEC) if two_heads(g) else (ident, P)
                dve.tensor_scalar(DG[:, i % 4, 0:cols], on[:, :], HG[:, par, k:k + 1], GT[:, par, k:k + 1],
                                  ALU.mult, ALU.mult).then_inc(dg.h, 1)
            else:
                i = g * SV + k // 4
                dve.tensor_tensor(HW[:, :], HG[:, par, k:k + 1], GT[:, par, k:k + 1], ALU.mult).then_inc(hw.h, 1)
                dve.wait_ge(hw.h, hw.at(i + 1))
                dve.wait_ge(va.h, va.at(i + SV))
                dve.wait_ge(xa.h, xa.at(2 * g + 2))
                dve.scalar_tensor_tensor(X[:, t, :], ring[:, k, D:2 * D], HW[:, :], X[:, t, :],
                                         ALU.mult, ALU.add).then_inc(va.h, 1)

        for b in range(SLOTS // 2):
            for k in (2 * b, 2 * b + 1):
                dot(k)
                if b:
                    weigh(k - 2)
            if b == 1 and route is not None:
                route()
        weigh(SLOTS - 2)
        weigh(SLOTS - 1)
        dve.wait_ge(va.h, va.at((g + 1) * SV + SV))
        for half in range(2):
            q = slice(512 * half, 512 * half + 512)
            dve.wait_ge(vd.h, vd.at((g + 1) * SP + SP))
            n = DEC if two_heads(g) else P
            dve.tensor_tensor(X[0:n, t, q], bank[1 + 2 * par + half][0:n, :], X[0:n, t, q],
                              ALU.add).then_inc(xa.h, 1)

    def pe_group(pe, g, par):
        n = DEC if two_heads(g) else P
        pe.wait_ge(xa.h, xa.at(2 * g))
        for k in range(SLOTS):
            if k % 4 == 3:
                continue
            i = k - k // 4
            pe.wait_ge(dg.h, dg.at(g * SP + i + 1))
            for half in range(2):
                m = pe.matmul(bank[1 + 2 * par + half][0:n, :], DG[:, i % 4, 0:n],
                              ring[:, k, D + 512 * half:D + 512 * half + 512],
                              start=(i == 0), stop=(i == SP - 1))
            m.then_inc(vd.h, 1)

    def groups(eng, body):
        with eng.Fori(0, 3) as t, eng.Fori(0, PH // 2) as j:
            for par in range(2):
                body(t * PH + j * 2 + par, t, par, j * 2 + par + 1, False)
        with eng.Fori(0, PH // 2 - 1) as j:
            for par in range(2):
                body(3 * PH + j * 2 + par, 3, par, j * 2 + par + 1, False)
        for g in range(4 * PH - 2, G):
            body(g, min(g // PH, 4), g % 2, g % PH + 1, g == G - 1)

    with nc.Block() as block:
        @block.sync
        def _(sp):
            sp_start(sp)
            if layer == 1:
                sp_store(sp)

        @block.gpsimd
        def _(pool):
            pool_start(pool)
            groups(pool, lambda g, t, par, hn, last: pool_group(pool, g, par))

        @block.tensor
        def _(pe):
            pe_start(pe)

            def body(g, t, par, hn, last):
                if not last:
                    pe_route(pe, g + 1, hn)
                pe_group(pe, g, par)
            groups(pe, body)
            pe.wait_ge(xa.h, xa.at(2 * G + 2))
            pe.wait_ge(va.h, va.at(G * SV + SV))
            for half in range(2):
                pe.matmul(bank[1 + half][0:DEC, :], ident[:, DEC:P], X[:, NT - 1, 512 * half:512 * half + 512],
                          start=True, stop=True).then_inc(mm_.h, 1)

        @block.scalar
        def _(act):
            act_start(act)

            def body(g, t, par, hn, last):
                if last:
                    act_group(act, g, par)
                    return
                act_route_in(act, g + 1)
                for b in range(SLOTS // 2):
                    act.wait_ge(ud.h, ud.at(g * SLOTS + 2 * b + 2 + 2))
                    act.activation(HG[:, par, 2 * b:2 * b + 2], HD[:, par, 2 * b:2 * b + 2],
                                   ACT.Gelu).then_inc(ge.h, 1)
                    if b == 1:
                        act_route_exp(act, g + 1)
            groups(act, body)

        @block.vector
        def _(dve):
            dve.engine_nop().then_inc(vd.h, SP)
            dve.engine_nop().then_inc(va.h, SV)
            dve.engine_nop().then_inc(ud.h, 2)
            dve.engine_nop().then_inc(xa.h, 2)
            dve.tensor_tensor(FOLD[:, :], ident[:, 0:DEC], ident[:, DEC:P], ALU.add).then_inc(fo.h, 1)
            dve.wait_ge(fo.h, fo.at(1))
            dve.wait_ge(kz.h, kz.at(2))
            dve_route(dve, 0, 0)

            def body(g, t, par, hn, last):
                dve_group(dve, g, t, par, None if last else lambda: dve_route(dve, g + 1, 1 - par))
            groups(dve, body)
            for half in range(2):
                q = slice(512 * half, 512 * half + 512)
                dve.wait_ge(mm_.h, mm_.at(QUERIES + half + 1))
                dve.tensor_tensor(X[0:DEC, NT - 1, q], bank[1 + half][0:DEC, :], X[0:DEC, NT - 1, q],
                                  ALU.add).then_inc(xd.h, 1)
    xd.end(2)
    if layer == 1:
        stored.end(16 * NT)
    mm_.end(QUERIES + 2), ev.end(QUERIES), wl.end(32), kz.end(3), kl.end(80), fo.end(1)
    dg.end(G * SP), xa.end(2 + 2 * G), hw.end(G * SV), va.end(SV + G * SV)
    passed.end(G * SLOTS), passed_v.end(G)
    qs.end(4 * PH - 1), rp.end(G), rc.end(G), rm.end(G), rx.end(G), ri.end(G), ud.end(2 + G * SLOTS), ge.end(G * SLOTS // 2)
    vd.end(SP + G * SP)
    for s in gd:
        s.end(16 * G * SLOTS // RING)
    st.close()


def layer1(nc, io, sb, sig, bank, ident, X, norm, attention):
    loaded, stored, dve_chain = sig("loaded"), sig("stored"), sig("dve_chain")
    st = ExitStack()
    PCm = sb(st, "PCm", [P, NT, CCOLS])
    OD = sb(st, "OD", [P, NT, 2 * DW])
    VN = sb(st, "VN", [P, NT, DW])
    WT = sb(st, "dwt", [P, 4, P])
    DB = sb(st, "dbs", [P, 4])
    VV = sb(st, "VVc", [P, KT7, CKV, CHD])
    IW = sb(st, "IWc", [P, NT, 8])
    wm, gl, mx, dd = sig("mix_masked"), sig("gains_loaded"), sig("mixed"), sig("added")
    with ExitStack() as s2:
        XT = sb(s2, "XT1", [P, KD, PADT])
        XN = sb(s2, "XN1", [P, NT, D])
        W = sb(s2, "W1", [P, KD, CCOLS + 2 * DW])
        CW = [(CCOLS, CCOLS + 512), (CCOLS + 512, CCOLS + 1024), (0, 512), (512, 1024), (1024, CCOLS)]
        wv = io["l1_w_in"].rearrange("(k p) n -> p k n", p=P)
        wl = [sig(f"weights_loaded{i}") for i in range(5)]
        mm_, ev = sig("products"), sig("evacuated")

        def load_w(sp):
            for i, (a, b) in enumerate(CW):
                sp.dma_start(W[:, :, a:b], wv[:, :, a:b]).then_inc(wl[i].h, 16)

        norm(s2, "c", io["l1_norm_mix"], False, XN, XT, load_w)
        jobs = [(t, i) for t in range(NT) for i in (0, 1)] + [(t, i) for t in range(NT) for i in (2, 3, 4)]
        lg = sb(s2, "dlg", [P, DW])
        lb = sb(s2, "dlb", [P, DW])
        JQ = XN[:, 0, 0:DW]
        SQ = XN[:, 1, 0:11 * CHD].rearrange("p (h n) -> p h n", n=CHD)
        RC, RS = (XN[:, i, 0:640].rearrange("p (h a n) -> p h a n", a=2, n=32) for i in (2, 3))
        ms = sb(s2, "ms", [P, NT, 2])
        gn = sb(s2, "gnc", [P, 3, CHD])
        RT = sb(s2, "RTc", [P, NT, 64])
        hs = sb(s2, "hsc", [P, 2, 11])
        roots = Roots(sig)
        vn, ro = sig("normed"), sig("rotated")
        STORES = 1 + 3 * NT
        with nc.Block() as block:
            @block.sync
            def _(sp):
                for dst, src in ((lg[:, :], io["d_ln_g"].partition_broadcast(P)),
                                 (lb[:, :], io["d_ln_b"].partition_broadcast(P)),
                                 (WT[:, :, :], io["dws_t"]), (DB[:, :], io["dbs_t"])):
                    sp.dma_start(dst, src).then_inc(loaded.h, 16)
                for dst, src in ((gn[:, 0, :], io["c_q_gain"].partition_broadcast(P)),
                                 (gn[:, 1, :], io["c_k_gain"].partition_broadcast(P)),
                                 (gn[:, 2, :], io["c_kidx_gain"].partition_broadcast(P)),
                                 (RT[:, :, :], io["rope_c"])):
                    sp.dma_start(dst, src).then_inc(gl.h, 16)
                sp.wait_ge(vn.h, vn.at(NT))
                sp.dma_start(io["out_d_v_s"][0], VN[0:DEC, 4, :]).then_inc(stored.h, 16)
                ns = 1
                for t in range(NT):
                    sp.wait_ge(ro.h, ro.at(t + 1))
                    n = P if t < 4 else DEC
                    for name, a, b in (("c_k", 512, 640), ("c_v", 640, 768), ("c_kidx", 1280, 1344)):
                        o = io[f"out_{name}_{'p' if t < 4 else 's'}"][0]
                        if name != "c_kidx":
                            o = o.rearrange("s h n -> s (h n)")
                        sp.dma_start(o[t % 4 * P:t % 4 * P + n, :], PCm[0:n, t, a:b]).then_inc(stored.h, 16)
                        ns += 1
                assert ns == STORES

            @block.tensor
            def _(pe):
                for n, (t, i) in enumerate(jobs):
                    a, b = CW[i]
                    if t == 0:
                        pe.wait_ge(wl[i].h, wl[i].at(16))
                    if n >= 4:
                        pe.wait_ge(ev.h, ev.at(n - 3))
                    for k in range(KD):
                        m = pe.matmul(bank[n % 4][:, 0:b - a], XT[:, k, t * P:(t + 1) * P], W[:, k, a:b],
                                      start=(k == 0), stop=(k == KD - 1))
                    m.then_inc(mm_.h, 1)

            @block.scalar
            def _(act):
                for n, (t, i) in enumerate(jobs):
                    a, b = CW[i]
                    act.wait_ge(mm_.h, mm_.at(n + 1))
                    src = bank[n % 4][:, 0:b - a]
                    if i >= 2:
                        ins = act.activation(PCm[:, t, a:b], src, ACT.Copy)
                    else:
                        ins = act.activation(OD[:, t, a - CCOLS:b - CCOLS], src, ACT.Gelu)
                    ins.then_inc(ev.h, 1)

            @block.gpsimd
            def _(pool):
                pool.wait_ge(loaded.h, loaded.at(64))
                pool.affine_select(out=WT[:, :, :], in_=WT[:, :, :], compare_op=ALU.is_ge, fill=0.0, base=0,
                                   pattern=[[0, 4], [1, P]], channel_multiplier=-1).then_inc(wm.h, 1)
                for t in range(NT):
                    roots.give(pool, t, ms[:, t, 1:2])
                for t in range(NT):
                    roots.give(pool, NT + t, hs[:, t % 2, :])

            @block.vector
            def _(dve):
                ch = Chain(dve, dve_chain)
                dve.wait_ge(loaded.h, loaded.at(64))
                for t in range(NT):
                    v = OD[:, t, DW:]
                    mean, var = ms[:, t, 0:1], ms[:, t, 1:2]
                    dve.wait_ge(ev.h, ev.at(2 * t + 2))
                    ch(dve.tensor_reduce(mean, v, AX.X, ALU.add))
                    ch(dve.tensor_scalar(mean, mean, 1.0 / DW, None, ALU.mult))
                    ch(dve.tensor_scalar(VN[:, t, :], v, mean, None, ALU.subtract))
                    ch(dve.tensor_tensor(JQ, VN[:, t, :], VN[:, t, :], ALU.mult))
                    ch(dve.tensor_reduce(var, JQ, AX.X, ALU.add))
                    roots.ask(dve, dve.tensor_scalar(var, var, 1.0 / DW, EPS, ALU.mult, ALU.add))
                    ch(dve.scalar_tensor_tensor(VN[:, t, :], VN[:, t, :], var, lg[:, :], ALU.mult, ALU.mult))
                    dve.tensor_tensor(VN[:, t, :], VN[:, t, :], lb[:, :], ALU.add).then_inc(vn.h, 1)
                dve.wait_ge(gl.h, gl.at(64))
                for t in range(NT):
                    dve.wait_ge(ev.h, ev.at(2 * NT + 3 * t + 3))
                    qk, ik = PCm[:, t, 0:640].rearrange("p (h n) -> p h n", h=10), PCm[:, t, 1280:1344].unsqueeze(1)
                    for y, a, b in ((qk, 0, 10), (ik, 10, 11)):
                        square_heads(dve, ch, y, SQ[:, a:b, :], hs[:, t % 2, a:b])
                    roots.send(mean_heads(dve, hs[:, t % 2, :], CHD))
                    ch.add(dve.tensor_copy(VV[:, t if t < 4 else 6, :, :].rearrange("p h n -> p (h n)"),
                                           PCm[:, t, 640:768]))
                    ch(dve.tensor_scalar(IW[:, t, :], PCm[:, t, 1344:1352], float(8 ** -0.5) * 0.125, None, ALU.mult))
                    roots.get(dve)
                    for y, a, b in ((qk, 0, 10), (ik, 10, 11)):
                        ch(dve.tensor_tensor(y, y, hs[:, t % 2, a:b].unsqueeze(2).broadcast_to([P, b - a, CHD]), ALU.mult))
                    for a, n, g in ((0, 8, 0), (8, 2, 1)):
                        y = qk[:, a:a + n, :]
                        ch.add(dve.tensor_tensor(y, y, gn[:, g, :].unsqueeze(1).broadcast_to([P, n, CHD]), ALU.mult))
                    ch(dve.tensor_tensor(ik[:, 0, :], ik[:, 0, :], gn[:, 2, :], ALU.mult))
                    rotate(dve, ch, qk, RT[:, t, :], RC[:, :, :, :], RS[:, :, :, :], 10, 32, None)
                    iqk = PCm[:, t, 768:1344].rearrange("p (h n) -> p h n", h=9)
                    rotate(dve, ch, iqk, RT[:, t, :], RC[:, 0:9, :, :], RS[:, 0:9, :, :], 9, 32, ro)
                dve_chain.end(ch.n)
        for s in wl:
            s.end(16)
        roots.end()
        mm_.end(5 * NT), ev.end(5 * NT), loaded.end(64), gl.end(64), wm.end(1), vn.end(NT), ro.end(NT)

    s3 = ExitStack()
    OC = sb(st, "OC1", [P, NT, 512])
    QT = sb(s3, "QTc", [P, CH_, PADT])
    KT = sb(s3, "KTc", [P, CKV, KT7 * P])
    MSK = sb(s3, "MSKc", [P, NT, 512])
    with ExitStack() as s2:
        IQT = sb(s2, "IQT", [P, 8, PADT])
        IKT = sb(s2, "IKT", [P, KT7 * P])
        LG = sb(s2, "LGc", [P, 2, 512])
        SCO = sb(s2, "SCO", [P, 512])
        WK = sb(s2, "WKc", [P, 512])
        M8 = sb(s2, "M8c", [P, 8])
        kz, tr, ev, ed = sig("keys_zeroed"), sig("heads_turned"), sig("heads_copied"), sig("heads_copied_dve")
        ix, rl, ac = sig("index_scores"), sig("index_relu"), sig("index_added")
        cols = [h * 64 for h in range(8)] + [768 + h * 64 for h in range(8)] + [512, 576, 1280]
        with nc.Block() as block:
            @block.gpsimd
            def _(pool):
                for buf in (QT, IQT, KT):
                    pool.memset(buf[64:P, :, :], 0.0).then_inc(kz.h, 1)
                pool.memset(IKT[64:P, :], 0.0).then_inc(kz.h, 1)

            @block.sync
            def _(sp):
                kvw = io["cache_c_v"][0].rearrange("(k p) h n -> p k h n", p=P)
                for dst, src in (
                    (KT[0:64, :, 4 * P:6 * P], io["ck_t"]), (IKT[0:64, 4 * P:6 * P], io["kidx_t"]),
                    (VV[:, 4:6, :, :].rearrange("p k h n -> p k (h n)"), kvw.rearrange("p k h n -> p k (h n)")),
                    (MSK[:, :, :], io["mask"]),
                ):
                    sp.dma_start(dst, src).then_inc(loaded.h, 16)
                sp.wait_ge(stored.h, stored.at(16 * STORES))

            @block.vector
            def _(dve):
                ch = Chain(dve, dve_chain)
                for t in range(NT):
                    dve.wait_ge(mx.h, mx.at(t + 1))
                    for g in range(4):
                        q = slice(g * P, (g + 1) * P)
                        ins = dve.scalar_tensor_tensor(OD[:, t, q], bank[5 + t % 2][:, q], DB[:, g:g + 1], OD[:, t, q],
                                                       ALU.add, ALU.mult)
                    ins.then_inc(dd.h, 1)
                for t in range(NT):
                    s = slice(t * P, (t + 1) * P)
                    for b, dst in ((1, QT[0:64, 4:8, s]), (3, IQT[0:64, 4:8, s])):
                        dve.wait_ge(tr.h, tr.at(5 * t + b + 1))
                        dve.tensor_copy(dst, bank[b][0:64, :].rearrange("p (h n) -> p h n", h=4)).then_inc(ed.h, 1)
                dve.wait_ge(loaded.h, loaded.at(64))
                for t in range(NT):
                    n = QT_KEYS[t] * P
                    for h in range(8):
                        i = t * 8 + h
                        dve.wait_ge(rl.h, rl.at(i + 1))
                        w = IW[:, t, h:h + 1]
                        prev = MSK[:, t, 0:n] if h == 0 else SCO[:, 0:n]
                        ch(dve.scalar_tensor_tensor(SCO[:, 0:n], LG[:, i % 2, 0:n], w, prev, ALU.mult, ALU.add))
                        dve.engine_nop().then_inc(ac.h, 1)
                    if SEL_KEYS[t]:
                        for r in range(SEL_KEYS[t] // 8):
                            src = SCO if r == 0 else WK
                            ch(dve.max(M8[:, :], src[:, 0:n]))
                            ch(dve.match_replace(WK[:, 0:n], M8[:, :], src[:, 0:n], -3e38))
                        ch(dve.tensor_scalar(WK[:, 0:n], WK[:, 0:n], -1e38, NEG, ALU.is_ge, ALU.mult))
                        ch(dve.tensor_tensor(MSK[:, t, 0:n], MSK[:, t, 0:n], WK[:, 0:n], ALU.min))
                dve_chain.end(ch.n)

            @block.tensor
            def _(pe):
                for t in range(NT):
                    if t >= 2:
                        pe.wait_ge(dd.h, dd.at(t - 1))
                    for g in range(4):
                        q = slice(g * P, (g + 1) * P)
                        m = pe.matmul(bank[5 + t % 2][:, q], WT[:, g, :], VN[:, t, q], start=True, stop=True)
                    m.then_inc(mx.h, 1)
                for t in range(NT):
                    for i, c in enumerate(cols):
                        b, o = i // 4, (i % 4) * P
                        if i % 4 == 0 and t >= 1 and b % 2 == 0:
                            pe.wait_ge(ev.h, ev.at(3 * (t - 1) + b // 2 + 1))
                        if i % 4 == 0 and t >= 1 and b % 2 == 1:
                            pe.wait_ge(ed.h, ed.at(2 * (t - 1) + b // 2 + 1))
                        m = pe.transpose(bank[b][0:64, o:o + P], PCm[:, t, c:c + 64], ident)
                        if i % 4 == 3 or i == len(cols) - 1:
                            m.then_inc(tr.h, 1)
                pe.wait_ge(dd.h, dd.at(NT))
                pe.wait_ge(kz.h, kz.at(4))
                pe.wait_ge(loaded.h, loaded.at(64))
                pe.wait_ge(ev.h, ev.at(3 * NT))
                pe.wait_ge(ed.h, ed.at(2 * NT))
                for t in range(NT):
                    n, f = QT_KEYS[t] * P, QT_FIRST[t] * P
                    for h in range(8):
                        i = t * 8 + h
                        if i >= 2:
                            pe.wait_ge(rl.h, rl.at(i - 1))
                        pe.matmul(bank[6 + i % 2][:, 0:n], IQT[:, h, t * P:(t + 1) * P], IKT[:, f:f + n],
                                  start=True, stop=True).then_inc(ix.h, 1)

            @block.scalar
            def _(act):
                for t in range(NT):
                    kt = t if t < 4 else 6
                    s = slice(t * P, (t + 1) * P)
                    kk = slice(kt * P, (kt + 1) * P)
                    v = lambda b, n: bank[b][0:64, 0:n * P].rearrange("p (h n) -> p h n", h=n)
                    for b, dst in ((0, QT[0:64, 0:4, s]), (2, IQT[0:64, 0:4, s])):
                        act.wait_ge(tr.h, tr.at(5 * t + b + 1))
                        act.activation(dst, v(b, 4), ACT.Copy).then_inc(ev.h, 1)
                    act.wait_ge(tr.h, tr.at(5 * t + 5))
                    act.activation(KT[0:64, :, kk], v(4, 2), ACT.Copy)
                    act.activation(IKT[0:64, kk], bank[4][0:64, 256:384], ACT.Copy).then_inc(ev.h, 1)
                for t in range(NT):
                    n = QT_KEYS[t] * P
                    for h in range(8):
                        i = t * 8 + h
                        act.wait_ge(ix.h, ix.at(i + 1))
                        if i >= 2:
                            act.wait_ge(ac.h, ac.at(i - 1))
                        act.activation(LG[:, i % 2, 0:n], bank[6 + i % 2][:, 0:n], ACT.Relu).then_inc(rl.h, 1)
        stored.end(16 * STORES), ed.end(2 * NT)
        loaded.end(64), kz.end(4), tr.end(5 * NT), ev.end(3 * NT), mx.end(NT), dd.end(NT)
        ix.end(40), rl.end(40), ac.end(40)
    WO = sb(s3, "WO1", [P, KD, D])
    attention("C", P, QT, lambda a, h, c, n: KT[:, a, c:c + n], lambda a, h, k: VV[:, k, a, :],
              MSK, 0.125, OC, prefetch=lambda sp: load_out(sp, io["l1_w_out"], WO, wl))
    project_out(nc, io["l1_w_out"], sb, sig, bank, ident, OC, None, OD, X, "1", WO)
    s3.close()
    st.close()


_OUTS = [
    ("y_p", (1, SEQ, D)), ("y_s", (1, DEC, D)),
    ("a_ckv_p", (1, SEQ, AC)), ("a_krope_p", (1, SEQ, AROPE)), ("b_wkv_p", (P, 4, 64)), ("b_shift_p", (P, BT)),
    ("c_k_p", (1, SEQ, CKV, CHD)), ("c_v_p", (1, SEQ, CKV, CHD)), ("c_kidx_p", (1, SEQ, 64)),
    ("a_ckv_s", (1, DEC, AC)), ("a_krope_s", (1, DEC, AROPE)), ("b_wkv_s", (P, 4, 64)), ("b_shift_s", (P, BT)),
    ("c_k_s", (1, DEC, CKV, CHD)), ("c_v_s", (1, DEC, CKV, CHD)), ("c_kidx_s", (1, DEC, 64)),
    ("d_v_s", (1, DEC, DW)),
]
_AS_THEY_ARE = [
    "x_prompt", "x_sample", "cache_a_krope", "cache_c_v", "l0_norm_mix", "l0_w_in", "a_q_norm", "a_w_uq",
    "a_kv_norm", "a_w_ukv", "a_q_gain", "a_k_gain", "b_w2", "b_a2", "b_g2", "l0_w_out", "l0_norm_ffn",
    "l0_peer_wq", "l1_norm_mix", "l1_w_in", "c_q_gain", "c_k_gain", "c_kidx_gain", "d_ln_g", "d_ln_b",
    "l1_w_out", "l1_norm_ffn", "l1_peer_wq",
]


def _constants():
    i = np.arange(P)
    blk = (i[:, None] // 64) == (i[None, :] // 64)
    b16 = (i[:, None] // 16) == (i[None, :] // 16)
    lt, le = i[:, None] < i[None, :], i[:, None] <= i[None, :]
    scan = np.ones(TOK)
    scan[::CHK] = 0
    cst = np.concatenate([
        blk, blk & lt, blk & le, b16, ~b16, b16 & (i[:, None] > i[None, :]),
        (i[:, None] % 64) == np.arange(64)[None, :], np.broadcast_to(scan, (P, TOK))], axis=1).astype(np.float32)
    idn = np.concatenate([np.eye(P), np.full((P, 1), -0.5), np.full((P, 1), 1e-12)], axis=1).astype(np.float32)
    mask = np.zeros((P, NT, 512), np.float32)
    for t in range(4):
        mask[0:64, t, t * P + 64:] = NEG
        mask[:, t, (t + 1) * P:] = NEG
    mask[:, 4, PAST + DEC:] = NEG

    def rope(pos, half):
        f = (np.float32(10000.0) ** (-np.arange(half, dtype=np.float32) / np.float32(half))).astype(np.float32)
        ang = (pos.astype(np.float32)[:, None] * f[None, :]).astype(np.float32)
        t = np.concatenate([np.cos(ang), np.sin(ang)], axis=1).astype(np.float32)
        return np.ascontiguousarray(t.reshape(-1, P, 2 * half).transpose(1, 0, 2))

    own = np.concatenate([np.arange(SEQ), PAST + np.arange(P)])
    keys = np.concatenate([np.arange(SEQ), np.arange(PAST + P)])
    return {"cst": cst, "idn": idn, "mask": mask, "rope_a": rope(keys, 16), "rope_c": rope(own, 32)}


def kernel(**inputs):
    import concourse.bacc as _bacc
    from concourse.bass_utils import run_bass_kernel_spmd as _run

    a = {k: np.asarray(v) for k, v in inputs.items()}
    col = lambda v: v.reshape(-1, P).T
    ins = {k: a[k] for k in _AS_THEY_ARE}
    ins |= _constants()
    ins["bvec"] = np.concatenate([col(a[k]) for k in ("b_w0", "b_a0", "b_kk", "b_ka")] + [col(a["b_rk"].reshape(-1))]
                                 + [col(a[k]) for k in ("b_ln_g", "b_ln_b", "b_mu")], axis=1)
    ins["shift_t"] = col(a["state_b_shift"][0])
    ins["wkv_t"] = a["state_b_wkv"][0].transpose(0, 2, 1).reshape(4, P, 64).transpose(1, 0, 2)
    ins["ckv_t"] = a["cache_a_ckv"][0].T
    ins["ck_t"] = a["cache_c_k"][0].transpose(2, 1, 0)
    ins["kidx_t"] = a["cache_c_kidx"][0].T
    ins["dws_t"] = a["d_ws"].transpose(2, 0, 1)
    ins["dbs_t"] = a["d_bs"].T
    for i in range(2):
        ins[f"keys_t{i}"] = a[f"l{i}_peer_keys"].transpose(0, 1, 3, 2)
        ins[f"uv{i}"] = np.concatenate([a[f"l{i}_peer_u"], a[f"l{i}_peer_v"]], axis=1)

    nc = _bacc.Bacc("TRN2", target_bir_lowering=False, num_devices=1)
    arrays, io = {}, {}
    for name, v in ins.items():
        v = np.ascontiguousarray(v)
        arrays[f"in_{name}"] = v
        io[name] = nc.dram_tensor(f"in_{name}", v.shape, mybir.dt.from_np(v.dtype), kind="ExternalInput").ap()
    for name, shape in _OUTS:
        io[f"out_{name}"] = nc.dram_tensor(f"out_{name}", shape, F32, kind="ExternalOutput").ap()
    encoder(nc, io)
    got = _run(nc, [arrays], core_ids=[0]).results[0]
    res = []
    for name, _ in _OUTS:
        v = got[f"out_{name}"]
        if "wkv" in name:
            v = v.reshape(2, 64, 4, 64).transpose(2, 0, 3, 1).reshape(1, BH, BHD, BHD)
        elif "shift" in name:
            v = v.T.reshape(1, BPROJ)
        res.append(np.ascontiguousarray(v))
    return tuple(res)
```
